# Optimizing a Trainium2 kernel written in Bass

```python
import math
import jax
import jax.numpy as jnp
from jax import lax
import numpy as np
import jax, jax.numpy as jnp

D_MODEL = 1024
BATCH = 1
SEQ = 256
DEPTH = 2

GRID_W = 64
CTX_LEN = 256
N_MOD = 9
RMS_EPS = 1e-6
GN_EPS = 1e-6
D_FF = 2816
NA_HEADS = 8
NA_HEAD_DIM = 64
NA_WIDTH = NA_HEADS * NA_HEAD_DIM
WIN_R = 8
WIN_C = 16
HY_WIDTH = D_MODEL - NA_WIDTH
HY_BANDS = 8
HY_EMB = 1 + 2 * HY_BANDS
HY_ORDER = 64
HY_TARGET = 1e-2
HY_FAST_PCT = 0.3
HY_SLOW_PCT = 1.5
EVEN_IN = 3 * NA_WIDTH + 3 * HY_WIDTH
EVEN_CAT = NA_WIDTH + HY_WIDTH
RET_HEADS = 4
RET_KEY_DIM = D_MODEL // RET_HEADS
RET_VAL_DIM = 2 * RET_KEY_DIM
RET_QK = RET_HEADS * RET_KEY_DIM
RET_V = RET_HEADS * RET_VAL_DIM
RET_IN = 2 * RET_QK + 2 * RET_V
RET_CHUNK = 128
ROPE_BASE = 10000.0


def rms_norm(x, gain):
    xf = x.astype(jnp.float32)
    y = xf * lax.rsqrt(jnp.mean(xf * xf, axis=-1, keepdims=True) + RMS_EPS)
    return (y * gain).astype(x.dtype)

def modulate(x, gain, shift, scale):
    return rms_norm(x, gain) * (1 + scale) + shift

def swiglu(h, w_in, w_out):
    a, b = jnp.split(h @ w_in, 2, axis=-1)
    return (jax.nn.silu(a) * b) @ w_out

def split_heads(t, n_heads):
    b, l, _ = t.shape
    return t.reshape(b, l, n_heads, -1).transpose(0, 2, 1, 3)

def merge_heads(t):
    b, h, l, d = t.shape
    return t.transpose(0, 2, 1, 3).reshape(b, l, h * d)

def axial_rope_tables(length, head_dim):
    t = jnp.arange(length)
    n_freq = head_dim // 4
    inv = ROPE_BASE ** (-jnp.arange(n_freq, dtype=jnp.float32) / n_freq)
    ang_r = (t // GRID_W).astype(jnp.float32)[:, None] * inv
    ang_c = (t % GRID_W).astype(jnp.float32)[:, None] * inv
    ang = jnp.concatenate([ang_r, ang_c], axis=-1)
    return jnp.cos(ang), jnp.sin(ang)

def apply_axial_rope(x, cos, sin):
    nf = x.shape[-1] // 4
    xr1, xr2, xc1, xc2 = jnp.split(x.astype(jnp.float32), 4, axis=-1)
    cr, cc = cos[:, :nf], cos[:, nf:]
    sr, sc = sin[:, :nf], sin[:, nf:]
    out = jnp.concatenate([xr1 * cr - xr2 * sr, xr1 * sr + xr2 * cr,
                           xc1 * cc - xc2 * sc, xc1 * sc + xc2 * cc], axis=-1)
    return out.astype(x.dtype)

def qk_norm(t, gain):
    tf = t.astype(jnp.float32)
    return (tf * lax.rsqrt(jnp.mean(tf * tf, axis=-1, keepdims=True) + RMS_EPS) * gain).astype(t.dtype)

def dense_attention(q, k, v):
    s = jnp.einsum('bhqd,bhkd->bhqk', q, k).astype(jnp.float32) * (q.shape[-1] ** -0.5)
    p = jax.nn.softmax(s, axis=-1).astype(v.dtype)
    return jnp.einsum('bhqk,bhkd->bhqd', p, v)

def neighbourhood_attention(q, k, v, k_ctx, v_ctx, rpb):
    b, h, length, d = q.shape
    rows = length // GRID_W
    wr = min(WIN_R, rows)
    q = q.reshape(b, h, rows, GRID_W, d)
    k = k.reshape(b, h, rows, GRID_W, d)
    v = v.reshape(b, h, rows, GRID_W, d)
    col = jnp.arange(GRID_W)
    col_start = jnp.clip(col - WIN_C // 2, 0, GRID_W - WIN_C)
    col_idx = col_start[:, None] + jnp.arange(WIN_C)[None, :]
    dc_idx = col_idx - col[:, None] + (WIN_C - 1)
    scale = d ** -0.5
    n_win = wr * WIN_C

    def row_block(r):
        rs = jnp.clip(r - wr // 2, 0, rows - wr)
        dr_idx = rs + jnp.arange(wr) - r + (WIN_R - 1)
        bias = rpb[:, dr_idx[None, :, None], dc_idx[:, None, :]].astype(jnp.float32)
        q_r = lax.dynamic_index_in_dim(q, r, axis=2, keepdims=False)
        k_w = jnp.take(lax.dynamic_slice_in_dim(k, rs, wr, axis=2), col_idx, axis=3)
        v_w = jnp.take(lax.dynamic_slice_in_dim(v, rs, wr, axis=2), col_idx, axis=3)
        s_win = jnp.einsum('bhqd,bhrqjd->bhqrj', q_r, k_w).astype(jnp.float32) * scale + bias
        s_ctx = jnp.einsum('bhqd,bhcd->bhqc', q_r, k_ctx).astype(jnp.float32) * scale
        s = jnp.concatenate([s_win.reshape(b, h, GRID_W, n_win), s_ctx], axis=-1)
        p = jax.nn.softmax(s, axis=-1).astype(v.dtype)
        p_win = p[..., :n_win].reshape(b, h, GRID_W, wr, WIN_C)
        return (jnp.einsum('bhqrj,bhrqjd->bhqd', p_win, v_w)
                + jnp.einsum('bhqc,bhcd->bhqd', p[..., n_win:], v_ctx))

    out = lax.map(row_block, jnp.arange(rows))
    return out.transpose(1, 2, 0, 3, 4).reshape(b, h, length, d)

def short_conv(u, w, b):
    up = jnp.pad(u, ((0, 0), (1, 1), (0, 0)))
    return up[:, :-2] * w[0] + up[:, 1:-1] * w[1] + up[:, 2:] * w[2] + b

def hyena_filter(length, fw1, fb1, fw2, fb2, fw3, fb3, fw4, freq):
    t = jnp.linspace(0.0, 1.0, length, dtype=jnp.float32)[:, None]
    w = 2.0 * math.pi * jnp.arange(length, dtype=jnp.float32)[:, None] / length
    bands = jnp.linspace(1e-4, HY_BANDS - 1, HY_BANDS, dtype=jnp.float32)
    emb = jnp.concatenate([t, jnp.cos(bands * w), -jnp.sin(bands * w)], axis=-1)
    h = jnp.sin(freq * (emb @ fw1 + fb1))
    h = jnp.sin(freq * (h @ fw2 + fb2))
    h = jnp.sin(freq * (h @ fw3 + fb3))
    h = (h @ fw4).astype(jnp.float32)
    max_decay = math.log(HY_TARGET) / HY_FAST_PCT
    min_decay = math.log(HY_TARGET) / HY_SLOW_PCT
    deltas = jnp.linspace(min_decay, max_decay, HY_WIDTH, dtype=jnp.float32)
    window = jnp.exp(-t * jnp.abs(deltas))
    h_fwd = h[:, :HY_WIDTH] * window
    h_bwd = h[:, HY_WIDTH:] * window
    return jnp.concatenate([h_fwd[:1] + h_bwd[:1], h_fwd[1:],
                            jnp.zeros((1, HY_WIDTH), jnp.float32), h_bwd[1:][::-1]], axis=0)

def long_conv(u, filt):
    length = u.shape[1]
    uf = jnp.fft.rfft(u.astype(jnp.float32), n=2 * length, axis=1)
    kf = jnp.fft.rfft(filt, n=2 * length, axis=0)
    return jnp.fft.irfft(uf * kf[None], n=2 * length, axis=1)[:, :length]

def hyena_operator(u, conv_w, conv_b, filter_params, d_bias):
    uc = short_conv(u, conv_w, conv_b)
    x0, x1, v = jnp.split(uc, 3, axis=-1)
    z = v * x1
    filt = hyena_filter(u.shape[1], *filter_params)
    y = long_conv(z, filt).astype(z.dtype) + z * d_bias
    return y * x0

def na_hyena_mixer(h_lat, h_ctx, w_in, w_out, q_gain, k_gain, rpb, conv_w, conv_b,
                   filter_params, d_bias, ctx_out):
    p_lat = h_lat @ w_in
    p_ctx = h_ctx @ w_in
    qa_l, ka_l, va_l = [split_heads(t, NA_HEADS) for t in jnp.split(p_lat[..., :3 * NA_WIDTH], 3, axis=-1)]
    qa_c, ka_c, va_c = [split_heads(t, NA_HEADS) for t in jnp.split(p_ctx[..., :3 * NA_WIDTH], 3, axis=-1)]
    k_c = qk_norm(ka_c, k_gain)
    a_lat = merge_heads(neighbourhood_attention(qk_norm(qa_l, q_gain), qk_norm(ka_l, k_gain), va_l,
                                                k_c, va_c, rpb))
    b_lat = hyena_operator(p_lat[..., 3 * NA_WIDTH:], conv_w, conv_b, filter_params, d_bias)
    o_lat = jnp.concatenate([a_lat, b_lat], axis=-1) @ w_out
    if not ctx_out:
        return o_lat, None
    a_ctx = merge_heads(dense_attention(qk_norm(qa_c, q_gain), k_c, va_c))
    b_ctx = hyena_operator(p_ctx[..., 3 * NA_WIDTH:], conv_w, conv_b, filter_params, d_bias)
    o_ctx = jnp.concatenate([a_ctx, b_ctx], axis=-1) @ w_out
    return o_lat, o_ctx

def retention_scan(q, k, v, log_gamma, state0):
    b, h, length, dk = q.shape
    dv = v.shape[-1]
    n = length // RET_CHUNK

    def chunks(a):
        return a.astype(jnp.float32).reshape(b, h, n, RET_CHUNK, a.shape[-1]).transpose(2, 0, 1, 3, 4)

    j = jnp.arange(RET_CHUNK, dtype=jnp.float32)
    diff = j[:, None] - j[None, :]
    lg = log_gamma.astype(jnp.float32)
    dmask = jnp.where(diff[None] >= 0, jnp.exp(lg[:, None, None] * jnp.maximum(diff, 0.0)[None]), 0.0)
    xi = jnp.exp(lg[:, None] * (j + 1.0))
    zeta = jnp.exp(lg[:, None] * (RET_CHUNK - 1.0 - j))
    g_chunk = jnp.exp(lg * RET_CHUNK)

    def step(state, inp):
        qc, kc, vc = inp
        inner = jnp.einsum('bhid,bhjd->bhij', qc, kc) * dmask
        o = (jnp.einsum('bhij,bhje->bhie', inner, vc)
             + jnp.einsum('bhid,bhde->bhie', qc, state) * xi[..., None])
        state = state * g_chunk[:, None, None] + jnp.einsum('bhjd,bhje->bhde', kc * zeta[..., None], vc)
        return state, o

    state, o = lax.scan(step, state0, (chunks(q), chunks(k), chunks(v)))
    return o.transpose(1, 2, 0, 3, 4).reshape(b, h, length, dv), state

def retention_mixer(h_lat, h_ctx, w_in, w_out, logit_f, logit_b, rope_cos, rope_sin, ctx_out):
    def project(hh):
        q, k, v, g = jnp.split(hh @ w_in, [RET_QK, 2 * RET_QK, 2 * RET_QK + RET_V], axis=-1)
        return (split_heads(q, RET_HEADS), split_heads(k, RET_HEADS) * (RET_KEY_DIM ** -0.5),
                split_heads(v, RET_HEADS), g)

    def output(y, g, dtype):
        mu = jnp.mean(y, axis=-1, keepdims=True)
        var = jnp.mean(jnp.square(y - mu), axis=-1, keepdims=True)
        y = merge_heads((y - mu) * lax.rsqrt(var + GN_EPS)).astype(dtype)
        return (jax.nn.silu(g) * y) @ w_out

    q_l, k_l, v_l, g_l = project(h_lat)
    q_l = apply_axial_rope(q_l, rope_cos, rope_sin)
    k_l = apply_axial_rope(k_l, rope_cos, rope_sin)
    q_c, k_c, v_c, g_c = project(h_ctx)
    lg_f = jax.nn.log_sigmoid(logit_f.astype(jnp.float32))
    lg_b = jax.nn.log_sigmoid(logit_b.astype(jnp.float32))
    zero = jnp.zeros((h_lat.shape[0], RET_HEADS, RET_KEY_DIM, RET_VAL_DIM), jnp.float32)
    flip = lambda a: jnp.flip(a, axis=2)
    o_cf, s_f = retention_scan(q_c, k_c, v_c, lg_f, zero)
    o_cb, s_b = retention_scan(flip(q_c), flip(k_c), flip(v_c), lg_b, zero)
    o_lf, _ = retention_scan(q_l, k_l, v_l, lg_f, s_f)
    o_lb, _ = retention_scan(flip(q_l), flip(k_l), flip(v_l), lg_b, s_b)
    o_lat = output(o_lf + flip(o_lb), g_l, h_lat.dtype)
    if not ctx_out:
        return o_lat, None
    o_ctx = output(o_cf + flip(o_cb), g_c, h_ctx.dtype)
    return o_lat, o_ctx

def first_inputs(seed: int = 0) -> dict:
    key = jax.random.key(seed)
    ks = iter(jax.random.split(key, 40))

    def nrm(shape, scale):
        return scale * jax.random.normal(next(ks), shape, jnp.float32)

    d = D_MODEL
    n_even = (DEPTH + 1) // 2
    n_odd = DEPTH // 2
    gamma = 1.0 - 2.0 ** (-5.0 - np.arange(RET_HEADS))
    logit0 = jnp.asarray(np.log(gamma / (1.0 - gamma)), jnp.float32)
    return {
        "x": nrm((BATCH, SEQ, d), 1.0),
        "c": nrm((BATCH, d), 1.0),
        "ctx": nrm((BATCH, CTX_LEN, d), 1.0),
        "c_ctx": nrm((d,), 1.0),
        "w_mod": nrm((DEPTH, d, N_MOD * d), 0.5 * d ** -0.5),
        "b_mod": nrm((DEPTH, N_MOD * d), 0.02),
        "norm_gain": 1.0 + nrm((DEPTH, 3, d), 0.05),
        "ffn_a_in": nrm((DEPTH, d, 2 * D_FF), d ** -0.5),
        "ffn_a_out": nrm((DEPTH, D_FF, d), D_FF ** -0.5),
        "ffn_b_in": nrm((DEPTH, d, 2 * D_FF), d ** -0.5),
        "ffn_b_out": nrm((DEPTH, D_FF, d), D_FF ** -0.5),
        "even_in": nrm((n_even, d, EVEN_IN), d ** -0.5),
        "even_out": nrm((n_even, EVEN_CAT, d), EVEN_CAT ** -0.5),
        "na_q_gain": 1.0 + nrm((n_even, NA_HEAD_DIM), 0.05),
        "na_k_gain": 1.0 + nrm((n_even, NA_HEAD_DIM), 0.05),
        "na_rpb": nrm((n_even, NA_HEADS, 2 * WIN_R - 1, 2 * WIN_C - 1), 0.1),
        "hy_conv_w": nrm((n_even, 3, 3 * HY_WIDTH), 3 ** -0.5),
        "hy_conv_b": nrm((n_even, 3 * HY_WIDTH), 0.02),
        "hy_fw1": nrm((n_even, HY_EMB, HY_ORDER), HY_EMB ** -0.5),
        "hy_fb1": nrm((n_even, HY_ORDER), 0.1),
        "hy_fw2": nrm((n_even, HY_ORDER, HY_ORDER), HY_ORDER ** -0.5),
        "hy_fb2": nrm((n_even, HY_ORDER), 0.1),
        "hy_fw3": nrm((n_even, HY_ORDER, HY_ORDER), HY_ORDER ** -0.5),
        "hy_fb3": nrm((n_even, HY_ORDER), 0.1),
        "hy_fw4": nrm((n_even, HY_ORDER, 2 * HY_WIDTH), 0.05 * HY_ORDER ** -0.5),
        "hy_freq": 1.0 + nrm((n_even, HY_ORDER), 0.1),
        "hy_bias": nrm((n_even, HY_WIDTH), 0.5),
        "ret_in": nrm((n_odd, d, RET_IN), d ** -0.5),
        "ret_out": nrm((n_odd, RET_V, d), RET_V ** -0.5),
        "ret_logit_f": logit0 + nrm((n_odd, RET_HEADS), 0.1),
        "ret_logit_b": logit0 + nrm((n_odd, RET_HEADS), 0.1),
    }

def first_block(x, c, ctx, c_ctx, w_mod, b_mod, norm_gain, ffn_a_in, ffn_a_out, ffn_b_in, ffn_b_out,
              even_in, even_out, na_q_gain, na_k_gain, na_rpb, hy_conv_w, hy_conv_b,
              hy_fw1, hy_fb1, hy_fw2, hy_fb2, hy_fw3, hy_fb3, hy_fw4, hy_freq, hy_bias,
              ret_in, ret_out, ret_logit_f, ret_logit_b):
    b = x.shape[0]
    rope_cos, rope_sin = axial_rope_tables(x.shape[1], RET_KEY_DIM)
    x_lat, x_ctx = x, ctx
    for i in range(DEPTH):
        last = i == DEPTH - 1
        mod_l = (jax.nn.silu(c) @ w_mod[i] + b_mod[i]).reshape(b, N_MOD, 1, D_MODEL)
        mod_c = (jax.nn.silu(c_ctx) @ w_mod[i] + b_mod[i]).reshape(N_MOD, 1, D_MODEL)
        x_lat = x_lat + 0.5 * mod_l[:, 2] * swiglu(modulate(x_lat, norm_gain[i, 0], mod_l[:, 0], mod_l[:, 1]),
                                                 ffn_a_in[i], ffn_a_out[i])
        x_ctx = x_ctx + 0.5 * mod_c[2] * swiglu(modulate(x_ctx, norm_gain[i, 0], mod_c[0], mod_c[1]),
                                              ffn_a_in[i], ffn_a_out[i])
        h_l = modulate(x_lat, norm_gain[i, 1], mod_l[:, 3], mod_l[:, 4])
        h_c = modulate(x_ctx, norm_gain[i, 1], mod_c[3], mod_c[4])
        if i % 2 == 0:
            e = i // 2
            filter_params = (hy_fw1[e], hy_fb1[e], hy_fw2[e], hy_fb2[e], hy_fw3[e], hy_fb3[e], hy_fw4[e], hy_freq[e])
            o_l, o_c = na_hyena_mixer(h_l, h_c, even_in[e], even_out[e], na_q_gain[e], na_k_gain[e], na_rpb[e],
                                      hy_conv_w[e], hy_conv_b[e], filter_params, hy_bias[e], not last)
        else:
            o = i // 2
            o_l, o_c = retention_mixer(h_l, h_c, ret_in[o], ret_out[o], ret_logit_f[o], ret_logit_b[o],
                                       rope_cos, rope_sin, not last)
        x_lat = x_lat + mod_l[:, 5] * o_l
        x_lat = x_lat + 0.5 * mod_l[:, 8] * swiglu(modulate(x_lat, norm_gain[i, 2], mod_l[:, 6], mod_l[:, 7]),
                                                 ffn_b_in[i], ffn_b_out[i])
        if not last:
            x_ctx = x_ctx + mod_c[5] * o_c
            x_ctx = x_ctx + 0.5 * mod_c[8] * swiglu(modulate(x_ctx, norm_gain[i, 2], mod_c[6], mod_c[7]),
                                                  ffn_b_in[i], ffn_b_out[i])
    return x_lat


DEPTH_2 = 1

HEAD_DIM = 64
MIX_WIDTH = D_MODEL
N_HEADS = MIX_WIDTH // HEAD_DIM
N_HEADS_B = N_HEADS // 4
N_HEADS_A = N_HEADS - N_HEADS_B
WIDTH_A = N_HEADS_A * HEAD_DIM
WIDTH_B = N_HEADS_B * HEAD_DIM
DILATED_PATTERNS = ((128, 1), (512, 4), (2048, 16))
DIL_BLOCK = 128
MOBA_BLOCK = 256
MOBA_TOPK = 3
MOBA_QCHUNK = 64
N_MEM = 256
CROSS_HEADS = 4
CROSS_HEAD_DIM = D_MODEL // CROSS_HEADS
D_FF_2 = ((8 * D_MODEL // 3 + 255) // 256) * 256
REL_BUCKETS = 32
REL_MAX_DIST = 2048
NORM_EPS = 1e-6
NEG_INF = -jnp.inf


def rms_norm_2(x, g):
    xf = x.astype(jnp.float32)
    y = xf * lax.rsqrt(jnp.mean(xf * xf, axis=-1, keepdims=True) + NORM_EPS)
    return (y * g.astype(jnp.float32)).astype(x.dtype)

def swiglu_2(x, w_gu, w_down):
    gu = x @ w_gu
    g, u = jnp.split(gu, 2, axis=-1)
    return (jax.nn.silu(g) * u) @ w_down

def rel_bucket(dist):
    max_exact = REL_BUCKETS // 2
    n = jnp.maximum(dist, 0)
    nf = jnp.maximum(n, 1).astype(jnp.float32)
    large = max_exact + (jnp.log(nf / max_exact) / math.log(REL_MAX_DIST / max_exact)
                         * (REL_BUCKETS - max_exact)).astype(jnp.int32)
    large = jnp.minimum(large, REL_BUCKETS - 1)
    return jnp.where(n < max_exact, n, large)

def split_heads_2(a, n_heads, head_dim):
    b, s, _ = a.shape
    return a.reshape(b, s, n_heads, head_dim).transpose(0, 2, 1, 3)

def merge_heads_2(a):
    b, h, s, e = a.shape
    return a.transpose(0, 2, 1, 3).reshape(b, s, h * e)

def dilated_window_pattern(q, k, v, bias_tab, window, dilation):
    B, H, S, E = q.shape
    n_steps = window // dilation
    L = S // dilation
    nblk = -(-L // DIL_BLOCK)
    Lp = nblk * DIL_BLOCK

    def to_sub(a):
        a = a.reshape(B, H, L, dilation, E).transpose(0, 1, 3, 2, 4)
        a = jnp.pad(a, ((0, 0), (0, 0), (0, 0), (0, Lp - L), (0, 0)))
        return a.reshape(B, H, dilation, nblk, DIL_BLOCK, E)

    def band(a):
        prev = jnp.pad(a, ((0, 0), (0, 0), (0, 0), (1, 0), (0, 0), (0, 0)))[:, :, :, :-1]
        return jnp.concatenate([prev, a], axis=4)

    qs, ks, vs = to_sub(q), to_sub(k), to_sub(v)
    kb, vb = band(ks), band(vs)
    scale = HEAD_DIM ** -0.5
    s = jnp.einsum('bhrnqe,bhrnke->bhrnqk', qs, kb).astype(jnp.float32) * scale
    i = jnp.arange(DIL_BLOCK)[:, None]
    j = jnp.arange(2 * DIL_BLOCK)[None, :]
    delta = DIL_BLOCK + i - j
    bias = bias_tab[:, rel_bucket(delta * dilation)].astype(jnp.float32)
    blk = jnp.arange(nblk)[:, None, None]
    valid = (delta >= 0) & (delta <= n_steps) & ((blk > 0) | (j >= DIL_BLOCK))
    s = jnp.where(valid, s + bias[None, :, None, None], NEG_INF)
    m = jnp.max(s, axis=-1, keepdims=True)
    p = jnp.exp(s - m)
    l = jnp.sum(p, axis=-1, keepdims=True)
    o = jnp.einsum('bhrnqk,bhrnke->bhrnqe', p, vb.astype(jnp.float32)) / l

    def from_sub(a):
        f = a.shape[-1]
        a = a.reshape(B, H, dilation, Lp, f)[:, :, :, :L]
        return a.transpose(0, 1, 3, 2, 4).reshape(B, H, S, f)

    return from_sub(o), from_sub(m), from_sub(l)

def dilated_attention(q, k, v, bias_tab):
    outs = [dilated_window_pattern(q, k, v, bias_tab, w, d) for (w, d) in DILATED_PATTERNS]
    m_all = outs[0][1]
    for _, m_i, _ in outs[1:]:
        m_all = jnp.maximum(m_all, m_i)
    num = 0.0
    den = 0.0
    for o_i, m_i, l_i in outs:
        w_i = l_i * jnp.exp(m_i - m_all)
        num = num + w_i * o_i
        den = den + w_i
    return num / den

def moba_attention(q, k, v, bias_tab):
    B, H, S, E = q.shape
    BS = MOBA_BLOCK
    nb = -(-S // BS)
    Sp = nb * BS
    pad = lambda a: jnp.pad(a, ((0, 0), (0, 0), (0, Sp - S), (0, 0)))
    qp, kp, vp = pad(q), pad(k), pad(v)
    kb = kp.reshape(B, H, nb, BS, E)
    vb = vp.reshape(B, H, nb, BS, E)
    kmean = jnp.mean(kb.astype(jnp.float32), axis=3)
    gate = jnp.einsum('bhse,bhne->bhsn', qp.astype(jnp.float32), kmean)
    qblk = jnp.arange(Sp) // BS
    past = jnp.arange(nb)[None, :] < qblk[:, None]
    gate = jnp.where(past, gate, NEG_INF)
    top = min(MOBA_TOPK, nb)
    _, sel = lax.top_k(gate, top)
    nc = Sp // MOBA_QCHUNK
    chunk = lambda a: jnp.moveaxis(a.reshape(B, H, nc, MOBA_QCHUNK, *a.shape[3:]), 2, 0)
    gather = jax.vmap(jax.vmap(lambda tab, ix: tab[ix]))
    head_idx = jnp.arange(H)[:, None, None, None]
    scale = HEAD_DIM ** -0.5

    def one_chunk(args):
        qc, selc, c = args
        t = c * MOBA_QCHUNK + jnp.arange(MOBA_QCHUNK)
        own = (c * MOBA_QCHUNK) // BS
        k_own = lax.dynamic_index_in_dim(kb, own, axis=2, keepdims=False)
        v_own = lax.dynamic_index_in_dim(vb, own, axis=2, keepdims=False)
        k_sel = gather(kb, selc)
        v_sel = gather(vb, selc)
        s_sel = jnp.einsum('bhqe,bhqjke->bhqjk', qc, k_sel).astype(jnp.float32) * scale
        key_pos = selc[..., None] * BS + jnp.arange(BS)
        s_sel = s_sel + bias_tab[head_idx, rel_bucket(t[:, None, None] - key_pos)].astype(jnp.float32)
        sel_valid = jnp.arange(top)[None, :] < (t // BS)[:, None]
        s_sel = jnp.where(sel_valid[:, :, None], s_sel, NEG_INF)
        s_own = jnp.einsum('bhqe,bhke->bhqk', qc, k_own).astype(jnp.float32) * scale
        dist_own = t[:, None] - (own * BS + jnp.arange(BS))[None, :]
        s_own = s_own + bias_tab[:, rel_bucket(dist_own)].astype(jnp.float32)[None]
        s_own = jnp.where(dist_own >= 0, s_own, NEG_INF)
        logits = jnp.concatenate([s_sel.reshape(B, H, MOBA_QCHUNK, top * BS), s_own], axis=-1)
        p = jax.nn.softmax(logits, axis=-1)
        p_sel = p[..., :top * BS].reshape(B, H, MOBA_QCHUNK, top, BS)
        p_own = p[..., top * BS:]
        return (jnp.einsum('bhqjk,bhqjke->bhqe', p_sel, v_sel.astype(jnp.float32))
                + jnp.einsum('bhqk,bhke->bhqe', p_own, v_own.astype(jnp.float32)))

    o = lax.map(one_chunk, (chunk(qp), chunk(sel), jnp.arange(nc)))
    o = jnp.moveaxis(o, 0, 2).reshape(B, H, Sp, E)[:, :, :S]
    return o

def memory_cross_attention(x, mem, g_x, g_mem, w_cq, w_ckv, w_co):
    B, S, _ = x.shape
    h = rms_norm_2(x, g_x)
    mn = rms_norm_2(mem, g_mem)
    q = (h @ w_cq).reshape(B, S, CROSS_HEADS, CROSS_HEAD_DIM)
    kv = mn @ w_ckv
    k, v = jnp.split(kv, 2, axis=-1)
    k = k.reshape(B, mem.shape[1], CROSS_HEADS, CROSS_HEAD_DIM)
    v = v.reshape(B, mem.shape[1], CROSS_HEADS, CROSS_HEAD_DIM)
    s = jnp.einsum('bshe,bmhe->bhsm', q, k).astype(jnp.float32) * CROSS_HEAD_DIM ** -0.5
    p = jax.nn.softmax(s, axis=-1)
    o = jnp.einsum('bhsm,bmhe->bshe', p, v.astype(jnp.float32)).reshape(B, S, D_MODEL)
    return o.astype(x.dtype) @ w_co

def second_inputs(seed: int = 0) -> dict:
    key = jax.random.key(seed)
    ks = jax.random.split(key, 24)
    f32 = jnp.float32

    def w(k, shape, fan_in):
        return jax.random.normal(k, shape, f32) * fan_in ** -0.5

    def gain(k, shape):
        return 1.0 + 0.05 * jax.random.normal(k, shape, f32)

    L = DEPTH_2
    return {
        "x": jax.random.normal(ks[0], (BATCH, SEQ, D_MODEL), f32),
        "mem": jax.random.normal(ks[1], (BATCH, N_MEM, D_MODEL), f32),
        "g_ffn1": gain(ks[2], (L, D_MODEL)),
        "w_ffn1_gu": w(ks[3], (L, D_MODEL, 2 * D_FF_2), D_MODEL),
        "w_ffn1_down": w(ks[4], (L, D_FF_2, D_MODEL), D_FF_2),
        "g_mix": gain(ks[5], (L, D_MODEL)),
        "w_in": w(ks[6], (L, D_MODEL, 3 * MIX_WIDTH), D_MODEL),
        "rel_bias": 0.5 * jax.random.normal(ks[7], (REL_BUCKETS, N_HEADS), f32),
        "g_out_a": gain(ks[8], (L, WIDTH_A)),
        "g_out_b": gain(ks[9], (L, WIDTH_B)),
        "w_out": w(ks[10], (L, MIX_WIDTH, D_MODEL), MIX_WIDTH),
        "g_cross": gain(ks[11], (L, D_MODEL)),
        "g_mem": gain(ks[12], (L, D_MODEL)),
        "w_cq": w(ks[13], (L, D_MODEL, D_MODEL), D_MODEL),
        "w_ckv": w(ks[14], (L, D_MODEL, 2 * D_MODEL), D_MODEL),
        "w_co": w(ks[15], (L, D_MODEL, D_MODEL), D_MODEL),
        "g_ffn2": gain(ks[16], (L, D_MODEL)),
        "w_ffn2_gu": w(ks[17], (L, D_MODEL, 2 * D_FF_2), D_MODEL),
        "w_ffn2_down": w(ks[18], (L, D_FF_2, D_MODEL), D_FF_2),
        "g_final": gain(ks[19], (D_MODEL,)),
    }

def second_block(x, mem, g_ffn1, w_ffn1_gu, w_ffn1_down, g_mix, w_in, rel_bias, g_out_a, g_out_b,
              w_out, g_cross, g_mem, w_cq, w_ckv, w_co, g_ffn2, w_ffn2_gu, w_ffn2_down, g_final):
    bias_a = rel_bias[:, :N_HEADS_A].T
    bias_b = rel_bias[:, N_HEADS_A:].T
    for layer in range(DEPTH_2):
        x = x + 0.5 * swiglu_2(rms_norm_2(x, g_ffn1[layer]), w_ffn1_gu[layer], w_ffn1_down[layer])
        h = rms_norm_2(x, g_mix[layer])
        proj = h @ w_in[layer]
        qa, ka, va, qb, kb, vb = jnp.split(
            proj, np.cumsum([WIDTH_A, WIDTH_A, WIDTH_A, WIDTH_B, WIDTH_B]).tolist(), axis=-1)
        oa = dilated_attention(split_heads_2(qa, N_HEADS_A, HEAD_DIM), split_heads_2(ka, N_HEADS_A, HEAD_DIM),
                               split_heads_2(va, N_HEADS_A, HEAD_DIM), bias_a)
        ob = moba_attention(split_heads_2(qb, N_HEADS_B, HEAD_DIM), split_heads_2(kb, N_HEADS_B, HEAD_DIM),
                            split_heads_2(vb, N_HEADS_B, HEAD_DIM), bias_b)
        ya = rms_norm_2(merge_heads_2(oa).astype(x.dtype), g_out_a[layer])
        yb = rms_norm_2(merge_heads_2(ob).astype(x.dtype), g_out_b[layer])
        x = x + jnp.concatenate([ya, yb], axis=-1) @ w_out[layer]
        x = x + memory_cross_attention(x, mem, g_cross[layer], g_mem[layer], w_cq[layer], w_ckv[layer], w_co[layer])
        x = x + 0.5 * swiglu_2(rms_norm_2(x, g_ffn2[layer]), w_ffn2_gu[layer], w_ffn2_down[layer])
    return rms_norm_2(x, g_final)


def setup_inputs(seed=0):
    out = dict(first_inputs(seed))
    for name, value in second_inputs(seed + 1).items():
        if name != "x":
            out[name + "_2"] = value
    return out


def reference(
    x, c, ctx, c_ctx, w_mod, b_mod, norm_gain, ffn_a_in, ffn_a_out, ffn_b_in, ffn_b_out,
    even_in, even_out, na_q_gain, na_k_gain, na_rpb, hy_conv_w, hy_conv_b, hy_fw1, hy_fb1,
    hy_fw2, hy_fb2, hy_fw3, hy_fb3, hy_fw4, hy_freq, hy_bias, ret_in, ret_out, ret_logit_f,
    ret_logit_b, mem_2, g_ffn1_2, w_ffn1_gu_2, w_ffn1_down_2, g_mix_2, w_in_2, rel_bias_2,
    g_out_a_2, g_out_b_2, w_out_2, g_cross_2, g_mem_2, w_cq_2, w_ckv_2, w_co_2, g_ffn2_2,
    w_ffn2_gu_2, w_ffn2_down_2, g_final_2,
):
    x = first_block(
        x, c, ctx, c_ctx, w_mod, b_mod, norm_gain, ffn_a_in, ffn_a_out, ffn_b_in, ffn_b_out,
        even_in, even_out, na_q_gain, na_k_gain, na_rpb, hy_conv_w, hy_conv_b, hy_fw1, hy_fb1,
        hy_fw2, hy_fb2, hy_fw3, hy_fb3, hy_fw4, hy_freq, hy_bias, ret_in, ret_out, ret_logit_f,
        ret_logit_b,
    )
    return second_block(
        x, mem_2, g_ffn1_2, w_ffn1_gu_2, w_ffn1_down_2, g_mix_2, w_in_2, rel_bias_2, g_out_a_2,
        g_out_b_2, w_out_2, g_cross_2, g_mem_2, w_cq_2, w_ckv_2, w_co_2, g_ffn2_2, w_ffn2_gu_2,
        w_ffn2_down_2, g_final_2,
    )


_drawn_inputs = setup_inputs


def setup_inputs(seed=0):
    import zlib

    import numpy as np

    out = dict(_drawn_inputs(seed))
    spreads = {}
    factors = {'na_q_gain': 8.0,
     'na_k_gain': 8.0,
     'na_rpb': 8.0,
     'hy_conv_b': 8.0,
     'hy_fb1': 6.974,
     'hy_fb2': 6.078,
     'hy_fb3': 5.008,
     'hy_freq': 8.0,
     'g_out_b_2': 3.424,
     'g_cross_2': 8.0,
     'g_mem_2': 8.0,
     'g_ffn2_2': 3.884}
    for name, (base, spread) in spreads.items():
        noise = np.random.default_rng([zlib.crc32(name.encode()), seed]).standard_normal(out[name].shape)
        drawn = base * np.exp(spread * noise) if base else spread * noise
        out[name] = jnp.asarray(drawn.astype(out[name].dtype))
    for name, factor in factors.items():
        out[name] = (out[name] * factor).astype(out[name].dtype)
    return out
```

```python
import math
from contextlib import ExitStack

import numpy as np

import concourse.bass as bass
from concourse import mybir

ACT = mybir.ActivationFunctionType
ALU = mybir.AluOpType
AXX = mybir.AxisListType.X
F32 = mybir.dt.float32
F16 = mybir.dt.float16
BF16 = mybir.dt.bfloat16

P = 128
D = 1024
DC = D // P
SEQ = 256
BOTH = 2 * SEQ
FF = 2816
FC = FF // P
N_MOD = 9
NEG = -1.0e30
EPS = 1e-6
GRID_W = 64
WIN_C = 16
NA_HEADS = 8
HY_W = 512
REL_BUCKETS = 32
N_HEADS_2 = 16
N_HEADS_A = 12
RET_HEADS = 4
KC_MAX = FC // 2


def shape_constants():
    f = np.float32
    eye = np.eye(P, dtype=f)
    block_ones = np.kron(np.eye(2, dtype=f), np.ones((64, 64), f))
    rot = np.zeros((P, P), f)
    for i in range(64):
        rot[64 + i, i] = -1.0
        rot[i, 64 + i] = 1.0
    mats = np.stack([eye, np.ones((P, P), f), block_ones, rot, eye[::-1]], 1)

    n = 2 * SEQ
    t = np.arange(SEQ)
    ang = 2.0 * np.pi * ((t[:, None] * t[None, :]) % n) / n
    cos, sin = np.cos(ang), np.sin(ang)
    nyq = (-1.0) ** t
    cos_n, sin_n = cos.copy(), sin.copy()
    cos_n[:, 0] = nyq
    sin_n[:, 0] = nyq
    fwd = np.stack([cos, cos_n, sin, sin_n], 0).reshape(4, 2, P, SEQ).transpose(2, 0, 1, 3)
    icos, isin = 2.0 * cos.T / n, 2.0 * sin.T / n
    icos[0] = 1.0 / n
    isin[0] = nyq / n
    inv = np.stack([icos, isin], 0).reshape(2, 2, P, SEQ).transpose(2, 0, 1, 3)

    pos = np.linspace(0.0, 1.0, SEQ, dtype=f)[:, None]
    w = f(2.0 * math.pi) * np.arange(SEQ, dtype=f)[:, None] / f(SEQ)
    bands = np.linspace(1e-4, 7, 8, dtype=f)
    emb = np.concatenate([pos, np.cos(bands * w), -np.sin(bands * w)], -1).astype(f)
    deltas = np.linspace(math.log(1e-2) / 1.5, math.log(1e-2) / 0.3, HY_W, dtype=f)
    window = np.exp(-pos * np.abs(deltas)).astype(f).reshape(2, P, HY_W).transpose(1, 0, 2)

    col = np.arange(GRID_W)
    start = np.clip(col - WIN_C // 2, 0, GRID_W - WIN_C)
    seen = (col[None] >= start[:, None]) & (col[None] < start[:, None] + WIN_C)
    seen = np.tile(seen, (2, SEQ // GRID_W))[::-1].astype(f)
    na_mask = np.stack([seen, (1.0 - seen) * f(NEG)], 1)

    dist = np.arange(SEQ - 1, -1, -1)
    large = 16 + (np.log(np.maximum(dist, 1).astype(f) / f(16)) / f(math.log(2048 / 16)) * f(16)).astype(np.int32)
    bucket = np.where(dist < 16, dist, np.minimum(large, REL_BUCKETS - 1))
    onehot = np.zeros((REL_BUCKETS, BOTH), f)
    onehot[bucket, np.arange(SEQ)] = 1.0
    count = (dist <= 128).astype(f) + (dist % 4 == 0) + (dist % 16 == 0)
    rel_mask = np.zeros((N_HEADS_2, BOTH), f)
    rel_mask[:, SEQ:] = NEG
    rel_mask[:N_HEADS_A, :SEQ][:, count == 0] = NEG
    per = np.concatenate([count, np.zeros(SEQ, f)])
    q, k = np.arange(SEQ)[:, None], np.arange(SEQ)[None]
    pair = per[np.minimum(SEQ - 1 - q + k, BOTH - 1)]
    rel_count = np.concatenate([pair[:P, :P], pair[P:, :]], 1)

    inv_f = f(10000.0) ** (-np.arange(64, dtype=f) / f(64))
    ang_r = (t // GRID_W).astype(f)[:, None] * inv_f
    ang_c = (t % GRID_W).astype(f)[:, None] * inv_f
    rope = np.stack([np.stack([np.tile(fn(a).T, (2, 1)) for fn in (np.cos, np.sin)], 0) for a in (ang_r, ang_c)], 0)
    rope = rope.transpose(2, 0, 1, 3)

    j, i = np.arange(SEQ)[:, None], np.arange(SEQ)[None]
    ret = np.stack([np.abs(i - j), i >= j, j >= i, i + SEQ - j, SEQ - i + j], 0)
    ret = ret.reshape(5, 2, P, SEQ).transpose(2, 0, 1, 3)
    return {n: np.ascontiguousarray(a, dtype=f) for n, a in dict(
        k_mats=mats, k_fwd=fwd, k_inv=inv, k_emb=emb.T, k_window=window, k_na_mask=na_mask,
        k_onehot=onehot, k_rel_mask=rel_mask, k_rel_count=rel_count, k_rope=rope, k_ret=ret).items()}


def program(nc, io, out):
    ctx = ExitStack()
    with ctx:
        def sb(name, shape, dt=F32):
            return ctx.enter_context(nc.sbuf_tensor(name, shape, dt))

        def sem(name):
            return ctx.enter_context(nc.semaphore(name))

        X = sb("X", [P, DC, BOTH])
        XH = sb("XH", [P, DC, BOTH], F16)
        XL = sb("XL", [P, DC, BOTH], BF16)
        W32 = sb("W32", [P, 2, 2, KC_MAX, P])
        WH = sb("WH", [P, 2, 2, KC_MAX, P], F16)
        WL = sb("WL", [P, 2, 2, KC_MAX, P], BF16)
        mats = sb("mats", [P, 5, P])
        prow = sb("prow", [P, 3, P])
        pcol = sb("pcol", [P, 3 * P])
        silu_c = sb("silu_c", [P, DC, 2])
        modT = sb("modT", [P, 2 * N_MOD * DC, 2])
        norm_a = sb("norm_a", [P, 6, DC, 2])
        lg = sb("lg", [P, 2 * RET_HEADS])
        lgt = sb("lgt", [P, 8, 2 * RET_HEADS])
        rstd = sb("rstd", [P, BOTH])
        var = sb("var", [P, BOTH])
        stats = sb("stats", [P, 3, 80])
        onorm = sb("onorm", [P, 12])
        embT = sb("embT", [17, SEQ])
        relb = sb("relb", [REL_BUCKETS, N_HEADS_2])
        relvec = sb("relvec", [N_HEADS_2, BOTH])
        arena = sb("arena", [P, 29184])
        PS = ctx.enter_context(nc.psum_tensor("PS", [P, 8, 512], F32))
        rel_dram = nc.dram_tensor("rel_scratch", (N_HEADS_2, BOTH), F32, kind="Internal").ap()

        def area(off, *shape, dt=F32):
            n = int(np.prod(shape)) // (2 if dt in (F16, BF16) else 1)
            a = arena[:, off:off + n]
            if dt is not F32:
                a = a.bitcast(dt)
            if len(shape) == 2:
                return a.rearrange("p (a b) -> p a b", a=shape[0])
            if len(shape) == 3:
                return a.rearrange("p (a b c) -> p a b c", a=shape[0], b=shape[1])
            return a

        eye, ones, block_ones, rot, flip = (mats[:, n, :] for n in range(5))
        SQ, SQ_mid = area(23040, DC, BOTH), area(13312, DC, BOTH)
        GH, GL = area(0, FC, BOTH, dt=F16), area(FC * SEQ, FC, BOTH, dt=BF16)
        ffn_s, ffn_g = area(2 * FC * SEQ, 2, BOTH), area(2 * FC * SEQ + 1024, 2, BOTH)
        x_tok = area(0, 4, D)
        h_window, h_sum, h_dif = area(4096, 2, HY_W), area(5120, 2, HY_W), area(6144, 2, HY_W)
        h_tmp, h_act = area(7168, 4, SEQ), area(8192, 2, SEQ)
        hy_taps = area(10240, 2, HY_W)
        fw = area(11264, 3 * 64 + D)[0:64]
        onehot, rel_mask = area(8704, BOTH), area(9216, BOTH)
        qk1, u1, V1 = area(0, 8, BOTH), area(4096, 12, BOTH), area(10240, 4, HY_W)
        filt, na_bias = area(13312, 5, HY_W), area(15872, 16, SEQ)
        dft, idft = area(19968, 8, SEQ), area(22016, 4, SEQ)
        na_mask = area(27136, 2, SEQ)
        probs, probsT = area(23040, 2, BOTH), area(24064, 2, BOTH)
        O1 = area(25088, 4, HY_W)
        hy_x0, hy_z, hy_zt = area(0, 4, BOTH), area(2048, 4, BOTH), area(10240, 4, HY_W)
        hy_xv, hy_spec, hy_y = area(27136, 4, BOTH), area(23040, 4, HY_W), area(4096, 8, HY_W)
        qr, kr, gr, Vr = area(0, 8, SEQ), area(2048, 8, BOTH), area(6144, 16, SEQ), area(10240, 4, 2 * D)
        decay, ret_k, rope = area(18432, 16, SEQ), area(22528, 5, BOTH), area(25088, 4, SEQ)
        ret_p, rope_t, ret_e = area(26112, 8, SEQ), area(28160, 4, SEQ), area(26112, 4, BOTH)
        ret_y, ret_sq = area(22528, 8, SEQ), area(25088, 4, SEQ)
        qk2, V2, rel_bias = area(0, 16, SEQ), area(4096, 2, D), area(13312, 16, 384)
        rel_count, mem_tok = area(19456, 384), area(19840, 2, D)
        qkc, Vc, memX = area(0, 16, SEQ), area(4096, 2, D), area(6144, DC, SEQ)
        MH, ML = area(8192, DC, SEQ, dt=F16), area(9216, DC, SEQ, dt=BF16)
        SQM = area(10240, DC, SEQ)
        O2, O2n = area(25088, 2, D), area(27136, 2, D)
        out_tok = area(19840, 2, D)
        ZH, ZL = (a[:, :, :].rearrange("p c (h t) -> p (c h) t", h=2) for a in (XH, XL))

        loaded = [[sem(f"loaded_{k}{t}") for t in range(2)] for k in range(2)]
        mod_used = sem("mod_used")
        hi_ready = sem("hi_ready")
        lo_ready = sem("lo_ready")
        block_used = sem("block_used")
        units_drained = sem("units_drained")
        silu_done, gh_done, gl_done = sem("silu_done"), sem("gh_done"), sem("gl_done")
        sq_ready, ms_ready, inv_ready, rstd_ready = sem("sq_ready"), sem("ms_ready"), sem("inv_ready"), sem("rstd_ready")
        t_ready, h_ready, xh_ready, xl_ready = sem("t_ready"), sem("h_ready"), sem("xh_ready"), sem("xl_ready")
        dve_chain, act_chain, pool_chain = sem("dve_chain"), sem("act_chain"), sem("pool_chain")
        mats_loaded, rows_clear, rows_loaded, x_loaded = sem("mats_loaded"), sem("rows_clear"), sem("rows_loaded"), sem("x_loaded")
        rows_turned, pcol_ready, x_turned, x_ready = sem("rows_turned"), sem("pcol_ready"), sem("x_turned"), sem("x_ready")
        silu_c_ready, mod_ready = sem("silu_c_ready"), sem("mod_ready")
        lg_loaded, lg_abs, lg_exp, lg_u, lg_ln, lg_ready = (sem(n) for n in ("lg_loaded", "lg_abs", "lg_exp", "lg_u", "lg_ln", "lg_ready"))
        filt_loaded, filt_mm, filt_arg, filt_sin, filt_win, filt_sd, filt_k, filt_ready = (
            sem(n) for n in ("filt_loaded", "filt_mm", "filt_arg", "filt_sin", "filt_win", "filt_sd", "filt_k", "filt_ready"))
        rel_loaded, rel_mm, rel_vec, rel_stored, rel_back = (sem(n) for n in ("rel_loaded", "rel_mm", "rel_vec", "rel_stored", "rel_back"))
        nab_loaded, nab_ready = sem("nab_loaded"), sem("nab_ready")
        qk_sq, qk_ms, qk_inv, qk_rstd, qk_ready = (sem(n) for n in ("qk_sq", "qk_ms", "qk_inv", "qk_rstd", "qk_ready"))
        scores_ready, max_ready, probs_ready, probs_counted = (sem(n) for n in ("scores_ready", "max_ready", "probs_ready", "probs_counted"))
        turned_ready, turned_copied, out_ready, out_done, denoms = (
            sem(n) for n in ("turned_ready", "turned_copied", "out_ready", "out_done", "denoms"))
        ot_turned, ot_hi, ot_lo = sem("ot_turned"), sem("ot_hi"), sem("ot_lo")
        conv_mid, conv_ready, z_ready = sem("conv_mid"), sem("conv_ready"), sem("z_ready")
        zt_turned, zt_copied, spec_mm, spec_copied, y_re, y_im = (
            sem(n) for n in ("zt_turned", "zt_copied", "spec_mm", "spec_copied", "y_re", "y_im"))
        inv_mm, hy_out, hy_hi, hy_lo = sem("inv_mm"), sem("hy_out"), sem("hy_hi"), sem("hy_lo")
        ret_loaded, dec_exp, dec_used, dec_ready = sem("ret_loaded"), sem("dec_exp"), sem("dec_used"), sem("dec_ready")
        rope_mm, rope_cos, rope_ready = sem("rope_mm"), sem("rope_cos"), sem("rope_ready")
        rs_ready, rp_ready, ry_ready, ryc_ready = sem("rs_ready"), sem("rp_ready"), sem("ry_ready"), sem("ryc_ready")
        rm_ready, rc_ready, rq_ready, rv_ready, ri_ready, rr_ready, rn_ready = (
            sem(n) for n in ("rm_ready", "rc_ready", "rq_ready", "rv_ready", "ri_ready", "rr_ready", "rn_ready"))
        rg_ready, rz_ready, zh_ready, zl_ready = sem("rg_ready"), sem("rz_ready"), sem("zh_ready"), sem("zl_ready")
        on_sq, on_inv, on_rstd, on_ready = sem("on_sq"), sem("on_inv"), sem("on_rstd"), sem("on_ready")
        mem_loaded, mem_turned, mem_ready = sem("mem_loaded"), sem("mem_turned"), sem("mem_ready")
        cnt_loaded, fin_turned, fin_copied, stored = sem("cnt_loaded"), sem("fin_turned"), sem("fin_copied"), sem("stored")

        ROWS = [("b_mod", 0, 0, 72), ("norm_gain", None, 72, 48), ("c", None, 120, 8),
                ("b_mod", 1, 128, 72), ("hy_conv_w", None, 200, 36), ("hy_conv_b", None, 236, 12), ("hy_bias", None, 248, 4),
                ("c_ctx", None, 256, 8), ("g_ffn1_2", None, 264, 8), ("g_mix_2", None, 272, 8), ("g_out_a_2", None, 280, 6),
                ("g_out_b_2", None, 286, 2), ("g_cross_2", None, 288, 8), ("g_mem_2", None, 296, 8),
                ("g_ffn2_2", None, 304, 8), ("g_final_2", None, 312, 8)]
        SHORT = [("na_q_gain", 320, 2), ("na_k_gain", 321, 2), ("hy_fb1", 322, 1), ("hy_fb2", 323, 1),
                 ("hy_fb3", 324, 1), ("hy_freq", 325, 1)]
        COL = {(n, i): at for n, i, at, _ in ROWS} | {(n, None): at for n, at, _ in SHORT}
        N_ROWS = len(ROWS) + sum(m for _, _, m in SHORT)

        def col(name, c=0, rows=P):
            at = COL[(name, None)] + c
            return pcol[0:rows, at:at + 1]

        def mod_col(layer, m, c, s):
            return modT[:, (layer * N_MOD + m) * DC + c, s:s + 1]

        def flat(ap):
            n = len(ap.shape)
            return ap.rearrange({1: "a -> a", 2: "a b -> (a b)", 3: "a b c -> (a b c)"}[n])

        GEMMS = []

        def gemm(name, kind, w, kc, blocks, T, cols, rhs, parts=1, tok=False, dest=None, scale=1.0, gate=None, ffn=None, need=()):
            g = dict(name=name, kind=kind, w=w, kc=kc, blocks=blocks, T=T, cols=cols, rhs=rhs, parts=parts, tok=tok,
                     dest=dest, scale=scale, gate=gate, ffn=ffn, units=blocks // parts, need=list(need))
            last = GEMMS[-1] if GEMMS else None
            g["w0"] = last["w0"] + last["blocks"] if last else 0
            g["u0"] = last["u0"] + last["units"] if last else 2 * N_MOD * DC // 2
            assert blocks % (2 * parts) == 0
            GEMMS.append(g)
            return g

        def x_rhs(kp, c, T, kc):
            return XH[:, c, 0:T], XL[:, c, 0:T]

        def z_rhs(kp, c, T, kc):
            return ZH[:, kp * kc + c, 0:T], ZL[:, kp * kc + c, 0:T]

        def g_rhs(kp, c, T, kc):
            return GH[:, kp * kc + c, 0:T], GL[:, kp * kc + c, 0:T]

        def m_rhs(kp, c, T, kc):
            return MH[:, c, 0:T], ML[:, c, 0:T]

        ffns = []

        def ffn(name, w_in, w_out, T, gate, norm):
            f = len(ffns)
            ffns.append(name)
            gemm(name + "_in", "ffn", w_in, DC, FC, T, None, x_rhs, ffn=f, need=[(xl_ready, DC * (norm + 1))])
            return gemm(name + "_out", "resid", w_out, KC_MAX, 8, T, 256, g_rhs, parts=2, gate=gate, need=[(gl_done, FC * (f + 1))])

        def gates(layer, m):
            return lambda c, s: mod_col(layer, m, c, s)

        w = io
        G = {}
        G["f0a"] = ffn("ffn_0a", w["ffn_a_in"][0], w["ffn_a_out"][0], BOTH, gates(0, 2), 0)
        n1 = [(xl_ready, DC * 2)]
        G["qk1"] = gemm("even_qk", "store", w["even_in"][0], DC, 4, BOTH, 256, x_rhs, dest=qk1, need=n1)
        G["v1"] = gemm("even_v", "store", w["even_in"][0][:, 1024:], DC, 2, BOTH, 256, x_rhs, tok=True, dest=V1)
        G["u1"] = gemm("even_u", "store", w["even_in"][0][:, 1536:], DC, 6, BOTH, 256, x_rhs, dest=u1)
        G["o1"] = gemm("even_out", "resid", w["even_out"][0], DC, 4, BOTH, 256, x_rhs, gate=gates(0, 5),
                       need=[(ot_lo, 4), (hy_lo, 4)])
        G["f0b"] = ffn("ffn_0b", w["ffn_b_in"][0], w["ffn_b_out"][0], BOTH, gates(0, 8), 2)
        G["f1a"] = ffn("ffn_1a", w["ffn_a_in"][1], w["ffn_a_out"][1], BOTH, gates(1, 2), 3)
        n4 = [(xl_ready, DC * 5)]
        G["qr"] = gemm("ret_q", "store", w["ret_in"][0], DC, 4, SEQ, 256, x_rhs, dest=qr, need=n4)
        G["kr"] = gemm("ret_k", "store", w["ret_in"][0][:, 1024:], DC, 4, BOTH, 256, x_rhs, dest=kr)
        G["vr"] = gemm("ret_v", "store", w["ret_in"][0][:, 2048:], DC, 8, BOTH, 256, x_rhs, tok=True, dest=Vr)
        G["gr"] = gemm("ret_g", "store", w["ret_in"][0][:, 4096:], DC, 8, SEQ, 256, x_rhs, dest=gr)
        G["or"] = gemm("ret_out", "resid", w["ret_out"][0], DC, 8, SEQ, 256, z_rhs, parts=2, gate=gates(1, 5),
                       need=[(zl_ready, 16)])
        G["f1b"] = ffn("ffn_1b", w["ffn_b_in"][1], w["ffn_b_out"][1], SEQ, gates(1, 8), 5)
        G["f2a"] = ffn("ffn_2a", w["w_ffn1_gu_2"][0], w["w_ffn1_down_2"][0], SEQ, 0.5, 6)
        wi = w["w_in_2"][0]
        n7 = [(xl_ready, DC * 8)]
        G["q2"] = gemm("mix_q", "store", wi, DC, 4, SEQ, [0, 256, 512, 2304], x_rhs, dest=qk2[:, 0:8], scale=0.125, need=n7)
        G["k2"] = gemm("mix_k", "store", wi, DC, 4, SEQ, [768, 1024, 1280, 2560], x_rhs, dest=qk2[:, 8:16])
        G["v2"] = gemm("mix_v", "store", wi, DC, 4, SEQ, [1536, 1792, 2048, 2816], x_rhs, tok=True, dest=V2)
        G["o2"] = gemm("mix_out", "resid", w["w_out_2"][0], DC, 4, SEQ, 256, x_rhs, gate=1.0, need=[(ot_lo, 4 + 8)])
        G["qc"] = gemm("cross_q", "store", w["w_cq_2"][0], DC, 4, SEQ, 256, x_rhs, dest=qkc[:, 0:8], scale=0.0625,
                       need=[(xl_ready, DC * 9)])
        G["kc"] = gemm("cross_k", "store", w["w_ckv_2"][0], DC, 4, SEQ, 256, m_rhs, dest=qkc[:, 8:16], need=[(xl_ready, DC * 10)])
        G["vc"] = gemm("cross_v", "store", w["w_ckv_2"][0][:, 1024:], DC, 4, SEQ, 256, m_rhs, tok=True, dest=Vc)
        G["oc"] = gemm("cross_out", "resid", w["w_co_2"][0], DC, 4, SEQ, 256, x_rhs, gate=1.0, need=[(ot_lo, 4 + 8 + 8)])
        G["f2b"] = ffn("ffn_2b", w["w_ffn2_gu_2"][0], w["w_ffn2_down_2"][0], SEQ, 0.5, 10)
        MOD_BLOCKS = 2 * N_MOD * DC // 2

        def drained(g):
            return g["u0"] + g["units"]

        def segs(T):
            return [(s, slice(s * SEQ, (s + 1) * SEQ)) for s in range(T // SEQ)]

        UNITS = []

        def na_units():
            for part in range(2):
                for h in range(NA_HEADS):
                    rows = slice(64 * (h % 2), 64 * (h % 2) + 64)
                    for qt in range(2):
                        q0, k0 = SEQ * part + P * qt, SEQ * part
                        UNITS.append(dict(
                            q=[qk1[rows, h // 2, q0:q0 + P]], k=[qk1[rows, 4 + h // 2, k0:BOTH]], nk=BOTH - k0,
                            bias=na_bias[:, 2 * h + qt, :] if part == 0 else None, count=None,
                            v=[V1[:, k0 // P + t, 64 * h:64 * h + 64] for t in range((BOTH - k0) // P)],
                            dst=O1[:, 2 * part + qt, 64 * h:64 * h + 64]))

        def rel_units():
            for h in range(N_HEADS_2):
                rows = slice(64 * (h % 2), 64 * (h % 2) + 64)
                for qt in range(2):
                    nk, at = P * (qt + 1), P * qt
                    UNITS.append(dict(
                        q=[qk2[rows, h // 2, P * qt:P * qt + P]], k=[qk2[rows, 8 + h // 2, 0:nk]], nk=nk,
                        bias=rel_bias[:, h, at:at + nk], count=rel_count[:, at:at + nk] if h < N_HEADS_A else None,
                        v=[V2[:, t, 64 * h:64 * h + 64] for t in range(qt + 1)], dst=O2[:, qt, 64 * h:64 * h + 64]))

        def cross_units():
            for h in range(4):
                for qt in range(2):
                    UNITS.append(dict(
                        q=[qkc[:, 2 * h + c, P * qt:P * qt + P] for c in range(2)], k=[qkc[:, 8 + 2 * h + c, :] for c in range(2)],
                        nk=SEQ, bias=None, count=None, v=[Vc[:, t, SEQ * h:SEQ * h + SEQ] for t in range(2)],
                        dst=O2[:, qt, SEQ * h:SEQ * h + SEQ]))

        na_units()
        NA = (0, len(UNITS))
        rel_units()
        REL = (NA[1], len(UNITS))
        cross_units()
        CROSS = (REL[1], len(UNITS))
        counted = [sum(u["count"] is not None for u in UNITS[:n + 1]) for n in range(len(UNITS))]

        def drained_chunk(g):
            return lambda c: (units_drained, g["u0"] + c // 2 + 1)

        def mod_norm(layer, j, T, wait):
            return dict(src=X, T=T, a=lambda c, s: norm_a[:, 3 * layer + j, c, s:s + 1],
                        b=lambda c, s: mod_col(layer, 3 * j, c, s), h=XH, l=XL, wait=wait, sq=SQ_mid if (layer, j) in ((0, 2), (1, 0), (1, 1)) else SQ)

        def gain_norm(name, wait, src=X, h=XH, l=XL, sq=SQ):
            return dict(src=src, T=SEQ, a=lambda c, s: col(name, c), b=None, h=h, l=l, wait=wait, sq=sq)

        NORMS = [mod_norm(0, 0, BOTH, lambda c: (x_ready, c + 1)), mod_norm(0, 1, BOTH, drained_chunk(G["f0a"])),
                 mod_norm(0, 2, BOTH, drained_chunk(G["o1"])), mod_norm(1, 0, BOTH, drained_chunk(G["f0b"])),
                 mod_norm(1, 1, BOTH, drained_chunk(G["f1a"])), mod_norm(1, 2, SEQ, drained_chunk(G["or"])),
                 gain_norm("g_ffn1_2", drained_chunk(G["f1b"])), gain_norm("g_mix_2", drained_chunk(G["f2a"])),
                 gain_norm("g_cross_2", drained_chunk(G["o2"])),
                 gain_norm("g_mem_2", lambda c: (mem_ready, c + 1), src=memX, h=MH, l=ML, sq=SQM),
                 gain_norm("g_ffn2_2", drained_chunk(G["oc"])), gain_norm("g_final_2", drained_chunk(G["f2b"]), h=None)]
        BANK_N = 4

        block = ctx.enter_context(nc.Block())

        @block.sync
        def _(sp):
            sp.dma_start(x_tok[:, 0:2, :], io["x"][0].rearrange("(t p) d -> p t d", p=P)).then_inc(x_loaded, 16)
            sp.dma_start(x_tok[:, 2:4, :], io["ctx"][0].rearrange("(t p) d -> p t d", p=P)).then_inc(x_loaded, 16)

            def mod_load(k, layer, col0):
                for t in range(2):
                    src = io["w_mod"][layer].rearrange("(c p) n -> p c n", p=P)[:, :, bass.ds(col0 + P * t, P)]
                    sp.dma_start(W32[:, k, t, 0:DC, :], src).then_inc(loaded[k][t], 16)

            for layer in range(2):
                first = 0
                if layer == 0:
                    for k in range(2):
                        mod_load(k, 0, 256 * k)
                    first = 1
                with sp.Fori(first, MOD_BLOCKS // 4) as i:
                    for k in range(2):
                        sp.wait_ge(mod_used, layer * (MOD_BLOCKS // 2) + 2 * i + k - 1)
                        mod_load(k, layer, 512 * i + 256 * k)

            def load(g, wv, k, t, col0, kp):
                src = wv[:, kp * g["kc"]:(kp + 1) * g["kc"], bass.ds(col0, P)]
                sp.dma_start(W32[:, k, t, 0:g["kc"], :], src).then_inc(loaded[k][t], 16)

            for g in GEMMS:
                wv = g["w"].rearrange("(c p) n -> p c n", p=P)

                def pair(i, slot_free, g=g, wv=wv):
                    for k in range(2):
                        for t in range(2):
                            slot_free(k, t)
                            if g["kind"] == "ffn":
                                load(g, wv, k, t, (2 * i + k) * P + t * FF, 0)
                            elif g["parts"] == 2:
                                load(g, wv, k, t, 256 * i + P * t, k)
                            elif g["cols"] == 256:
                                load(g, wv, k, t, 512 * i + 256 * k + P * t, 0)
                            else:
                                load(g, wv, k, t, g["cols"][2 * i + k] + P * t, 0)

                def split_before(i, w0=g["w0"]):
                    return lambda k, t: sp.wait_ge(lo_ready, 2 * (w0 - 2 + k) + t + 1 + 4 * i)

                n = g["blocks"] // 2
                if g["w0"] == 0:
                    pair(0, lambda k, t: sp.wait_ge(mod_used, MOD_BLOCKS - 1 + k))
                    with sp.Fori(1, n) as i:
                        pair(i, split_before(i))
                elif isinstance(g["cols"], list):
                    for i in range(n):
                        pair(i, split_before(i))
                else:
                    with sp.Fori(0, n) as i:
                        pair(i, split_before(i))

            sp.wait_ge(stored, 32)

        @block.tensor
        def _(pe):
            mm, turn = pe.matmul, pe.transpose

            def pe_gemm(g):
                kc, T = g["kc"], g["T"]

                def one(k, kp, pair, w, u):
                    if kp == 0:
                        pe.wait_ge(units_drained, u - 1)
                    if g["tok"]:
                        pe.wait_ge(lo_ready, 2 * w + 2)
                        for tt in range(T // P):
                            dst = PS[:, 2 * pair + tt // 2, 256 * (tt % 2):256 * (tt % 2) + 256].rearrange("p (a b) -> p a b", a=2)
                            for c in range(kc):
                                xh, xl = g["rhs"](kp, c, T, kc)
                                xh, xl = xh[:, P * tt:P * tt + P], xl[:, P * tt:P * tt + P]
                                wh, wl = WH[:, k, :, c, :], WL[:, k, :, c, :]
                                mm(dst, xh, wh, start=(c == 0), stop=False)
                                mm(dst, xh, wl, start=False, stop=False)
                                ins = mm(dst, xl, wh, start=False, stop=(c == kc - 1))
                    else:
                        for t in range(2):
                            pe.wait_ge(lo_ready, 2 * w + t + 1)
                            dst = PS[:, 2 * pair + t, 0:T]
                            for c in range(kc):
                                xh, xl = g["rhs"](kp, c, T, kc)
                                wh, wl = WH[:, k, t, c, :], WL[:, k, t, c, :]
                                mm(dst, wh, xh, start=(kp == 0 and c == 0), stop=False, skip_group_check=True)
                                mm(dst, wh, xl, start=False, stop=False, skip_group_check=True)
                                ins = mm(dst, wl, xh, start=False, stop=(kp == g["parts"] - 1 and c == kc - 1),
                                         skip_group_check=True)
                    ins.then_inc(block_used, 1)

                for s, v in g["need"]:
                    pe.wait_ge(s, v)
                with pe.Fori(0, g["units"] // 2) as i:
                    for b in range(2 * g["parts"]):
                        pair, kp = b // g["parts"], b % g["parts"]
                        one(b % 2, kp, pair, g["w0"] + b + 2 * g["parts"] * i, g["u0"] + pair + 2 * i)

            def pe_norm(n):
                N = NORMS[n]
                for c in range(DC):
                    pe.wait_ge(sq_ready, DC * n + c + 1)
                    ins = mm(PS[:, BANK_N, 0:N["T"]], ones, N["sq"][:, c, 0:N["T"]], start=(c == 0), stop=(c == DC - 1))
                ins.then_inc(ms_ready, 1)

            def pe_attend(span):
                lo, hi = span
                for u in range(lo, hi + 2):
                    if u < hi:
                        U = UNITS[u]
                        s = PS[:, 4 + u % 2, 0:U["nk"]]
                        if u - lo >= 2:
                            pe.wait_ge(probs_ready, u - 1)
                        for c, (q, k) in enumerate(zip(U["q"], U["k"])):
                            ins = mm(s, q, k, start=(c == 0), stop=(c == len(U["q"]) - 1 and U["bias"] is None), skip_group_check=True)
                        if U["bias"] is not None:
                            nb = U["bias"].shape[-1]
                            ins = mm(s[:, 0:nb], flip, U["bias"],
                                     start=False, stop=True, skip_group_check=True)
                        ins.then_inc(scores_ready, 1)
                    if lo <= u - 1 < hi:
                        U = UNITS[u - 1]
                        if U["count"] is None:
                            pe.wait_ge(probs_ready, u)
                        else:
                            pe.wait_ge(probs_counted, counted[u - 1])
                        if u - 1 - lo >= 2:
                            pe.wait_ge(turned_copied, u - 2)
                        for t in range(U["nk"] // P):
                            ins = turn(PS[:, 2 + (u - 1) % 2, P * t:P * t + P], probs[:, (u - 1) % 2, P * t:P * t + P], eye)
                        ins.then_inc(turned_ready, 1)
                    if u - 2 >= lo:
                        U = UNITS[u - 2]
                        pe.wait_ge(turned_copied, u - 1)
                        if u - 2 - lo >= 2:
                            pe.wait_ge(out_done, u - 3)
                        dv = U["dst"].shape[-1]
                        for t, v in enumerate(U["v"]):
                            ins = mm(PS[:, 6 + u % 2, 0:dv], probsT[:, u % 2, P * t:P * t + P], v,
                                     start=(t == 0), stop=(t == len(U["v"]) - 1))
                        ins.then_inc(out_ready, 1)

            def pe_turn_out(O, tiles, n, base, need):
                pe.wait_ge(*need)
                for c in range(n):
                    if c >= 2:
                        pe.wait_ge(ot_lo, base + c - 1)
                    for t in range(tiles):
                        ins = turn(PS[:, 4 + c % 2, P * t:P * t + P], O[:, t, P * c:P * c + P], eye)
                    ins.then_inc(ot_turned, 1)

            pe.wait_ge(mats_loaded, 16)
            pe.wait_ge(rows_loaded, 16 * N_ROWS)
            for n in range(3):
                ins = turn(PS[:, 4, P * n:P * n + P], prow[:, n, :], eye)
            ins.then_inc(rows_turned, 1)
            pe.wait_ge(x_loaded, 32)
            for c in range(DC):
                if c % 4 == 0:
                    pe.wait_ge(pcol_ready, 1)
                if c >= 4:
                    pe.wait_ge(x_ready, c - 3)
                for t in range(4):
                    ins = turn(PS[:, 4 + c % 4, P * t:P * t + P], x_tok[:, t, P * c:P * c + P], eye)
                ins.then_inc(x_turned, 1)
            pe.wait_ge(filt_loaded, 16 * 8)
            pe.wait_ge(x_ready, DC)
            for n in range(3):
                if n == 0:
                    ins = mm(PS[0:64, 4, 0:SEQ], fw[0:17, 0:64], embT[:, :], start=True, stop=True)
                else:
                    pe.wait_ge(filt_sin, n)
                    ins = mm(PS[0:64, 4, 0:SEQ], fw[:, 64 * n:64 * n + 64], h_act[0:64, (n - 1) % 2, :], start=True, stop=True)
                ins.then_inc(filt_mm, 1)
            pe.wait_ge(filt_sin, 3)
            for n in range(4):
                ins = mm(PS[:, 4 + n, :], h_act[0:64, 0, P * (n // 2):P * (n // 2) + P],
                         fw[:, 192 + HY_W * (n % 2):192 + HY_W * (n % 2) + HY_W], start=True, stop=True)
                ins.then_inc(filt_mm, 1)
            pe.wait_ge(filt_sd, 4)
            for n, (m, f, h) in enumerate([(0, 0, h_sum), (0, 1, h_sum), (1, 0, h_sum), (2, 0, h_dif), (2, 1, h_dif)]):
                if n == 4:
                    pe.wait_ge(filt_ready, 1)
                for t in range(2):
                    ins = mm(PS[:, 4 + n % 4, :], dft[:, 2 * m + t, P * f:P * f + P], h[:, t, :], start=(t == 0), stop=(t == 1))
                ins.then_inc(filt_k, 1)
            pe.wait_ge(rel_loaded, 48)
            pe.wait_ge(filt_ready, 5)
            mm(PS[0:N_HEADS_2, 5, :], relb[:, :], onehot[0:REL_BUCKETS, :], start=True, stop=True).then_inc(rel_mm, 1)
            pe.wait_ge(silu_c_ready, 2)

            def mod_pair(i, first):
                for k in range(2):
                    if not first:
                        pe.wait_ge(units_drained, 2 * i + k - 1)
                    for t in range(2):
                        pe.wait_ge(loaded[k][t], 16 * i + 16)
                        for c in range(DC):
                            ins = mm(PS[:, 2 * k, 2 * t:2 * t + 2], W32[:, k, t, c, :], silu_c[:, c, :],
                                     start=(c == 0), stop=(c == DC - 1), skip_group_check=True)
                    ins.then_inc(mod_used, 1)

            mod_pair(0, True)
            with pe.Fori(1, MOD_BLOCKS // 2) as i:
                mod_pair(i, False)

            pe_norm(0)
            gi = {g["name"]: g for g in GEMMS}
            pe_gemm(gi["ffn_0a_in"])
            pe_gemm(gi["ffn_0a_out"])
            pe_norm(1)
            for n in ("even_qk", "even_v", "even_u"):
                pe_gemm(gi[n])
            for t in range(8):
                pe.wait_ge(qk_sq, t + 1)
                if t >= 2:
                    pe.wait_ge(qk_inv, t - 1)
                mm(PS[:, 4 + t % 2, :], block_ones, area(23040 + 512 * (t % 2), BOTH), start=True, stop=True).then_inc(qk_ms, 1)
            pe.wait_ge(qk_ready, 8)
            pe.wait_ge(nab_ready, 16)
            pe.wait_ge(units_drained, drained(gi["even_v"]))
            pe_attend(NA)
            pe_turn_out(O1, 4, 4, 0, (out_done, NA[1]))
            pe.wait_ge(z_ready, 4)
            for t in range(4):
                for c in range(4):
                    ins = turn(PS[:, (6, 7, 2, 3)[t], P * c:P * c + P], hy_z[:, c, P * t:P * t + P], eye)
                ins.then_inc(zt_turned, 1)
            pe.wait_ge(zt_copied, 4)
            pe.wait_ge(ot_lo, 4)
            for s in range(2):
                for n in range(4):
                    if s == 1:
                        pe.wait_ge(spec_copied, n + 1)
                    m = 0 if n < 2 else 3
                    for t in range(2):
                        ins = mm(PS[:, 4 + n, :], dft[:, 2 * m + t, P * (n % 2):P * (n % 2) + P], hy_zt[:, 2 * s + t, :],
                                 start=(t == 0), stop=(t == 1))
                    ins.then_inc(spec_mm, 1)
            pe.wait_ge(y_re, 4)
            pe.wait_ge(y_im, 4)
            for c in range(4):
                if c >= 2:
                    pe.wait_ge(hy_out, c - 1)
                for s in range(2):
                    for n in range(4):
                        ins = mm(PS[:, 2 + c % 2, SEQ * s:SEQ * s + SEQ], hy_y[:, 4 * s + n, P * c:P * c + P], idft[:, n, :],
                                 start=(n == 0), stop=(n == 3), skip_group_check=True)
                ins.then_inc(inv_mm, 1)
            pe_gemm(gi["even_out"])
            pe_norm(2)
            pe_gemm(gi["ffn_0b_in"])
            pe_gemm(gi["ffn_0b_out"])
            pe_norm(3)
            pe_gemm(gi["ffn_1a_in"])
            pe_gemm(gi["ffn_1a_out"])
            pe_norm(4)
            for n in ("ret_q", "ret_k", "ret_v", "ret_g"):
                pe_gemm(gi[n])
            for t in range(16):
                pe.wait_ge(units_drained, drained(gi["ret_q"] if t < 8 else gi["ret_k"]))
                if t >= 2:
                    pe.wait_ge(rope_ready, t - 1)
                src = qr[:, t, :] if t < 8 else kr[:, t - 8, 0:SEQ]
                mm(PS[:, 4 + t % 2, 0:SEQ], rot, src, start=True, stop=True).then_inc(rope_mm, 1)
            pe.wait_ge(rope_ready, 16)
            pe.wait_ge(units_drained, drained(gi["ret_g"]))
            for h in range(RET_HEADS):
                for t in range(4):
                    n = 4 * h + t
                    if n >= 2:
                        pe.wait_ge(rp_ready, n - 1)
                    for c in range(2):
                        ins = mm(PS[:, 4 + t % 2, 0:SEQ], kr[:, 2 * h + c, P * t:P * t + P], qr[:, 2 * h + c, :],
                                 start=(c == 0), stop=(c == 1))
                    ins.then_inc(rs_ready, 1)
                pe.wait_ge(rp_ready, 4 * h + 4)
                if h:
                    pe.wait_ge(ryc_ready, 4 * h)
                for e in range(4):
                    for t in range(4):
                        ins = mm(PS[:, 6 + e // 2, SEQ * (e % 2):SEQ * (e % 2) + SEQ], Vr[:, t, 512 * h + P * e:512 * h + P * e + P],
                                 ret_p[:, 4 * (h % 2) + t, :], start=(t == 0), stop=(t == 3), skip_group_check=True)
                    ins.then_inc(ry_ready, 1)
                for e in range(4):
                    pe.wait_ge(ryc_ready, 4 * h + e + 1)
                    ins = mm(PS[:, 2, 0:SEQ], ones, ret_y[:, 4 * (h % 2) + e, :], start=(e == 0), stop=(e == 3))
                ins.then_inc(rm_ready, 1)
                for e in range(4):
                    pe.wait_ge(rq_ready, 4 * h + e + 1)
                    ins = mm(PS[:, 3, 0:SEQ], ones, ret_sq[:, e, :], start=(e == 0), stop=(e == 3))
                ins.then_inc(rv_ready, 1)
            pe_gemm(gi["ret_out"])
            pe_norm(5)
            pe_gemm(gi["ffn_1b_in"])
            pe_gemm(gi["ffn_1b_out"])
            pe_norm(6)
            pe_gemm(gi["ffn_2a_in"])
            pe_gemm(gi["ffn_2a_out"])
            pe_norm(7)
            for n in ("mix_q", "mix_k", "mix_v"):
                pe_gemm(gi[n])
            pe.wait_ge(units_drained, drained(gi["mix_v"]))
            pe.wait_ge(rel_back, 32)
            pe_attend(REL)
            pe_turn_out(O2n, 2, 8, 4, (on_ready, 4))
            pe_gemm(gi["mix_out"])
            pe_norm(8)
            pe_gemm(gi["cross_q"])
            pe.wait_ge(mem_loaded, 16)
            for c in range(DC):
                if c >= 2:
                    pe.wait_ge(mem_ready, c - 1)
                for t in range(2):
                    ins = turn(PS[:, 6 + c % 2, P * t:P * t + P], mem_tok[:, t, P * c:P * c + P], eye)
                ins.then_inc(mem_turned, 1)
            pe_norm(9)
            pe_gemm(gi["cross_k"])
            pe_gemm(gi["cross_v"])
            pe.wait_ge(units_drained, drained(gi["cross_v"]))
            pe_attend(CROSS)
            pe_turn_out(O2, 2, 8, 12, (out_done, CROSS[1]))
            pe_gemm(gi["cross_out"])
            pe_norm(10)
            pe_gemm(gi["ffn_2b_in"])
            pe_gemm(gi["ffn_2b_out"])
            pe_norm(11)
            pe.wait_ge(h_ready, DC * 12)
            for t in range(2):
                for c in range(DC):
                    ins = turn(PS[:, 4 + 2 * t + c // 4, P * (c % 4):P * (c % 4) + P], SQ[:, c, P * t:P * t + P], eye)
                    if c % 4 == 3:
                        ins.then_inc(fin_turned, 1)

        @block.scalar
        def _(act):
            def copy(dst, src, scale=1.0):
                return act.activation(dst, src, ACT.Copy, scale=scale)

            def split(g, i, k, first=False):
                if not (first and g["w0"] == 0):
                    act.wait_ge(block_used, g["w0"] + k - 1 + 2 * i)
                for t in range(2):
                    act.wait_ge(loaded[k][t], 16 * ((MOD_BLOCKS + g["w0"]) // 2 + 1) + 16 * i)
                    copy(WH[:, k, t, 0:g["kc"], :], W32[:, k, t, 0:g["kc"], :]).then_inc(hi_ready, 1)

            def begin(g):
                for k in range(2):
                    split(g, 0, k, True)

            def act_gemm(g):
                n, T, u0 = g["blocks"] // 2, g["T"], g["u0"]

                def silu(i, k):
                    act.wait_ge(block_used, g["w0"] + k + 1 + 2 * i)
                    act.wait_ge(units_drained, u0 + k - 1 + 2 * i)
                    act.activation(ffn_s[:, k, 0:T], PS[:, 2 * k, 0:T], ACT.Silu).then_inc(silu_done, 1)

                def hidden(i, k):
                    act.wait_ge(units_drained, u0 + k + 1 + 2 * i)
                    copy(GH[:, bass.ds(2 * i + k, 1), 0:T], ffn_g[:, k:k + 1, 0:T]).then_inc(gh_done, 1)

                is_ffn = g["kind"] == "ffn"
                if n > 1:
                    with act.Fori(1, n) as i:
                        for k in range(2):
                            if is_ffn:
                                silu(i - 1, k)
                            split(g, i, k)
                            if is_ffn:
                                hidden(i - 1, k)
                if is_ffn:
                    for k in range(2):
                        silu(n - 1, k)
                        hidden(n - 1, k)

            def act_norm(n):
                N = NORMS[n]
                T = N["T"]
                for c in range(DC):
                    act.wait_ge(*N["wait"](c))
                    act.activation(N["sq"][:, c, 0:T], N["src"][:, c, 0:T], ACT.Square).then_inc(sq_ready, 1)
                act.wait_ge(inv_ready, n + 1)
                act.activation(rstd[:, 0:T], var[:, 0:T], ACT.Sqrt).then_inc(rstd_ready, 1)
                if N["h"] is not None:
                    for c in range(DC):
                        act.wait_ge(h_ready, DC * n + c + 1)
                        copy(N["h"][:, c, 0:T], N["sq"][:, c, 0:T]).then_inc(xh_ready, 1)

            def act_attend(span):
                lo, hi = span
                for u in range(lo, hi + 1):
                    if u < hi:
                        U = UNITS[u]
                        act.wait_ge(max_ready, u + 1)
                        if u - lo >= 2:
                            act.wait_ge(turned_ready, u - 1)
                        act.activation(probs[:, u % 2, 0:U["nk"]], PS[:, 4 + u % 2, 0:U["nk"]], ACT.Exp, bias=stats[:, 0, u:u + 1],
                                       accum_out=stats[:, 1, u:u + 1]).then_inc(probs_ready, 1)
                    if u - 1 >= lo:
                        v, nk = u - 1, UNITS[u - 1]["nk"]
                        act.wait_ge(turned_ready, v + 1)
                        if v - lo >= 2:
                            act.wait_ge(out_ready, v - 1)
                        copy(probsT[:, v % 2, 0:nk], PS[:, 2 + v % 2, 0:nk]).then_inc(turned_copied, 1)

            def act_turn_out(n, T, base, gain=None):
                for c in range(n):
                    act.wait_ge(ot_turned, base + c + 1)
                    copy(XH[:, c, 0:T], PS[:, 4 + c % 2, 0:T], gain(c) if gain else 1.0).then_inc(ot_hi, 1)

            act.dma_start(mats[:, :, :], io["k_mats"]).then_inc(mats_loaded, 16)
            act.wait_ge(rows_clear, 1)
            for name, index, at, n in ROWS:
                src = flat(io[name] if index is None else io[name][index]).rearrange("(r p) -> r p", p=P)
                act.dma_start(prow[at % P:at % P + n, at // P, :], src).then_inc(rows_loaded, 16)
            for name, at, n in SHORT:
                for m in range(n):
                    act.dma_start(prow[at % P:at % P + 1, at // P, 64 * m:64 * m + 64], io[name]).then_inc(rows_loaded, 16)
            for n, name in enumerate(("ret_logit_f", "ret_logit_b")):
                src = bass.AP(tensor=io[name].tensor, offset=0, ap=[[0, P], [1, RET_HEADS]])
                act.dma_start(lg[:, RET_HEADS * n:RET_HEADS * n + RET_HEADS], src).then_inc(lg_loaded, 16)
            act.dma_start(fw[0:17, 0:64], io["hy_fw1"][0]).then_inc(filt_loaded, 16)
            act.dma_start(fw[:, 64:128], io["hy_fw2"][0]).then_inc(filt_loaded, 16)
            act.dma_start(fw[:, 128:192], io["hy_fw3"][0]).then_inc(filt_loaded, 16)
            act.dma_start(fw[:, 192:192 + D], io["hy_fw4"][0]).then_inc(filt_loaded, 16)
            act.dma_start(embT[:, :], io["k_emb"]).then_inc(filt_loaded, 16)
            act.dma_start(h_window, io["k_window"]).then_inc(filt_loaded, 16)
            act.dma_start(dft, io["k_fwd"].rearrange("p m t f -> p (m t) f")).then_inc(filt_loaded, 16)
            act.dma_start(idft, io["k_inv"].rearrange("p m t f -> p (m t) f")).then_inc(filt_loaded, 16)
            act.dma_start(relb[:, :], io["rel_bias_2"]).then_inc(rel_loaded, 16)
            act.dma_start(onehot[0:REL_BUCKETS, :], io["k_onehot"]).then_inc(rel_loaded, 16)
            act.dma_start(rel_mask[0:N_HEADS_2, :], io["k_rel_mask"]).then_inc(rel_loaded, 16)

            act.wait_ge(pcol_ready, 1)
            for s, name in enumerate(("c", "c_ctx")):
                at = COL[(name, None)]
                act.activation(silu_c[:, :, s], pcol[:, at:at + DC], ACT.Silu).then_inc(silu_c_ready, 1)
            for c in range(DC):
                act.wait_ge(x_turned, c + 1)
                copy(X[:, c, :], PS[:, 4 + c % 4, :]).then_inc(x_ready, 1)
            act.wait_ge(lg_abs, 1)
            act.activation(lgt[:, 1, :], lgt[:, 0, :], ACT.Exp, scale=-1.0).then_inc(lg_exp, 1)
            act.wait_ge(lg_u, 1)
            act.activation(lgt[:, 3, :], lgt[:, 2, :], ACT.Ln).then_inc(lg_ln, 1)
            for n in range(3):
                act.wait_ge(filt_arg, n + 1)
                act.activation(h_act[0:64, n % 2, :], h_tmp[0:64, 2, :], ACT.Sin).then_inc(filt_sin, 1)
            for n in range(5):
                act.wait_ge(filt_k, n + 1)
                copy(filt[:, n, :], PS[:, 4 + n % 4, :]).then_inc(filt_ready, 1)
            act.wait_ge(rel_vec, 1)
            act.dma_start(rel_dram, relvec[:, :]).then_inc(rel_stored, 16)

            order = iter(GEMMS[1:] + [None])

            def run(name):
                g = next(x for x in GEMMS if x["name"] == name)
                act_gemm(g)
                after = next(order)
                if after is not None:
                    begin(after)

            begin(GEMMS[0])
            act_norm(0)
            run("ffn_0a_in")
            run("ffn_0a_out")
            act_norm(1)
            run("even_qk")
            run("even_v")
            run("even_u")
            for t in range(9):
                if t < 8:
                    if t >= 2:
                        act.wait_ge(qk_ms, t - 1)
                    act.wait_ge(units_drained, G["qk1"]["u0"] + t // 2 + 1)
                    act.activation(area(23040 + 512 * (t % 2), BOTH), qk1[:, t, :], ACT.Square).then_inc(qk_sq, 1)
                if t >= 1:
                    act.wait_ge(qk_inv, t)
                    if t >= 3:
                        act.wait_ge(qk_ready, t - 2)
                    act.activation(area(24064 + 512 * ((t - 1) % 2), BOTH), area(25088 + 512 * ((t - 1) % 2), BOTH),
                                   ACT.Sqrt).then_inc(qk_rstd, 1)
            act.wait_ge(qk_ready, 8)
            act_attend(NA)
            act.wait_ge(out_done, NA[1])
            for n in range(12):
                tile = n if n < 4 else (4 + (n - 4) // 2 if n % 2 == 0 else 8 + (n - 4) // 2)
                if n < 4:
                    dst = hy_x0[:, n, :]
                else:
                    c = (n - 4) // 2
                    if c >= 2 and n % 2 == 0:
                        act.wait_ge(z_ready, c - 1)
                    dst = hy_xv[:, 2 * (c % 2) + n % 2, :]
                act.wait_ge(units_drained, drained(G["u1"]))
                act.activation(dst, u1[:, tile, :], ACT.Identity, scale=col("hy_conv_w", 12 + tile),
                               bias=col("hy_conv_b", tile)).then_inc(conv_mid, 1)
            act_turn_out(4, BOTH, 0)
            for t in range(4):
                act.wait_ge(zt_turned, t + 1)
                copy(hy_zt[:, t, :], PS[:, (6, 7, 2, 3)[t], :]).then_inc(zt_copied, 1)
            for s in range(2):
                if s:
                    act.wait_ge(y_re, 2)
                    act.wait_ge(y_im, 2)
                for n in range(4):
                    act.wait_ge(spec_mm, 4 * s + n + 1)
                    copy(hy_spec[:, n, :], PS[:, 4 + n, :]).then_inc(spec_copied, 1)
            for c in range(4):
                act.wait_ge(hy_out, c + 1)
                copy(XH[:, 4 + c, :], hy_z[:, c, :]).then_inc(hy_hi, 1)
            run("even_out")
            act_norm(2)
            run("ffn_0b_in")
            act.wait_ge(ret_loaded, 32)
            act.wait_ge(lg_ready, 1)
            for h in range(RET_HEADS):
                if h:
                    act.wait_ge(dec_ready, h)
                for n, (d, m) in enumerate(((h, 0), (RET_HEADS + h, 0), (h, 3), (RET_HEADS + h, 4))):
                    act.activation(ret_e[:, n, :], ret_k[:, m, :], ACT.Exp, scale=lg[:, d:d + 1]).then_inc(dec_exp, 1)
            run("ffn_0b_out")
            act_norm(3)
            run("ffn_1a_in")
            run("ffn_1a_out")
            act_norm(4)
            run("ret_q")
            run("ret_k")
            run("ret_v")
            run("ret_g")
            act.wait_ge(units_drained, drained(G["gr"]))
            for h in range(RET_HEADS):
                act.activation(gr[:, 4 * h:4 * h + 4, :], gr[:, 4 * h:4 * h + 4, :], ACT.Silu).then_inc(rg_ready, 1)
            act.wait_ge(rope_ready, 16)
            act.wait_ge(dec_ready, RET_HEADS)
            for h in range(RET_HEADS):
                y = 4 * (h % 2)
                if h >= 2:
                    act.wait_ge(zl_ready, 4 * (h - 1))
                for e in range(4):
                    act.wait_ge(ry_ready, 4 * h + 2 * (e // 2) + 2)
                    copy(ret_y[:, y + e, :], PS[:, 6 + e // 2, SEQ * (e % 2):SEQ * (e % 2) + SEQ]).then_inc(ryc_ready, 1)
                if h:
                    act.wait_ge(rv_ready, h)
                for e in range(4):
                    act.wait_ge(rc_ready, 4 * h + e + 1)
                    act.activation(ret_sq[:, e, :], ret_y[:, y + e, :], ACT.Square).then_inc(rq_ready, 1)
                act.wait_ge(ri_ready, h + 1)
                act.activation(rstd[:, 0:SEQ], var[:, 0:SEQ], ACT.Sqrt).then_inc(rr_ready, 1)
                for e in range(4):
                    act.wait_ge(rz_ready, 4 * h + e + 1)
                    copy(ZH[:, 4 * h + e, :], ret_y[:, y + e, :]).then_inc(zh_ready, 1)
            run("ret_out")
            act_norm(5)
            run("ffn_1b_in")
            run("ffn_1b_out")
            act_norm(6)
            run("ffn_2a_in")
            run("ffn_2a_out")
            act_norm(7)
            run("mix_q")
            run("mix_k")
            run("mix_v")
            act_attend(REL)
            act.wait_ge(out_done, REL[1])
            for t in range(2):
                for n, (a, b) in enumerate(((0, 768), (768, D))):
                    act.activation(O2n[:, t, a:b], O2[:, t, a:b], ACT.Square,
                                   accum_out=onorm[:, 2 * n + t:2 * n + t + 1]).then_inc(on_sq, 1)
            act.wait_ge(on_inv, 1)
            act.activation(onorm[:, 8:12], onorm[:, 4:8], ACT.Sqrt).then_inc(on_rstd, 1)
            act_turn_out(8, SEQ, 4, lambda c: col("g_out_a_2", c))
            run("mix_out")
            act_norm(8)
            run("cross_q")
            for c in range(DC):
                act.wait_ge(mem_turned, c + 1)
                copy(memX[:, c, :], PS[:, 6 + c % 2, 0:SEQ]).then_inc(mem_ready, 1)
            act_norm(9)
            run("cross_k")
            run("cross_v")
            act_attend(CROSS)
            act_turn_out(8, SEQ, 12)
            run("cross_out")
            act_norm(10)
            run("ffn_2b_in")
            run("ffn_2b_out")
            act_norm(11)
            for n in range(4):
                act.wait_ge(fin_turned, n + 1)
                copy(out_tok[:, n // 2, 512 * (n % 2):512 * (n % 2) + 512], PS[:, 4 + n, :]).then_inc(fin_copied, 1)
                if n % 2:
                    act.wait_ge(fin_copied, n + 1)
                    act.dma_start(out[0, P * (n // 2):P * (n // 2) + P, :], out_tok[:, n // 2, :]).then_inc(stored, 16)

        @block.vector
        def _(dve):
            links = [0]

            def link(ins):
                links[0] += 1
                ins.then_inc(dve_chain, 1)
                dve.wait_ge(dve_chain, links[0])

            tt, ts, stt = dve.tensor_tensor, dve.tensor_scalar, dve.scalar_tensor_tensor

            def inverse(dst, sums, n, done):
                link(ts(dst, sums, 1.0 / n, EPS, ALU.mult, ALU.add))
                dve.reciprocal(dst, dst).then_inc(done, 1)

            def split(g, i, k):
                for t in range(2):
                    dve.wait_ge(hi_ready, 2 * (g["w0"] + k) + t + 1 + 4 * i)
                    tt(WL[:, k, t, 0:g["kc"], :], W32[:, k, t, 0:g["kc"], :], WH[:, k, t, 0:g["kc"], :], ALU.subtract)\
                        .then_inc(lo_ready, 1)

            def begin(g):
                for k in range(2):
                    split(g, 0, k)

            def dve_gemm(g):
                n, T, u0, w0 = g["blocks"] // 2, g["T"], g["u0"], g["w0"]

                def product(i, k):
                    dve.wait_ge(silu_done, FC * g["ffn"] + k + 1 + 2 * i)
                    tt(ffn_g[:, k, 0:T], ffn_s[:, k, 0:T], PS[:, 2 * k + 1, 0:T], ALU.mult).then_inc(units_drained, 1)

                def rest(i, k):
                    dve.wait_ge(gh_done, FC * g["ffn"] + k + 1 + 2 * i)
                    j = bass.ds(2 * i + k, 1)
                    tt(GL[:, j, 0:T], ffn_g[:, k:k + 1, 0:T], GH[:, j, 0:T], ALU.subtract).then_inc(gl_done, 1)

                def store(i, k):
                    dve.wait_ge(block_used, w0 + k + 1 + 2 * i)
                    if g["tok"]:
                        src = PS[:, 2 * k:2 * k + 2, :].rearrange("p b (t n) -> p (b t) n", t=2)[:, 0:T // P, :]
                        dst = g["dest"][:, 0:T // P, bass.ds(512 * i + 256 * k, 256)]
                    else:
                        src, dst = PS[:, 2 * k:2 * k + 2, 0:T], g["dest"][:, bass.ds(4 * i + 2 * k, 2), 0:T]
                    ts(dst, src, g["scale"], None, ALU.mult).then_inc(units_drained, 1)

                def add(u):
                    dve.wait_ge(block_used, w0 + g["parts"] * (u + 1))
                    for t in range(2):
                        c = 2 * u + t
                        for s, tok in segs(T):
                            gate = g["gate"](c, s) if callable(g["gate"]) else g["gate"]
                            ins = stt(X[:, c, tok], PS[:, 2 * (u % 2) + t, tok], gate, X[:, c, tok], ALU.mult, ALU.add)
                    ins.then_inc(units_drained, 1)

                if g["kind"] == "ffn":
                    with dve.Fori(1, n) as i:
                        for k in range(2):
                            product(i - 1, k)
                            split(g, i, k)
                            rest(i - 1, k)
                    for k in range(2):
                        product(n - 1, k)
                        rest(n - 1, k)
                elif g["kind"] == "store":
                    if n > 1:
                        with dve.Fori(1, n) as i:
                            for k in range(2):
                                store(i - 1, k)
                                split(g, i, k)
                    for k in range(2):
                        store(n - 1, k)
                else:
                    u = 0
                    for b in range(2, g["blocks"]):
                        if g["parts"] == 1:
                            add(u)
                            u += 1
                        split(g, b // 2, b % 2)
                        if g["parts"] == 2 and b % 2:
                            add(u)
                            u += 1
                    while u < g["units"]:
                        add(u)
                        u += 1

            def dve_norm(n):
                N = NORMS[n]
                T, sq = N["T"], N["sq"]
                dve.wait_ge(ms_ready, n + 1)
                inverse(var[:, 0:T], PS[:, BANK_N, 0:T], D, inv_ready)
                for c in range(DC + 1):
                    if c < DC:
                        dve.wait_ge(t_ready, DC * n + c + 1)
                        for s, tok in segs(T):
                            if N["b"]:
                                ins = ts(sq[:, c, tok], sq[:, c, tok], N["a"](c, s), N["b"](c, s), ALU.mult, ALU.add)
                            else:
                                ins = ts(sq[:, c, tok], sq[:, c, tok], N["a"](c, s), None, ALU.mult)
                        ins.then_inc(h_ready, 1)
                    if c and N["h"] is not None:
                        dve.wait_ge(xh_ready, DC * n + c)
                        tt(N["l"][:, c - 1, 0:T], sq[:, c - 1, 0:T], N["h"][:, c - 1, 0:T], ALU.subtract).then_inc(xl_ready, 1)

            def dve_attend(span):
                lo, hi = span
                for u in range(lo, hi + 2):
                    if u < hi:
                        dve.wait_ge(scores_ready, u + 1)
                        dve.tensor_reduce(stats[:, 0, u:u + 1], PS[:, 4 + u % 2, 0:UNITS[u]["nk"]], AXX, ALU.max,
                                          negate=True).then_inc(max_ready, 1)
                    if lo <= u - 1 < hi:
                        v = u - 1
                        U = UNITS[v]
                        dve.wait_ge(probs_ready, v + 1)
                        if U["count"] is not None:
                            p = probs[:, v % 2, 0:U["nk"]]
                            dve.tensor_tensor_reduce(p, p, U["count"], 1.0, 0.0, ALU.mult, ALU.add,
                                                     stats[:, 1, v:v + 1]).then_inc(probs_counted, 1)
                            dve.wait_ge(probs_counted, counted[v])
                        dve.reciprocal(stats[:, 2, v:v + 1], stats[:, 1, v:v + 1]).then_inc(denoms, 1)
                    if u - 2 >= lo:
                        v = u - 2
                        dst = UNITS[v]["dst"]
                        dve.wait_ge(denoms, v + 1)
                        dve.wait_ge(out_ready, v + 1)
                        ts(dst, PS[:, 6 + v % 2, 0:dst.shape[-1]], stats[:, 2, v:v + 1], None, ALU.mult).then_inc(out_done, 1)

            def dve_turn_out(n, T, base, gain=None):
                for c in range(n):
                    dve.wait_ge(ot_hi, base + c + 1)
                    stt(XL[:, c, 0:T], PS[:, 4 + c % 2, 0:T], gain(c) if gain else 1.0, XH[:, c, 0:T],
                        ALU.mult, ALU.subtract).then_inc(ot_lo, 1)

            dve.memset(prow[:, :, :], 0.0).then_inc(rows_clear, 1)
            dve.wait_ge(rows_turned, 1)
            link(dve.tensor_copy(pcol[:, :], PS[:, 4, 0:3 * P]))
            q_gain = col("na_q_gain")
            ts(q_gain, q_gain, 0.125, None, ALU.mult).then_inc(pcol_ready, 1)
            dve.wait_ge(lg_loaded, 32)
            stt(lgt[:, 0, :], lg[:, :], -1.0, lg[:, :], ALU.mult, ALU.max).then_inc(lg_abs, 1)
            dve.wait_ge(lg_exp, 1)
            ts(lgt[:, 2, :], lgt[:, 1, :], 1.0, None, ALU.add).then_inc(lg_u, 1)
            dve.wait_ge(lg_u, 1)
            link(ts(lgt[:, 4, :], lgt[:, 2, :], -1.0, 1e-30, ALU.add, ALU.max))
            link(dve.reciprocal(lgt[:, 5, :], lgt[:, 4, :]))
            link(tt(lgt[:, 6, :], lgt[:, 5, :], lgt[:, 1, :], ALU.mult))
            dve.wait_ge(lg_ln, 1)
            link(tt(lgt[:, 6, :], lgt[:, 6, :], lgt[:, 3, :], ALU.mult))
            link(ts(lgt[:, 7, :], lg[:, :], 0.0, None, ALU.min))
            tt(lg[:, :], lgt[:, 7, :], lgt[:, 6, :], ALU.subtract).then_inc(lg_ready, 1)
            a, k_, r = (h_tmp[0:64, n, :] for n in range(3))
            MAGIC = 1.5 * 2.0 ** 23
            C1 = 6.28125
            C2 = float(np.float32(np.round((2 * math.pi - C1) * 2 ** 20) / 2 ** 20))
            C3 = 2 * math.pi - C1 - C2
            PI = 3.1415925
            for n in range(3):
                dve.wait_ge(filt_mm, n + 1)
                if n:
                    dve.wait_ge(filt_sin, n)
                link(ts(a, PS[0:64, 4, 0:SEQ], col(f"hy_fb{n + 1}", 0, 64), col("hy_freq", 0, 64), ALU.add, ALU.mult))
                link(ts(k_, a, 1.0 / (2 * math.pi), MAGIC, ALU.mult, ALU.add))
                link(ts(k_, k_, -MAGIC, None, ALU.add))
                link(stt(r, k_, -C1, a, ALU.mult, ALU.add))
                link(stt(r, k_, -C2, r, ALU.mult, ALU.add))
                link(stt(r, k_, -C3, r, ALU.mult, ALU.add))
                ts(r, r, PI, -PI, ALU.min, ALU.max).then_inc(filt_arg, 1)
            dve.wait_ge(filt_mm, 3 + 4)
            dve.wait_ge(x_ready, DC)
            for t in range(2):
                link(tt(h_sum[:, t, :], PS[:, 4 + 2 * t, :], h_window[:, t, :], ALU.mult))
                link(tt(hy_taps[:, t, :], PS[:, 5 + 2 * t, :], h_window[:, t, :], ALU.mult))
                tt(h_dif[:, t, :], h_sum[:, t, :], hy_taps[:, t, :], ALU.subtract).then_inc(filt_sd, 1)
                tt(h_sum[:, t, :], h_sum[:, t, :], hy_taps[:, t, :], ALU.add).then_inc(filt_sd, 1)
            dve.wait_ge(rel_mm, 1)
            tt(relvec[:, :], PS[0:N_HEADS_2, 5, :], rel_mask[0:N_HEADS_2, :], ALU.add).then_inc(rel_vec, 1)
            with dve.Fori(0, MOD_BLOCKS // 2) as i:
                for k in range(2):
                    dve.wait_ge(mod_used, 2 * i + k + 1)
                    dve.tensor_copy(modT[:, bass.ds(4 * i + 2 * k, 2), :],
                                    PS[:, 2 * k, 0:4].rearrange("p (t s) -> p t s", t=2)).then_inc(units_drained, 1)
            begin(GEMMS[0])
            dve.wait_ge(units_drained, MOD_BLOCKS)
            per = N_MOD * DC
            for layer in range(2):
                at = COL[("b_mod", layer)]
                for s in range(2):
                    m = modT[:, per * layer:per * layer + per, s]
                    ins = tt(m, m, pcol[:, at:at + per], ALU.add)
            link(ins)
            for layer in range(2):
                for m in (2, 8):
                    gm = modT[:, per * layer + DC * m:per * layer + DC * m + DC, :]
                    ts(gm, gm, 0.5, None, ALU.mult)
                for j in range(3):
                    at = COL[("norm_gain", None)] + (3 * layer + j) * DC
                    for s in range(2):
                        sc = per * layer + DC * (3 * j + 1)
                        ins = stt(norm_a[:, 3 * layer + j, :, s], modT[:, sc:sc + DC, s], 1.0, pcol[:, at:at + DC], ALU.add, ALU.mult)
            link(ins)

            order = iter(GEMMS[1:] + [None])

            def run(name):
                g = next(x for x in GEMMS if x["name"] == name)
                dve_gemm(g)
                after = next(order)
                if after is not None:
                    begin(after)

            dve_norm(0)
            run("ffn_0a_in")
            run("ffn_0a_out")
            dve_norm(1)
            run("even_qk")
            run("even_v")
            run("even_u")
            for t in range(9):
                if t < 8:
                    dve.wait_ge(qk_ms, t + 1)
                    inverse(area(25088 + 512 * (t % 2), BOTH), PS[:, 4 + t % 2, :], 64, qk_inv)
                if t >= 1:
                    dve.wait_ge(qk_rstd, t)
                    gain = col("na_q_gain" if t - 1 < 4 else "na_k_gain")
                    stt(qk1[:, t - 1, :], qk1[:, t - 1, :], gain, area(24064 + 512 * ((t - 1) % 2), BOTH),
                        ALU.mult, ALU.mult).then_inc(qk_ready, 1)
            dve_attend(NA)
            for n in range(12):
                tile = n if n < 4 else (4 + (n - 4) // 2 if n % 2 == 0 else 8 + (n - 4) // 2)
                dst = hy_x0[:, n, :] if n < 4 else hy_xv[:, 2 * (((n - 4) // 2) % 2) + n % 2, :]
                dst, src = (a.rearrange("p (s t) -> p s t", s=2) for a in (dst, u1[:, tile, :]))
                dve.wait_ge(conv_mid, n + 1)
                link(stt(dst[:, :, 1:], src[:, :, :SEQ - 1], col("hy_conv_w", tile), dst[:, :, 1:], ALU.mult, ALU.add))
                stt(dst[:, :, :SEQ - 1], src[:, :, 1:], col("hy_conv_w", 24 + tile), dst[:, :, :SEQ - 1],
                    ALU.mult, ALU.add).then_inc(conv_ready, 1)
            dve_turn_out(4, BOTH, 0)
            for s in range(2):
                dve.wait_ge(spec_copied, 4 * s + 4)
                for f in range(2):
                    y, t = hy_y[:, 4 * s + f, :], hy_xv[:, f, :]
                    tt(y, hy_spec[:, f, :], filt[:, f, :], ALU.mult)
                    link(tt(t, hy_spec[:, 2 + f, :], filt[:, 3 + f, :], ALU.mult))
                    tt(y, y, t, ALU.subtract).then_inc(y_re, 1)
            for c in range(5):
                if c < 4:
                    dve.wait_ge(inv_mm, c + 1)
                    link(stt(hy_xv[:, c % 2, :], hy_z[:, c, :], col("hy_bias", c), PS[:, 2 + c % 2, :], ALU.mult, ALU.add))
                    tt(hy_z[:, c, :], hy_xv[:, c % 2, :], hy_x0[:, c, :], ALU.mult).then_inc(hy_out, 1)
                if c >= 1:
                    dve.wait_ge(hy_hi, c)
                    tt(XL[:, 3 + c, :], hy_z[:, c - 1, :], XH[:, 3 + c, :], ALU.subtract).then_inc(hy_lo, 1)
            run("even_out")
            dve_norm(2)
            run("ffn_0b_in")
            run("ffn_0b_out")
            dve_norm(3)
            run("ffn_1a_in")
            run("ffn_1a_out")
            dve_norm(4)
            run("ret_q")
            run("ret_k")
            run("ret_v")
            run("ret_g")
            for t in range(16):
                x = qr[:, t, :] if t < 8 else kr[:, t - 8, 0:SEQ]
                dve.wait_ge(rope_mm, t + 1)
                link(tt(rope_t[:, 2 + t % 2, :], PS[:, 4 + t % 2, 0:SEQ], rope[:, 2 * (t % 2) + 1, :], ALU.mult))
                dve.wait_ge(rope_cos, t + 1)
                tt(x, rope_t[:, t % 2, :], rope_t[:, 2 + t % 2, :], ALU.add).then_inc(rope_ready, 1)
            dve.wait_ge(dec_ready, RET_HEADS)
            for h in range(RET_HEADS):
                y = 4 * (h % 2)
                for t in range(4):
                    dve.wait_ge(rs_ready, 4 * h + t + 1)
                    stt(ret_p[:, y + t, :], PS[:, 4 + t % 2, 0:SEQ], 0.0625, decay[:, 4 * h + t, :], ALU.mult, ALU.mult)\
                        .then_inc(rp_ready, 1)
                dve.wait_ge(rm_ready, h + 1)
                for e in range(4):
                    stt(ret_y[:, y + e, :], PS[:, 2, 0:SEQ], -1.0 / 512, ret_y[:, y + e, :], ALU.mult, ALU.add)\
                        .then_inc(rc_ready, 1)
                dve.wait_ge(rv_ready, h + 1)
                inverse(var[:, 0:SEQ], PS[:, 3, 0:SEQ], 512, ri_ready)
                dve.wait_ge(rg_ready, h + 1)
                for e in range(5):
                    if e < 4:
                        dve.wait_ge(rn_ready, 4 * h + e + 1)
                        tt(ret_y[:, y + e, :], ret_y[:, y + e, :], gr[:, 4 * h + e, :], ALU.mult).then_inc(rz_ready, 1)
                    if e >= 1:
                        dve.wait_ge(zh_ready, 4 * h + e)
                        tt(ZL[:, 4 * h + e - 1, :], ret_y[:, y + e - 1, :], ZH[:, 4 * h + e - 1, :], ALU.subtract)\
                            .then_inc(zl_ready, 1)
            run("ret_out")
            dve_norm(5)
            run("ffn_1b_in")
            run("ffn_1b_out")
            dve_norm(6)
            run("ffn_2a_in")
            run("ffn_2a_out")
            dve_norm(7)
            run("mix_q")
            run("mix_k")
            run("mix_v")
            dve.wait_ge(cnt_loaded, 16)
            dve_attend(REL)
            dve.wait_ge(on_sq, 4)
            for n, width in enumerate((768, 256)):
                ins = ts(onorm[:, 4 + 2 * n:6 + 2 * n], onorm[:, 2 * n:2 * n + 2], 1.0 / width, EPS, ALU.mult, ALU.add)
            link(ins)
            dve.reciprocal(onorm[:, 4:8], onorm[:, 4:8]).then_inc(on_inv, 1)
            dve.wait_ge(on_rstd, 1)
            for t in range(2):
                for n, (a, b) in enumerate(((0, 768), (768, D))):
                    ts(O2n[:, t, a:b], O2[:, t, a:b], onorm[:, 8 + 2 * n + t:9 + 2 * n + t], None, ALU.mult).then_inc(on_ready, 1)
            dve_turn_out(8, SEQ, 4, lambda c: col("g_out_a_2", c))
            run("mix_out")
            dve_norm(8)
            run("cross_q")
            dve_norm(9)
            run("cross_k")
            run("cross_v")
            dve_attend(CROSS)
            dve_turn_out(8, SEQ, 12)
            run("cross_out")
            dve_norm(10)
            run("ffn_2b_in")
            run("ffn_2b_out")
            dve_norm(11)

        @block.gpsimd
        def _(pool):
            tt = pool.tensor_tensor

            def pool_norm(n):
                T = NORMS[n]["T"]
                pool.wait_ge(rstd_ready, n + 1)
                for c in range(DC):
                    tt(NORMS[n]["sq"][:, c, 0:T], NORMS[n]["src"][:, c, 0:T], rstd[:, 0:T], ALU.mult).then_inc(t_ready, 1)

            pool.dma_start(na_mask, io["k_na_mask"]).then_inc(nab_loaded, 16)
            width, rows = 2 * WIN_C - 1, 15
            for h in range(NA_HEADS):
                for r in range(4):
                    src = bass.AP(tensor=io["na_rpb"].tensor, offset=(h * rows + 7 - r) * width + WIN_C - GRID_W,
                                  ap=[[1, GRID_W], [width, 4], [1, GRID_W]])
                    at = GRID_W * (1 - r % 2)
                    dst = na_bias[at:at + GRID_W, 2 * h + r // 2, :].rearrange("p (a b) -> p a b", a=4)
                    pool.dma_start(dst, src).then_inc(nab_loaded, 16)
            pool.wait_ge(nab_loaded, 16 * 33)
            for n in range(16):
                tt(na_bias[:, n, :], na_bias[:, n, :], na_mask[:, 0, :], ALU.mult).then_inc(pool_chain, 1)
            for n in range(16):
                pool.wait_ge(pool_chain, n + 1)
                tt(na_bias[:, n, :], na_bias[:, n, :], na_mask[:, 1, :], ALU.add).then_inc(nab_ready, 1)
            pool_norm(0)
            pool_norm(1)
            for c in range(4):
                pool.wait_ge(conv_ready, 4 + 2 * c + 2)
                tt(hy_z[:, c, :], hy_xv[:, 2 * (c % 2), :], hy_xv[:, 2 * (c % 2) + 1, :], ALU.mult).then_inc(z_ready, 1)
            for s in range(2):
                pool.wait_ge(spec_copied, 4 * s + 4)
                for f in range(2):
                    y, t = hy_y[:, 4 * s + 2 + f, :], hy_xv[:, 2 + f, :]
                    tt(y, hy_spec[:, f, :], filt[:, 3 + f, :], ALU.mult).then_inc(pool_chain, 1)
                    tt(t, hy_spec[:, 2 + f, :], filt[:, 2 if f == 0 else 1, :], ALU.mult).then_inc(pool_chain, 1)
                    pool.wait_ge(pool_chain, 16 + 2 * (2 * s + f + 1))
                    tt(y, y, t, ALU.add).then_inc(y_im, 1)
            pool.wait_ge(hy_lo, 4)
            pool.dma_start(ret_k, io["k_ret"].rearrange("p m t q -> p m (t q)")).then_inc(ret_loaded, 16)
            pool.dma_start(rope, io["k_rope"].rearrange("p a b t -> p (a b) t")).then_inc(ret_loaded, 16)
            pool_norm(2)
            for h in range(RET_HEADS):
                pool.wait_ge(dec_exp, 4 * h + 4)
                lat, cx = (decay[:, 4 * h + 2 * n:4 * h + 2 * n + 2, :].rearrange("p a b -> p (a b)") for n in range(2))
                tt(ret_e[:, 0, :], ret_e[:, 0, :], ret_k[:, 1, :], ALU.mult).then_inc(dec_used, 1)
                tt(ret_e[:, 1, :], ret_e[:, 1, :], ret_k[:, 2, :], ALU.mult).then_inc(dec_used, 1)
                tt(cx, ret_e[:, 2, :], ret_e[:, 3, :], ALU.add).then_inc(dec_used, 1)
                pool.wait_ge(dec_used, 3 * h + 3)
                tt(lat, ret_e[:, 0, :], ret_e[:, 1, :], ALU.add).then_inc(dec_ready, 1)
            pool_norm(3)
            pool_norm(4)
            for t in range(16):
                x = qr[:, t, :] if t < 8 else kr[:, t - 8, 0:SEQ]
                pool.wait_ge(units_drained, drained(G["qr"] if t < 8 else G["kr"]))
                if t >= 2:
                    pool.wait_ge(rope_ready, t - 1)
                tt(rope_t[:, t % 2, :], x, rope[:, 2 * (t % 2), :], ALU.mult).then_inc(rope_cos, 1)
            for h in range(RET_HEADS):
                pool.wait_ge(rr_ready, h + 1)
                for e in range(4):
                    y = ret_y[:, 4 * (h % 2) + e, :]
                    tt(y, y, rstd[:, 0:SEQ], ALU.mult).then_inc(rn_ready, 1)
            pool.wait_ge(zl_ready, 16)
            pool.wait_ge(rel_stored, 16)
            for t in range(2):
                src = bass.AP(tensor=rel_dram.tensor, offset=P - P * t, ap=[[1, P], [BOTH, N_HEADS_2], [1, P * (t + 1)]])
                pool.dma_start(rel_bias[:, :, P * t:P * t + P * (t + 1)], src).then_inc(rel_back, 16)
            pool.dma_start(rel_count, io["k_rel_count"]).then_inc(cnt_loaded, 16)
            pool.dma_start(mem_tok, io["mem_2"][0].rearrange("(t p) d -> p t d", p=P)).then_inc(mem_loaded, 16)
            for n in range(5, 12):
                pool_norm(n)


def kernel(**inputs):
    import concourse.bacc as bacc
    from concourse.bass_utils import run_bass_kernel_spmd

    nc = bacc.Bacc("TRN2", target_bir_lowering=False, num_devices=1)
    arrays, io = {}, {}
    for name, a in {**inputs, **shape_constants()}.items():
        a = np.ascontiguousarray(a)
        arrays[f"in_{name}"] = a
        io[name] = nc.dram_tensor(f"in_{name}", a.shape, mybir.dt.from_np(a.dtype), kind="ExternalInput").ap()
    out = nc.dram_tensor("out", (1, SEQ, D), F32, kind="ExternalOutput").ap()
    program(nc, io, out)
    r = run_bass_kernel_spmd(nc, [arrays], core_ids=[0])
    return r.results[0]["out"]
```

```python
import math
from contextlib import ExitStack

import numpy as np

import concourse.bass as bass
from concourse import mybir

ACT = mybir.ActivationFunctionType
ALU = mybir.AluOpType
AXX = mybir.AxisListType.X
F32 = mybir.dt.float32
F16 = mybir.dt.float16
BF16 = mybir.dt.bfloat16

P = 128
D = 1024
DC = D // P
SEQ = 256
BOTH = 2 * SEQ
FF = 2816
FC = FF // P
N_MOD = 9
NEG = -1.0e30
EPS = 1e-6
GRID_W = 64
WIN_C = 16
NA_HEADS = 8
HY_W = 512
REL_BUCKETS = 32
N_HEADS_2 = 16
N_HEADS_A = 12
RET_HEADS = 4
KC_MAX = FC // 2
W_SCALE = 64.0


def shape_constants():
    f = np.float32
    eye = np.eye(P, dtype=f)
    block_ones = np.kron(np.eye(2, dtype=f), np.ones((64, 64), f))
    rot = np.zeros((P, P), f)
    for i in range(64):
        rot[64 + i, i] = -1.0
        rot[i, 64 + i] = 1.0
    mats = np.stack([eye, np.ones((P, P), f), block_ones, rot, eye[::-1]], 1)

    n = 2 * SEQ
    t = np.arange(SEQ)
    ang = 2.0 * np.pi * ((t[:, None] * t[None, :]) % n) / n
    cos, sin = np.cos(ang), np.sin(ang)
    nyq = (-1.0) ** t
    cos_n, sin_n = cos.copy(), sin.copy()
    cos_n[:, 0] = nyq
    sin_n[:, 0] = nyq
    fwd = np.stack([cos, cos_n, sin, sin_n], 0).reshape(4, 2, P, SEQ).transpose(2, 0, 1, 3)
    icos, isin = 2.0 * cos.T / n, 2.0 * sin.T / n
    icos[0] = 1.0 / n
    isin[0] = nyq / n
    inv = np.stack([icos, isin], 0).reshape(2, 2, P, SEQ).transpose(2, 0, 1, 3)

    pos = np.linspace(0.0, 1.0, SEQ, dtype=f)[:, None]
    w = f(2.0 * math.pi) * np.arange(SEQ, dtype=f)[:, None] / f(SEQ)
    bands = np.linspace(1e-4, 7, 8, dtype=f)
    emb = np.concatenate([pos, np.cos(bands * w), -np.sin(bands * w)], -1).astype(f)
    deltas = np.linspace(math.log(1e-2) / 1.5, math.log(1e-2) / 0.3, HY_W, dtype=f)
    window = np.exp(-pos * np.abs(deltas)).astype(f).reshape(2, P, HY_W).transpose(1, 0, 2)

    col = np.arange(GRID_W)
    start = np.clip(col - WIN_C // 2, 0, GRID_W - WIN_C)
    seen = (col[None] >= start[:, None]) & (col[None] < start[:, None] + WIN_C)
    seen = np.tile(seen, (2, SEQ // GRID_W))[::-1].astype(f)
    na_mask = np.stack([seen, (1.0 - seen) * f(NEG)], 1)

    dist = np.arange(SEQ - 1, -1, -1)
    large = 16 + (np.log(np.maximum(dist, 1).astype(f) / f(16)) / f(math.log(2048 / 16)) * f(16)).astype(np.int32)
    bucket = np.where(dist < 16, dist, np.minimum(large, REL_BUCKETS - 1))
    onehot = np.zeros((REL_BUCKETS, BOTH), f)
    onehot[bucket, np.arange(SEQ)] = 1.0
    count = (dist <= 128).astype(f) + (dist % 4 == 0) + (dist % 16 == 0)
    rel_mask = np.zeros((N_HEADS_2, BOTH), f)
    rel_mask[:, SEQ:] = NEG
    rel_mask[:N_HEADS_A, :SEQ][:, count == 0] = NEG
    per = np.concatenate([count, np.zeros(SEQ, f)])
    q, k = np.arange(SEQ)[:, None], np.arange(SEQ)[None]
    pair = per[np.minimum(SEQ - 1 - q + k, BOTH - 1)]
    rel_count = np.concatenate([pair[:P, :P], pair[P:, :]], 1)

    inv_f = f(10000.0) ** (-np.arange(64, dtype=f) / f(64))
    ang_r = (t // GRID_W).astype(f)[:, None] * inv_f
    ang_c = (t % GRID_W).astype(f)[:, None] * inv_f
    rope = np.stack([np.stack([np.tile(fn(a).T, (2, 1)) for fn in (np.cos, np.sin)], 0) for a in (ang_r, ang_c)], 0)
    rope = rope.transpose(2, 0, 1, 3)

    j, i = np.arange(SEQ)[:, None], np.arange(SEQ)[None]
    ret = np.stack([np.abs(i - j), i >= j, j >= i, i + SEQ - j, SEQ - i + j], 0)
    ret = ret.reshape(5, 2, P, SEQ).transpose(2, 0, 1, 3)
    return {n: np.ascontiguousarray(a, dtype=f) for n, a in dict(
        k_mats=mats, k_fwd=fwd, k_inv=inv, k_emb=emb.T, k_window=window, k_na_mask=na_mask,
        k_onehot=onehot, k_rel_mask=rel_mask, k_rel_count=rel_count, k_rope=rope, k_ret=ret).items()}


def program(nc, io, out):
    ctx = ExitStack()
    with ctx:
        def sb(name, shape, dt=F32):
            return ctx.enter_context(nc.sbuf_tensor(name, shape, dt))

        def sem(name):
            return ctx.enter_context(nc.semaphore(name))

        X = sb("X", [P, DC, BOTH])
        XH = sb("XH", [P, DC, BOTH], F16)
        XL = sb("XL", [P, DC, BOTH], F16)
        W32 = sb("W32", [P, 2, 2, KC_MAX, P])
        WH = sb("WH", [P, 2, 2, KC_MAX, P], F16)
        WL = sb("WL", [P, 2, 2, KC_MAX, P], F16)
        mats = sb("mats", [P, 5, P])
        prow = sb("prow", [P, 3, P])
        pcol = sb("pcol", [P, 3 * P])
        silu_c = sb("silu_c", [P, DC, 2])
        silu_s = sb("silu_s", [P, DC, 4], F16)
        modT = sb("modT", [P, 2 * N_MOD * DC, 2])
        norm_a = sb("norm_a", [P, 6, DC, 2])
        lg = sb("lg", [P, 2 * RET_HEADS])
        lgt = sb("lgt", [P, 8, 2 * RET_HEADS])
        rstd = sb("rstd", [P, BOTH])
        var = sb("var", [P, BOTH])
        stats = sb("stats", [P, 3, 80])
        onorm = sb("onorm", [P, 12])
        embT = sb("embT", [17, SEQ])
        relb = sb("relb", [REL_BUCKETS, N_HEADS_2])
        warm = sb("warm", [P, 2])
        relvec = sb("relvec", [N_HEADS_2, BOTH])
        arena = sb("arena", [P, 29184])
        PS = ctx.enter_context(nc.psum_tensor("PS", [P, 8, 512], F32))
        rel_dram = nc.dram_tensor("rel_scratch", (N_HEADS_2, BOTH), F32, kind="Internal").ap()

        def area(off, *shape, dt=F32):
            n = int(np.prod(shape)) // (2 if dt is F16 else 1)
            a = arena[:, off:off + n]
            if dt is not F32:
                a = a.bitcast(dt)
            if len(shape) == 2:
                return a.rearrange("p (a b) -> p a b", a=shape[0])
            if len(shape) == 3:
                return a.rearrange("p (a b c) -> p a b c", a=shape[0], b=shape[1])
            return a

        eye, ones, block_ones, rot, flip = (mats[:, n, :] for n in range(5))
        SQ, SQ_first, SQ_mid = area(23040, DC, BOTH), area(0, DC, BOTH), area(13312, DC, BOTH)
        GH, GL = area(0, FC, BOTH, dt=F16), area(FC * SEQ, FC, BOTH, dt=F16)
        ffn_s, ffn_g = area(2 * FC * SEQ, 2, BOTH), area(2 * FC * SEQ + 1024, 2, BOTH)
        M32 = [area(19968 + 2048 * k, 2, DC, P) for k in range(2)]
        MWH = [area(24064 + 2048 * k, 2, DC, P, dt=F16) for k in range(2)]
        MWL = [area(25088 + 2048 * k, 2, DC, P, dt=F16) for k in range(2)]
        dft_setup = area(0, 8, SEQ)
        x_tok = area(0, 4, D)
        h_window, h_sum, h_dif = area(4096, 2, HY_W), area(5120, 2, HY_W), area(6144, 2, HY_W)
        h_tmp, h_act = area(7168, 4, SEQ), area(8192, 2, SEQ)
        hy_taps = area(10240, 2, HY_W)
        fw = area(11264, 3 * 64 + D)[0:64]
        onehot, rel_mask = area(8704, BOTH), area(9216, BOTH)
        qk1, u1, V1 = area(0, 8, BOTH), area(4096, 12, BOTH), area(10240, 4, HY_W)
        filt, na_bias = area(13312, 5, HY_W), area(15872, 16, SEQ)
        dft, idft = area(19968, 8, SEQ), area(22016, 4, SEQ)
        na_mask = area(28160, 2, SEQ)
        probs, probsT = area(23040, 2, BOTH), area(24064, 2, BOTH)
        O1 = area(25088, 4, HY_W)
        hy_x0, hy_z, hy_zt = area(0, 4, BOTH), area(2048, 4, BOTH), area(10240, 4, HY_W)
        hy_xv, hy_spec, hy_y = area(27136, 4, BOTH), area(23040, 4, HY_W), area(4096, 8, HY_W)
        qr, kr, gr, Vr = area(0, 8, SEQ), area(2048, 8, BOTH), area(6144, 16, SEQ), area(10240, 4, 2 * D)
        decay, ret_k, rope = area(18432, 16, SEQ), area(22528, 5, BOTH), area(25088, 4, SEQ)
        ret_p, rope_t, ret_e = area(26112, 8, SEQ), area(28160, 4, SEQ), area(26112, 4, BOTH)
        ret_y, ret_sq = area(22528, 8, SEQ), area(25088, 4, SEQ)
        qk2, V2, rel_bias = area(0, 16, SEQ), area(4096, 2, D), area(13312, 16, 384)
        rel_count, mem_tok = area(19456, 384), area(19840, 2, D)
        qkc, Vc, memX = area(0, 16, SEQ), area(4096, 2, D), area(6144, DC, SEQ)
        MH, ML = area(8192, DC, SEQ, dt=F16), area(9216, DC, SEQ, dt=F16)
        SQM = area(10240, DC, SEQ)
        O2, O2n = area(25088, 2, D), area(27136, 2, D)
        out_tok = area(19840, 2, D)
        ZH, ZL = (a[:, :, :].rearrange("p c (h t) -> p (c h) t", h=2) for a in (XH, XL))

        loaded = [[sem(f"loaded_{k}{t}") for t in range(2)] for k in range(2)]
        mod_loaded = [[sem(f"mod_loaded_{k}{t}") for t in range(2)] for k in range(2)]
        mod_hi, mod_lo = sem("mod_hi"), sem("mod_lo")
        mod_used, mod_drained = sem("mod_used"), sem("mod_drained")
        hi_ready = sem("hi_ready")
        lo_ready = sem("lo_ready")
        block_used = sem("block_used")
        units_drained = sem("units_drained")
        silu_done, gh_done, gl_done = sem("silu_done"), sem("gh_done"), sem("gl_done")
        sq_ready, ms_ready, inv_ready, rstd_ready = sem("sq_ready"), sem("ms_ready"), sem("inv_ready"), sem("rstd_ready")
        t_ready, h_ready, xh_ready, xl_ready = sem("t_ready"), sem("h_ready"), sem("xh_ready"), sem("xl_ready")
        dve_chain, act_chain, pool_chain = sem("dve_chain"), sem("act_chain"), sem("pool_chain")
        mats_loaded, rows_clear, rows_loaded, x_loaded = sem("mats_loaded"), sem("rows_clear"), sem("rows_loaded"), sem("x_loaded")
        rows_turned, pcol_ready, x_turned, x_ready = sem("rows_turned"), sem("pcol_ready"), sem("x_turned"), sem("x_ready")
        silu_c_ready, silu_hi, silu_s_ready = sem("silu_c_ready"), sem("silu_hi"), sem("silu_s_ready")
        dft_loaded, dft_back = sem("dft_loaded"), sem("dft_back")
        lg_loaded, lg_abs, lg_exp, lg_u, lg_ln, lg_ready = (sem(n) for n in ("lg_loaded", "lg_abs", "lg_exp", "lg_u", "lg_ln", "lg_ready"))
        filt_loaded, filt_mm, filt_arg, filt_sin, filt_win, filt_sd, filt_k, filt_ready = (
            sem(n) for n in ("filt_loaded", "filt_mm", "filt_arg", "filt_sin", "filt_win", "filt_sd", "filt_k", "filt_ready"))
        rel_loaded, rel_mm, rel_vec, rel_stored, rel_back = (sem(n) for n in ("rel_loaded", "rel_mm", "rel_vec", "rel_stored", "rel_back"))
        nab_loaded, nab_ready = sem("nab_loaded"), sem("nab_ready")
        qk_sq, qk_ms, qk_inv, qk_rstd, qk_ready = (sem(n) for n in ("qk_sq", "qk_ms", "qk_inv", "qk_rstd", "qk_ready"))
        scores_ready, max_ready, probs_ready, probs_counted = (sem(n) for n in ("scores_ready", "max_ready", "probs_ready", "probs_counted"))
        turned_ready, turned_copied, out_ready, out_done, denoms = (
            sem(n) for n in ("turned_ready", "turned_copied", "out_ready", "out_done", "denoms"))
        ot_turned, ot_hi, ot_lo = sem("ot_turned"), sem("ot_hi"), sem("ot_lo")
        conv_mid, conv_ready, z_ready = sem("conv_mid"), sem("conv_ready"), sem("z_ready")
        zt_turned, zt_copied, spec_mm, spec_copied, y_re, y_im = (
            sem(n) for n in ("zt_turned", "zt_copied", "spec_mm", "spec_copied", "y_re", "y_im"))
        inv_mm, hy_out, hy_hi, hy_lo = sem("inv_mm"), sem("hy_out"), sem("hy_hi"), sem("hy_lo")
        ret_loaded, dec_exp, dec_used, dec_ready = sem("ret_loaded"), sem("dec_exp"), sem("dec_used"), sem("dec_ready")
        rope_mm, rope_cos, rope_ready = sem("rope_mm"), sem("rope_cos"), sem("rope_ready")
        rs_ready, rp_ready, ry_ready, ryc_ready = sem("rs_ready"), sem("rp_ready"), sem("ry_ready"), sem("ryc_ready")
        rm_ready, rc_ready, rq_ready, rv_ready, ri_ready, rr_ready, rn_ready = (
            sem(n) for n in ("rm_ready", "rc_ready", "rq_ready", "rv_ready", "ri_ready", "rr_ready", "rn_ready"))
        rg_ready, rz_ready, zh_ready, zl_ready = sem("rg_ready"), sem("rz_ready"), sem("zh_ready"), sem("zl_ready")
        on_sq, on_inv, on_rstd, on_ready = sem("on_sq"), sem("on_inv"), sem("on_rstd"), sem("on_ready")
        mem_loaded, mem_turned, mem_ready = sem("mem_loaded"), sem("mem_turned"), sem("mem_ready")
        cnt_loaded, fin_turned, fin_copied, stored = sem("cnt_loaded"), sem("fin_turned"), sem("fin_copied"), sem("stored")

        ROWS = [("b_mod", 0, 0, 72), ("norm_gain", None, 72, 48), ("c", None, 120, 8),
                ("b_mod", 1, 128, 72), ("hy_conv_w", None, 200, 36), ("hy_conv_b", None, 236, 12), ("hy_bias", None, 248, 4),
                ("c_ctx", None, 256, 8), ("g_ffn1_2", None, 264, 8), ("g_mix_2", None, 272, 8), ("g_out_a_2", None, 280, 6),
                ("g_out_b_2", None, 286, 2), ("g_cross_2", None, 288, 8), ("g_mem_2", None, 296, 8),
                ("g_ffn2_2", None, 304, 8), ("g_final_2", None, 312, 8)]
        SHORT = [("na_q_gain", 320, 2), ("na_k_gain", 321, 2), ("hy_fb1", 322, 1), ("hy_fb2", 323, 1),
                 ("hy_fb3", 324, 1), ("hy_freq", 325, 1)]
        COL = {(n, i): at for n, i, at, _ in ROWS} | {(n, None): at for n, at, _ in SHORT}
        N_ROWS = len(ROWS) + sum(m for _, _, m in SHORT)

        def col(name, c=0, rows=P):
            at = COL[(name, None)] + c
            return pcol[0:rows, at:at + 1]

        def mod_col(layer, m, c, s):
            return modT[:, (layer * N_MOD + m) * DC + c, s:s + 1]

        def flat(ap):
            n = len(ap.shape)
            return ap.rearrange({1: "a -> a", 2: "a b -> (a b)", 3: "a b c -> (a b c)"}[n])

        GEMMS = []

        def gemm(name, kind, w, kc, blocks, T, cols, rhs, parts=1, tok=False, dest=None, scale=1.0, gate=None, ffn=None, need=(), norm=None):
            g = dict(name=name, kind=kind, w=w, kc=kc, blocks=blocks, T=T, cols=cols, rhs=rhs, parts=parts, tok=tok,
                     dest=dest, scale=scale, gate=gate, ffn=ffn, units=blocks // parts, need=list(need), norm=norm, mods=0, m0=0)
            last = GEMMS[-1] if GEMMS else None
            g["w0"] = last["w0"] + last["blocks"] if last else 0
            g["u0"] = last["u0"] + last["units"] if last else 0
            assert blocks % (2 * parts) == 0
            GEMMS.append(g)
            return g

        def x_rhs(kp, c, T, kc):
            return XH[:, c, 0:T], XL[:, c, 0:T]

        def z_rhs(kp, c, T, kc):
            return ZH[:, kp * kc + c, 0:T], ZL[:, kp * kc + c, 0:T]

        def g_rhs(kp, c, T, kc):
            return GH[:, kp * kc + c, 0:T], GL[:, kp * kc + c, 0:T]

        def m_rhs(kp, c, T, kc):
            return MH[:, c, 0:T], ML[:, c, 0:T]

        ffns = []

        def ffn(name, w_in, w_out, T, gate, norm):
            f = len(ffns)
            ffns.append(name)
            gemm(name + "_in", "ffn", w_in, DC, FC, T, None, x_rhs, ffn=f, norm=norm)
            return gemm(name + "_out", "resid", w_out, KC_MAX, 8, T, 256, g_rhs, parts=2, gate=gate, need=[(gl_done, FC * f + KC_MAX)], ffn=f)

        def gates(layer, m):
            return lambda c, s: mod_col(layer, m, c, s)

        w = io
        G = {}
        G["f0a"] = ffn("ffn_0a", w["ffn_a_in"][0], w["ffn_a_out"][0], BOTH, gates(0, 2), 0)
        G["qk1"] = gemm("even_qk", "store", w["even_in"][0], DC, 4, BOTH, 256, x_rhs, dest=qk1, norm=1)
        G["v1"] = gemm("even_v", "store", w["even_in"][0][:, 1024:], DC, 2, BOTH, 256, x_rhs, tok=True, dest=V1)
        G["u1"] = gemm("even_u", "store", w["even_in"][0][:, 1536:], DC, 6, BOTH, 256, x_rhs, dest=u1)
        G["o1"] = gemm("even_out", "resid", w["even_out"][0], DC, 4, BOTH, 256, x_rhs, gate=gates(0, 5),
                       need=[(ot_lo, 4), (hy_lo, 4)])
        G["f0b"] = ffn("ffn_0b", w["ffn_b_in"][0], w["ffn_b_out"][0], BOTH, gates(0, 8), 2)
        G["f1a"] = ffn("ffn_1a", w["ffn_a_in"][1], w["ffn_a_out"][1], BOTH, gates(1, 2), 3)
        G["qr"] = gemm("ret_q", "store", w["ret_in"][0], DC, 4, SEQ, 256, x_rhs, dest=qr, norm=4)
        G["kr"] = gemm("ret_k", "store", w["ret_in"][0][:, 1024:], DC, 4, BOTH, 256, x_rhs, dest=kr)
        G["vr"] = gemm("ret_v", "store", w["ret_in"][0][:, 2048:], DC, 8, BOTH, 256, x_rhs, tok=True, dest=Vr)
        G["gr"] = gemm("ret_g", "store", w["ret_in"][0][:, 4096:], DC, 8, SEQ, 256, x_rhs, dest=gr)
        G["or"] = gemm("ret_out", "resid", w["ret_out"][0], DC, 8, SEQ, 256, z_rhs, parts=2, gate=gates(1, 5),
                       need=[(zl_ready, 16)])
        G["f1b"] = ffn("ffn_1b", w["ffn_b_in"][1], w["ffn_b_out"][1], SEQ, gates(1, 8), 5)
        G["f2a"] = ffn("ffn_2a", w["w_ffn1_gu_2"][0], w["w_ffn1_down_2"][0], SEQ, 0.5, 6)
        wi = w["w_in_2"][0]
        G["q2"] = gemm("mix_q", "store", wi, DC, 4, SEQ, [0, 256, 512, 2304], x_rhs, dest=qk2[:, 0:8], scale=0.125, norm=7)
        G["k2"] = gemm("mix_k", "store", wi, DC, 4, SEQ, [768, 1024, 1280, 2560], x_rhs, dest=qk2[:, 8:16])
        G["v2"] = gemm("mix_v", "store", wi, DC, 4, SEQ, [1536, 1792, 2048, 2816], x_rhs, tok=True, dest=V2)
        G["o2"] = gemm("mix_out", "resid", w["w_out_2"][0], DC, 4, SEQ, 256, x_rhs, gate=1.0, need=[(ot_lo, 4 + 8)])
        G["qc"] = gemm("cross_q", "store", w["w_cq_2"][0], DC, 4, SEQ, 256, x_rhs, dest=qkc[:, 0:8], scale=0.0625, norm=8)
        G["kc"] = gemm("cross_k", "store", w["w_ckv_2"][0], DC, 4, SEQ, 256, m_rhs, dest=qkc[:, 8:16], norm=9)
        G["vc"] = gemm("cross_v", "store", w["w_ckv_2"][0][:, 1024:], DC, 4, SEQ, 256, m_rhs, tok=True, dest=Vc)
        G["oc"] = gemm("cross_out", "resid", w["w_co_2"][0], DC, 4, SEQ, 256, x_rhs, gate=1.0, need=[(ot_lo, 4 + 8 + 8)])
        G["f2b"] = ffn("ffn_2b", w["w_ffn2_gu_2"][0], w["w_ffn2_down_2"][0], SEQ, 0.5, 10)
        MOD_BLOCKS = N_MOD * DC
        MOD_FIRST = 10
        m = MOD_FIRST
        for name, pairs in (("ffn_0a_in", FC // 2), ("ffn_0b_in", FC // 2), ("ffn_1a_in", 9)):
            g = next(x for x in GEMMS if x["name"] == name)
            g["mods"], g["m0"] = pairs, m
            m += 2 * pairs
        assert m == MOD_BLOCKS

        def drained(g):
            return g["u0"] + g["units"]

        def segs(T):
            return [(s, slice(s * SEQ, (s + 1) * SEQ)) for s in range(T // SEQ)]

        UNITS = []

        def na_units():
            for part in range(2):
                for h in range(NA_HEADS):
                    rows = slice(64 * (h % 2), 64 * (h % 2) + 64)
                    for qt in range(2):
                        q0, k0 = SEQ * part + P * qt, SEQ * part
                        UNITS.append(dict(
                            q=[qk1[rows, h // 2, q0:q0 + P]], k=[qk1[rows, 4 + h // 2, k0:BOTH]], nk=BOTH - k0,
                            bias=na_bias[:, 2 * h + qt, :] if part == 0 else None, count=None,
                            v=[V1[:, k0 // P + t, 64 * h:64 * h + 64] for t in range((BOTH - k0) // P)],
                            dst=O1[:, 2 * part + qt, 64 * h:64 * h + 64]))

        def rel_units():
            for h in range(N_HEADS_2):
                rows = slice(64 * (h % 2), 64 * (h % 2) + 64)
                for qt in range(2):
                    nk, at = P * (qt + 1), P * qt
                    UNITS.append(dict(
                        q=[qk2[rows, h // 2, P * qt:P * qt + P]], k=[qk2[rows, 8 + h // 2, 0:nk]], nk=nk,
                        bias=rel_bias[:, h, at:at + nk], count=rel_count[:, at:at + nk] if h < N_HEADS_A else None,
                        v=[V2[:, t, 64 * h:64 * h + 64] for t in range(qt + 1)], dst=O2[:, qt, 64 * h:64 * h + 64]))

        def cross_units():
            for h in range(4):
                for qt in range(2):
                    UNITS.append(dict(
                        q=[qkc[:, 2 * h + c, P * qt:P * qt + P] for c in range(2)], k=[qkc[:, 8 + 2 * h + c, :] for c in range(2)],
                        nk=SEQ, bias=None, count=None, v=[Vc[:, t, SEQ * h:SEQ * h + SEQ] for t in range(2)],
                        dst=O2[:, qt, SEQ * h:SEQ * h + SEQ]))

        na_units()
        NA = (0, len(UNITS))
        rel_units()
        REL = (NA[1], len(UNITS))
        cross_units()
        CROSS = (REL[1], len(UNITS))
        counted = [sum(u["count"] is not None for u in UNITS[:n + 1]) for n in range(len(UNITS))]

        def drained_chunk(g):
            return lambda c: (units_drained, g["u0"] + c // 2 + 1)

        def mod_norm(layer, j, T, wait):
            return dict(src=X, T=T, a=lambda c, s: norm_a[:, 3 * layer + j, c, s:s + 1],
                        b=lambda c, s: mod_col(layer, 3 * j, c, s), h=XH, l=XL, wait=wait, sq={(0, 0): SQ_first, (0, 1): SQ, (1, 2): SQ}.get((layer, j), SQ_mid))

        def gain_norm(name, wait, src=X, h=XH, l=XL, sq=SQ):
            return dict(src=src, T=SEQ, a=lambda c, s: col(name, c), b=None, h=h, l=l, wait=wait, sq=sq)

        NORMS = [mod_norm(0, 0, BOTH, lambda c: (x_ready, c + 1)), mod_norm(0, 1, BOTH, drained_chunk(G["f0a"])),
                 mod_norm(0, 2, BOTH, drained_chunk(G["o1"])), mod_norm(1, 0, BOTH, drained_chunk(G["f0b"])),
                 mod_norm(1, 1, BOTH, drained_chunk(G["f1a"])), mod_norm(1, 2, SEQ, drained_chunk(G["or"])),
                 gain_norm("g_ffn1_2", drained_chunk(G["f1b"])), gain_norm("g_mix_2", drained_chunk(G["f2a"])),
                 gain_norm("g_cross_2", drained_chunk(G["o2"])),
                 gain_norm("g_mem_2", lambda c: (mem_ready, c + 1), src=memX, h=MH, l=ML, sq=SQM),
                 gain_norm("g_ffn2_2", drained_chunk(G["oc"])), gain_norm("g_final_2", drained_chunk(G["f2b"]), h=None)]
        BANK_N = 4

        block = ctx.enter_context(nc.Block())

        @block.sync
        def _(sp):
            sp.dma_start(x_tok[:, 0:2, :], io["x"][0].rearrange("(t p) d -> p t d", p=P)).then_inc(x_loaded, 16)
            sp.dma_start(x_tok[:, 2:4, :], io["ctx"][0].rearrange("(t p) d -> p t d", p=P)).then_inc(x_loaded, 16)

            mod_w = io["w_mod"].rearrange("l (c p) n -> p l c n", p=P)

            def mod_load(m0, i, k):
                layer, first = divmod(m0, MOD_BLOCKS // 2)
                for t in range(2):
                    if not (isinstance(i, int) and m0 + 2 * i < 2):
                        sp.wait_ge(mod_lo, 2 * (m0 + k - 2) + t + 1 + 4 * i)
                    src = mod_w[:, layer, :, bass.ds(256 * (first + k) + P * t + 512 * i, P)]
                    sp.dma_start(M32[k][:, t], src).then_inc(mod_loaded[k][t], 16)

            def load(g, wv, k, t, col0, kp):
                src = wv[:, kp * g["kc"]:(kp + 1) * g["kc"], bass.ds(col0, P)]
                sp.dma_start(W32[:, k, t, 0:g["kc"], :], src).then_inc(loaded[k][t], 16)

            for g in GEMMS:
                wv = g["w"].rearrange("(c p) n -> p c n", p=P)

                def pair(i, slot_free, g=g, wv=wv):
                    for k in range(2):
                        for t in range(2):
                            slot_free(k, t)
                            if g["kind"] == "ffn":
                                load(g, wv, k, t, (2 * i + k) * P + t * FF, 0)
                            elif g["parts"] == 2:
                                load(g, wv, k, t, 256 * i + P * t, k)
                            elif g["cols"] == 256:
                                load(g, wv, k, t, 512 * i + 256 * k + P * t, 0)
                            else:
                                load(g, wv, k, t, g["cols"][2 * i + k] + P * t, 0)

                def split_before(i, w0=g["w0"]):
                    return lambda k, t: sp.wait_ge(lo_ready, 2 * (w0 - 2 + k) + t + 1 + 4 * i)

                n, mods = g["blocks"] // 2, g["mods"]
                begin = 0
                if g["w0"] == 0:
                    for i in range(2):
                        for k in range(2):
                            mod_load(0, i, k)
                    pair(0, lambda k, t: None)
                    with sp.Fori(2, MOD_FIRST // 2) as i:
                        for k in range(2):
                            mod_load(0, i, k)
                    for k in range(2):
                        mod_load(g["m0"], 0, k)
                    begin = 1
                if mods:
                    if g["name"] == "ffn_0b_in":
                        pair(0, split_before(0))
                        sp.wait_ge(hy_lo, 4)
                        for k in range(2):
                            mod_load(g["m0"], 0, k)
                        begin = 1
                    edge = min(max((MOD_BLOCKS // 2 - g["m0"]) // 2, 0), mods) or mods
                    for lo, hi in ((begin, edge), (edge, mods)):
                        if lo < hi:
                            with sp.Fori(lo, hi) as i:
                                pair(i, split_before(i))
                                for k in range(2):
                                    if lo == edge:
                                        mod_load(g["m0"] + 2 * edge, i - edge, k)
                                    else:
                                        mod_load(g["m0"], i, k)
                    begin = mods
                if isinstance(g["cols"], list):
                    for i in range(n):
                        pair(i, split_before(i))
                elif begin < n:
                    with sp.Fori(begin, n) as i:
                        pair(i, split_before(i))

            sp.wait_ge(stored, 32)

        @block.tensor
        def _(pe):
            mm, turn = pe.matmul, pe.transpose

            def pe_mod(m, k):
                for t in range(2):
                    pe.wait_ge(mod_lo, 2 * m + t + 1)
                    if t == 0 and not (isinstance(m, int) and m < 2):
                        pe.wait_ge(mod_drained, m - 1)
                    dst = PS[:, 6 + k, 4 * t:4 * t + 4]
                    for c in range(DC):
                        mm(dst, MWH[k][:, t, c], silu_s[:, c, :], start=(c == 0), stop=False, skip_group_check=True)
                        ins = mm(dst[:, 0:2], MWL[k][:, t, c], silu_s[:, c, 0:2], start=False, stop=(c == DC - 1),
                                 skip_group_check=True)
                ins.then_inc(mod_used, 1)

            def pe_gemm(g):
                kc, T = g["kc"], g["T"]

                def three(dst, t, k, kp, c):
                    xh, xl = g["rhs"](kp, c, T, kc)
                    wh, wl = WH[:, k, t, c, :], WL[:, k, t, c, :]
                    mm(dst, wh, xh, start=(kp == 0 and c == 0), stop=False, skip_group_check=True)
                    mm(dst, wh, xl, start=False, stop=False, skip_group_check=True)
                    return mm(dst, wl, xh, start=False, stop=(kp == g["parts"] - 1 and c == kc - 1), skip_group_check=True)

                def one(k, kp, pair, w, u, first=False):
                    if kp == 0 and not (isinstance(u, int) and u < 2):
                        pe.wait_ge(units_drained, u - 1)
                    if kp == 1 and g["kind"] == "resid" and g["ffn"] is not None:
                        pe.wait_ge(gl_done, FC * (g["ffn"] + 1))
                    if g["tok"]:
                        pe.wait_ge(lo_ready, 2 * w + 2)
                        for tt in range(T // P):
                            dst = PS[:, 2 * pair + tt // 2, 256 * (tt % 2):256 * (tt % 2) + 256].rearrange("p (a b) -> p a b", a=2)
                            for c in range(kc):
                                xh, xl = g["rhs"](kp, c, T, kc)
                                xh, xl = xh[:, P * tt:P * tt + P], xl[:, P * tt:P * tt + P]
                                wh, wl = WH[:, k, :, c, :], WL[:, k, :, c, :]
                                mm(dst, xh, wh, start=(c == 0), stop=False)
                                mm(dst, xh, wl, start=False, stop=False)
                                ins = mm(dst, xl, wh, start=False, stop=(c == kc - 1))
                    elif first and g["norm"] is not None:
                        pe.wait_ge(lo_ready, 2 * w + 2)
                        for c in range(kc):
                            pe.wait_ge(xl_ready, DC * g["norm"] + c + 1)
                            for t in range(2):
                                ins = three(PS[:, 2 * pair + t, 0:T], t, k, kp, c)
                    else:
                        for t in range(2):
                            pe.wait_ge(lo_ready, 2 * w + t + 1)
                            for c in range(kc):
                                ins = three(PS[:, 2 * pair + t, 0:T], t, k, kp, c)
                    ins.then_inc(block_used, 1)

                def turn_of(i, mods, first=False):
                    for b in range(2 * g["parts"]):
                        pair, kp = b // g["parts"], b % g["parts"]
                        one(b % 2, kp, pair, g["w0"] + b + 2 * g["parts"] * i, g["u0"] + pair + 2 * i, first and b == 0)
                        if mods:
                            pe_mod(g["m0"] + b + 2 * i, b)

                for s, v in g["need"]:
                    pe.wait_ge(s, v)
                n, mods, begin = g["units"] // 2, g["mods"], 0
                if g["norm"] is not None:
                    turn_of(0, mods > 0, True)
                    begin = 1
                if mods > begin:
                    with pe.Fori(begin, mods) as i:
                        turn_of(i, True)
                    begin = mods
                if begin < n:
                    with pe.Fori(begin, n) as i:
                        turn_of(i, False)

            def pe_norm(n):
                N = NORMS[n]
                for c in range(DC):
                    pe.wait_ge(sq_ready, DC * n + c + 1)
                    ins = mm(PS[:, BANK_N, 0:N["T"]], ones, N["sq"][:, c, 0:N["T"]], start=(c == 0), stop=(c == DC - 1))
                ins.then_inc(ms_ready, 1)

            def pe_attend(span):
                lo, hi = span
                for u in range(lo, hi + 2):
                    if u < hi:
                        U = UNITS[u]
                        s = PS[:, 4 + u % 2, 0:U["nk"]]
                        if u - lo >= 2:
                            pe.wait_ge(probs_ready, u - 1)
                        for c, (q, k) in enumerate(zip(U["q"], U["k"])):
                            ins = mm(s, q, k, start=(c == 0), stop=(c == len(U["q"]) - 1 and U["bias"] is None), skip_group_check=True)
                        if U["bias"] is not None:
                            nb = U["bias"].shape[-1]
                            ins = mm(s[:, 0:nb], flip, U["bias"],
                                     start=False, stop=True, skip_group_check=True)
                        ins.then_inc(scores_ready, 1)
                    if lo <= u - 1 < hi:
                        U = UNITS[u - 1]
                        if U["count"] is None:
                            pe.wait_ge(probs_ready, u)
                        else:
                            pe.wait_ge(probs_counted, counted[u - 1])
                        if u - 1 - lo >= 2:
                            pe.wait_ge(turned_copied, u - 2)
                        for t in range(U["nk"] // P):
                            ins = turn(PS[:, 2 + (u - 1) % 2, P * t:P * t + P], probs[:, (u - 1) % 2, P * t:P * t + P], eye)
                        ins.then_inc(turned_ready, 1)
                    if u - 2 >= lo:
                        U = UNITS[u - 2]
                        pe.wait_ge(turned_copied, u - 1)
                        if u - 2 - lo >= 2:
                            pe.wait_ge(out_done, u - 3)
                        dv = U["dst"].shape[-1]
                        for t, v in enumerate(U["v"]):
                            ins = mm(PS[:, 6 + u % 2, 0:dv], probsT[:, u % 2, P * t:P * t + P], v,
                                     start=(t == 0), stop=(t == len(U["v"]) - 1))
                        ins.then_inc(out_ready, 1)

            def pe_turn_out(O, tiles, n, base, need):
                pe.wait_ge(*need)
                for c in range(n):
                    if c >= 2:
                        pe.wait_ge(ot_lo, base + c - 1)
                    for t in range(tiles):
                        ins = turn(PS[:, 4 + c % 2, P * t:P * t + P], O[:, t, P * c:P * c + P], eye)
                    ins.then_inc(ot_turned, 1)

            pe.wait_ge(mats_loaded, 16)
            pe.wait_ge(rows_loaded, 16 * N_ROWS)
            for n in range(3):
                ins = turn(PS[:, 4, P * n:P * n + P], prow[:, n, :], eye)
            ins.then_inc(rows_turned, 1)
            pe.wait_ge(x_loaded, 32)
            for c in range(DC):
                if c % 4 == 0:
                    pe.wait_ge(pcol_ready, 1)
                if c >= 4:
                    pe.wait_ge(x_ready, c - 3)
                for t in range(4):
                    ins = turn(PS[:, 4 + c % 4, P * t:P * t + P], x_tok[:, t, P * c:P * c + P], eye)
                ins.then_inc(x_turned, 1)
            def filter_step(n):
                if n < 3:
                    if n == 0:
                        pe.wait_ge(filt_loaded, 16 * 6)
                        pe.wait_ge(x_ready, DC)
                        ins = mm(PS[0:64, 4, 0:SEQ], fw[0:17, 0:64], embT[:, :], start=True, stop=True)
                    else:
                        pe.wait_ge(filt_sin, n)
                        ins = mm(PS[0:64, 4, 0:SEQ], fw[:, 64 * n:64 * n + 64], h_act[0:64, (n - 1) % 2, :], start=True, stop=True)
                    ins.then_inc(filt_mm, 1)
                elif n == 3:
                    pe.wait_ge(filt_sin, 3)
                    for q in range(4):
                        ins = mm(PS[:, 2 + q, :], h_act[0:64, 0, P * (q // 2):P * (q // 2) + P],
                                 fw[:, 192 + HY_W * (q % 2):192 + HY_W * (q % 2) + HY_W], start=True, stop=True)
                        ins.then_inc(filt_mm, 1)
                else:
                    pe.wait_ge(filt_sd, 4)
                    pe.wait_ge(dft_loaded, 16)
                    for q, (m, f, h) in enumerate([(0, 0, h_sum), (0, 1, h_sum), (1, 0, h_sum), (2, 0, h_dif), (2, 1, h_dif)]):
                        for t in range(2):
                            ins = mm(PS[:, q, :], dft_setup[:, 2 * m + t, P * f:P * f + P], h[:, t, :], start=(t == 0), stop=(t == 1))
                        ins.then_inc(filt_k, 1)

            pe.wait_ge(silu_s_ready, 1)
            for i in range(MOD_FIRST // 2):
                for k in range(2):
                    pe_mod(2 * i + k, k)
                filter_step(i)
            pe.wait_ge(rel_loaded, 48)
            mm(PS[0:N_HEADS_2, 5, :], relb[:, :], onehot[0:REL_BUCKETS, :], start=True, stop=True).then_inc(rel_mm, 1)
            pe.wait_ge(filt_ready, 5)
            pe.wait_ge(rel_vec, 1)
            pe_norm(0)
            gi = {g["name"]: g for g in GEMMS}
            pe_gemm(gi["ffn_0a_in"])
            pe_gemm(gi["ffn_0a_out"])
            pe_norm(1)
            for n in ("even_qk", "even_v", "even_u"):
                pe_gemm(gi[n])
            for t in range(8):
                pe.wait_ge(qk_sq, t + 1)
                if t >= 2:
                    pe.wait_ge(qk_inv, t - 1)
                mm(PS[:, 4 + t % 2, :], block_ones, area(23040 + 512 * (t % 2), BOTH), start=True, stop=True).then_inc(qk_ms, 1)
            pe.wait_ge(qk_ready, 8)
            pe.wait_ge(nab_ready, 16)
            pe.wait_ge(units_drained, drained(gi["even_v"]))
            pe_attend(NA)
            pe_turn_out(O1, 4, 4, 0, (out_done, NA[1]))
            pe.wait_ge(z_ready, 4)
            for t in range(4):
                for c in range(4):
                    ins = turn(PS[:, (6, 7, 2, 3)[t], P * c:P * c + P], hy_z[:, c, P * t:P * t + P], eye)
                ins.then_inc(zt_turned, 1)
            pe.wait_ge(zt_copied, 4)
            pe.wait_ge(ot_lo, 4)
            pe.wait_ge(dft_back, 32)
            for s in range(2):
                for n in range(4):
                    if s == 1:
                        pe.wait_ge(spec_copied, n + 1)
                    m = 0 if n < 2 else 3
                    for t in range(2):
                        ins = mm(PS[:, 4 + n, :], dft[:, 2 * m + t, P * (n % 2):P * (n % 2) + P], hy_zt[:, 2 * s + t, :],
                                 start=(t == 0), stop=(t == 1))
                    ins.then_inc(spec_mm, 1)
            pe.wait_ge(y_re, 4)
            pe.wait_ge(y_im, 4)
            for c in range(4):
                if c >= 2:
                    pe.wait_ge(hy_out, c - 1)
                for s in range(2):
                    for n in range(4):
                        ins = mm(PS[:, 2 + c % 2, SEQ * s:SEQ * s + SEQ], hy_y[:, 4 * s + n, P * c:P * c + P], idft[:, n, :],
                                 start=(n == 0), stop=(n == 3), skip_group_check=True)
                ins.then_inc(inv_mm, 1)
            pe_gemm(gi["even_out"])
            pe_norm(2)
            pe_gemm(gi["ffn_0b_in"])
            pe_gemm(gi["ffn_0b_out"])
            pe_norm(3)
            pe_gemm(gi["ffn_1a_in"])
            pe_gemm(gi["ffn_1a_out"])
            pe_norm(4)
            for n in ("ret_q", "ret_k", "ret_v", "ret_g"):
                pe_gemm(gi[n])
            for t in range(16):
                pe.wait_ge(units_drained, drained(gi["ret_q"] if t < 8 else gi["ret_k"]))
                if t >= 2:
                    pe.wait_ge(rope_ready, t - 1)
                src = qr[:, t, :] if t < 8 else kr[:, t - 8, 0:SEQ]
                mm(PS[:, 4 + t % 2, 0:SEQ], rot, src, start=True, stop=True).then_inc(rope_mm, 1)
            pe.wait_ge(rope_ready, 16)
            pe.wait_ge(units_drained, drained(gi["ret_g"]))
            for h in range(RET_HEADS):
                for t in range(4):
                    n = 4 * h + t
                    if n >= 2:
                        pe.wait_ge(rp_ready, n - 1)
                    for c in range(2):
                        ins = mm(PS[:, 4 + t % 2, 0:SEQ], kr[:, 2 * h + c, P * t:P * t + P], qr[:, 2 * h + c, :],
                                 start=(c == 0), stop=(c == 1))
                    ins.then_inc(rs_ready, 1)
                pe.wait_ge(rp_ready, 4 * h + 4)
                if h:
                    pe.wait_ge(ryc_ready, 4 * h)
                for e in range(4):
                    for t in range(4):
                        ins = mm(PS[:, 6 + e // 2, SEQ * (e % 2):SEQ * (e % 2) + SEQ], Vr[:, t, 512 * h + P * e:512 * h + P * e + P],
                                 ret_p[:, 4 * (h % 2) + t, :], start=(t == 0), stop=(t == 3), skip_group_check=True)
                    ins.then_inc(ry_ready, 1)
                for e in range(4):
                    pe.wait_ge(ryc_ready, 4 * h + e + 1)
                    ins = mm(PS[:, 2, 0:SEQ], ones, ret_y[:, 4 * (h % 2) + e, :], start=(e == 0), stop=(e == 3))
                ins.then_inc(rm_ready, 1)
                for e in range(4):
                    pe.wait_ge(rq_ready, 4 * h + e + 1)
                    ins = mm(PS[:, 3, 0:SEQ], ones, ret_sq[:, e, :], start=(e == 0), stop=(e == 3))
                ins.then_inc(rv_ready, 1)
            pe_gemm(gi["ret_out"])
            pe_norm(5)
            pe_gemm(gi["ffn_1b_in"])
            pe_gemm(gi["ffn_1b_out"])
            pe_norm(6)
            pe_gemm(gi["ffn_2a_in"])
            pe_gemm(gi["ffn_2a_out"])
            pe_norm(7)
            for n in ("mix_q", "mix_k", "mix_v"):
                pe_gemm(gi[n])
            pe.wait_ge(units_drained, drained(gi["mix_v"]))
            pe.wait_ge(rel_back, 32)
            pe_attend(REL)
            pe_turn_out(O2n, 2, 8, 4, (on_ready, 4))
            pe_gemm(gi["mix_out"])
            pe_norm(8)
            pe_gemm(gi["cross_q"])
            pe.wait_ge(mem_loaded, 16)
            for c in range(DC):
                if c >= 2:
                    pe.wait_ge(mem_ready, c - 1)
                for t in range(2):
                    ins = turn(PS[:, 6 + c % 2, P * t:P * t + P], mem_tok[:, t, P * c:P * c + P], eye)
                ins.then_inc(mem_turned, 1)
            pe_norm(9)
            pe_gemm(gi["cross_k"])
            pe_gemm(gi["cross_v"])
            pe.wait_ge(units_drained, drained(gi["cross_v"]))
            pe_attend(CROSS)
            pe_turn_out(O2, 2, 8, 12, (out_done, CROSS[1]))
            pe_gemm(gi["cross_out"])
            pe_norm(10)
            pe_gemm(gi["ffn_2b_in"])
            pe_gemm(gi["ffn_2b_out"])
            pe_norm(11)
            pe.wait_ge(h_ready, DC * 12)
            for t in range(2):
                for c in range(DC):
                    ins = turn(PS[:, 4 + 2 * t + c // 4, P * (c % 4):P * (c % 4) + P], SQ[:, c, P * t:P * t + P], eye)
                    if c % 4 == 3:
                        ins.then_inc(fin_turned, 1)

        @block.scalar
        def _(act):
            def copy(dst, src, scale=1.0):
                return act.activation(dst, src, ACT.Copy, scale=scale)

            def split(g, i, k, first=False):
                if not (first and g["w0"] == 0):
                    act.wait_ge(block_used, g["w0"] + k - 1 + 2 * i)
                for t in range(2):
                    act.wait_ge(loaded[k][t], 16 * (g["w0"] // 2 + 1) + 16 * i)
                    copy(WH[:, k, t, 0:g["kc"], :], W32[:, k, t, 0:g["kc"], :], W_SCALE).then_inc(hi_ready, 1)

            def mod_split(m0, i, k, first=False):
                if not first:
                    act.wait_ge(mod_used, m0 + k - 1 + 2 * i)
                for t in range(2):
                    act.wait_ge(mod_loaded[k][t], 16 * (m0 // 2 + 1) + 16 * i)
                    copy(MWH[k][:, t], M32[k][:, t], W_SCALE).then_inc(mod_hi, 1)

            def begin(g):
                for k in range(2):
                    split(g, 0, k, True)
                    if g["mods"]:
                        mod_split(g["m0"], 0, k)

            def act_gemm(g):
                n, T, u0 = g["blocks"] // 2, g["T"], g["u0"]

                def silu(i, k):
                    act.wait_ge(block_used, g["w0"] + k + 1 + 2 * i)
                    act.activation(ffn_s[:, k, 0:T], PS[:, 2 * k, 0:T], ACT.Silu, scale=1.0 / W_SCALE).then_inc(silu_done, 1)

                def hidden(i, k):
                    act.wait_ge(units_drained, u0 + k + 1 + 2 * i)
                    copy(GH[:, bass.ds(2 * i + k, 1), 0:T], ffn_g[:, k:k + 1, 0:T]).then_inc(gh_done, 1)

                is_ffn = g["kind"] == "ffn"
                for lo, hi, mods in ((1, g["mods"], True), (max(g["mods"], 1), n, False)):
                    if lo < hi:
                        with act.Fori(lo, hi) as i:
                            for k in range(2):
                                if is_ffn:
                                    silu(i - 1, k)
                                split(g, i, k)
                                if is_ffn:
                                    hidden(i - 1, k)
                                if mods:
                                    mod_split(g["m0"], i, k)
                if is_ffn:
                    for k in range(2):
                        silu(n - 1, k)
                        hidden(n - 1, k)

            def act_norm(n):
                N = NORMS[n]
                T = N["T"]
                act.activation(warm[:, 1:2], mats[:, 1, 0:1], ACT.Sqrt)
                for c in range(DC):
                    act.wait_ge(*N["wait"](c))
                    act.activation(N["sq"][:, c, 0:T], N["src"][:, c, 0:T], ACT.Square).then_inc(sq_ready, 1)
                act.wait_ge(inv_ready, n + 1)
                act.activation(rstd[:, 0:T], var[:, 0:T], ACT.Sqrt).then_inc(rstd_ready, 1)
                act.activation(warm[:, 0:1], mats[:, 1, 0:1], ACT.Silu)
                if N["h"] is not None:
                    for c in range(DC):
                        act.wait_ge(h_ready, DC * n + c + 1)
                        copy(N["h"][:, c, 0:T], N["sq"][:, c, 0:T]).then_inc(xh_ready, 1)

            def act_attend(span):
                lo, hi = span
                for u in range(lo, hi + 1):
                    if u < hi:
                        U = UNITS[u]
                        act.wait_ge(max_ready, u + 1)
                        if u - lo >= 2:
                            act.wait_ge(turned_ready, u - 1)
                        act.activation(probs[:, u % 2, 0:U["nk"]], PS[:, 4 + u % 2, 0:U["nk"]], ACT.Exp, bias=stats[:, 0, u:u + 1],
                                       accum_out=stats[:, 1, u:u + 1]).then_inc(probs_ready, 1)
                    if u - 1 >= lo:
                        v, nk = u - 1, UNITS[u - 1]["nk"]
                        act.wait_ge(turned_ready, v + 1)
                        if v - lo >= 2:
                            act.wait_ge(out_ready, v - 1)
                        copy(probsT[:, v % 2, 0:nk], PS[:, 2 + v % 2, 0:nk]).then_inc(turned_copied, 1)

            def act_turn_out(n, T, base, gain=None):
                for c in range(n):
                    act.wait_ge(ot_turned, base + c + 1)
                    copy(XH[:, c, 0:T], PS[:, 4 + c % 2, 0:T], gain(c) if gain else 1.0).then_inc(ot_hi, 1)

            act.dma_start(mats[:, :, :], io["k_mats"]).then_inc(mats_loaded, 16)
            act.wait_ge(rows_clear, 1)
            for name, index, at, n in ROWS:
                src = flat(io[name] if index is None else io[name][index]).rearrange("(r p) -> r p", p=P)
                act.dma_start(prow[at % P:at % P + n, at // P, :], src).then_inc(rows_loaded, 16)
            for name, at, n in SHORT:
                for m in range(n):
                    act.dma_start(prow[at % P:at % P + 1, at // P, 64 * m:64 * m + 64], io[name]).then_inc(rows_loaded, 16)
            for n, name in enumerate(("ret_logit_f", "ret_logit_b")):
                src = bass.AP(tensor=io[name].tensor, offset=0, ap=[[0, P], [1, RET_HEADS]])
                act.dma_start(lg[:, RET_HEADS * n:RET_HEADS * n + RET_HEADS], src).then_inc(lg_loaded, 16)
            act.dma_start(fw[0:17, 0:64], io["hy_fw1"][0]).then_inc(filt_loaded, 16)
            act.dma_start(fw[:, 64:128], io["hy_fw2"][0]).then_inc(filt_loaded, 16)
            act.dma_start(fw[:, 128:192], io["hy_fw3"][0]).then_inc(filt_loaded, 16)
            act.dma_start(fw[:, 192:192 + D], io["hy_fw4"][0]).then_inc(filt_loaded, 16)
            act.dma_start(embT[:, :], io["k_emb"]).then_inc(filt_loaded, 16)
            act.dma_start(h_window, io["k_window"]).then_inc(filt_loaded, 16)
            act.dma_start(relb[:, :], io["rel_bias_2"]).then_inc(rel_loaded, 16)
            act.dma_start(onehot[0:REL_BUCKETS, :], io["k_onehot"]).then_inc(rel_loaded, 16)
            act.dma_start(rel_mask[0:N_HEADS_2, :], io["k_rel_mask"]).then_inc(rel_loaded, 16)

            act.wait_ge(pcol_ready, 1)
            for s, name in enumerate(("c", "c_ctx")):
                at = COL[(name, None)]
                act.activation(silu_c[:, :, s], pcol[:, at:at + DC], ACT.Silu).then_inc(silu_c_ready, 1)
            act.wait_ge(silu_c_ready, 2)
            copy(silu_s[:, :, 0:2], silu_c[:, :, :]).then_inc(silu_hi, 1)
            for c in range(DC):
                act.wait_ge(x_turned, c + 1)
                copy(X[:, c, :], PS[:, 4 + c % 4, :]).then_inc(x_ready, 1)
            act.wait_ge(x_ready, DC)
            act.dma_start(dft_setup, io["k_fwd"].rearrange("p m t f -> p (m t) f")).then_inc(dft_loaded, 16)
            act.wait_ge(lg_abs, 1)
            act.activation(lgt[:, 1, :], lgt[:, 0, :], ACT.Exp, scale=-1.0).then_inc(lg_exp, 1)
            act.wait_ge(lg_u, 1)
            act.activation(lgt[:, 3, :], lgt[:, 2, :], ACT.Ln).then_inc(lg_ln, 1)
            for i in range(MOD_FIRST // 2):
                for k in range(2):
                    mod_split(0, i, k, i == 0)
                if i < 3:
                    act.wait_ge(filt_arg, i + 1)
                    act.activation(h_act[0:64, i % 2, :], h_tmp[0:64, 2, :], ACT.Sin).then_inc(filt_sin, 1)
            for n in range(5):
                act.wait_ge(filt_k, n + 1)
                copy(filt[:, n, :], PS[:, n, :]).then_inc(filt_ready, 1)
            act.wait_ge(rel_vec, 1)
            act.dma_start(rel_dram, relvec[:, :]).then_inc(rel_stored, 16)

            order = iter(GEMMS[1:] + [None])

            def run(name):
                g = next(x for x in GEMMS if x["name"] == name)
                act_gemm(g)
                after = next(order)
                if after is not None:
                    begin(after)

            begin(GEMMS[0])
            act_norm(0)
            run("ffn_0a_in")
            run("ffn_0a_out")
            act_norm(1)
            run("even_qk")
            run("even_v")
            run("even_u")
            for t in range(9):
                if t < 8:
                    if t >= 2:
                        act.wait_ge(qk_ms, t - 1)
                    act.wait_ge(units_drained, G["qk1"]["u0"] + t // 2 + 1)
                    act.activation(area(23040 + 512 * (t % 2), BOTH), qk1[:, t, :], ACT.Square).then_inc(qk_sq, 1)
                if t >= 1:
                    act.wait_ge(qk_inv, t)
                    if t >= 3:
                        act.wait_ge(qk_ready, t - 2)
                    act.activation(area(24064 + 512 * ((t - 1) % 2), BOTH), area(25088 + 512 * ((t - 1) % 2), BOTH),
                                   ACT.Sqrt).then_inc(qk_rstd, 1)
            act.wait_ge(qk_ready, 8)
            act_attend(NA)
            act.wait_ge(out_done, NA[1])
            for n in range(12):
                tile = n if n < 4 else (4 + (n - 4) // 2 if n % 2 == 0 else 8 + (n - 4) // 2)
                if n < 4:
                    dst = hy_x0[:, n, :]
                else:
                    c = (n - 4) // 2
                    if c >= 2 and n % 2 == 0:
                        act.wait_ge(z_ready, c - 1)
                    dst = hy_xv[:, 2 * (c % 2) + n % 2, :]
                act.wait_ge(units_drained, drained(G["u1"]))
                act.activation(dst, u1[:, tile, :], ACT.Identity, scale=col("hy_conv_w", 12 + tile),
                               bias=col("hy_conv_b", tile)).then_inc(conv_mid, 1)
            act_turn_out(4, BOTH, 0)
            for t in range(4):
                act.wait_ge(zt_turned, t + 1)
                copy(hy_zt[:, t, :], PS[:, (6, 7, 2, 3)[t], :]).then_inc(zt_copied, 1)
            for s in range(2):
                if s:
                    act.wait_ge(y_re, 2)
                    act.wait_ge(y_im, 2)
                for n in range(4):
                    act.wait_ge(spec_mm, 4 * s + n + 1)
                    copy(hy_spec[:, n, :], PS[:, 4 + n, :]).then_inc(spec_copied, 1)
            for c in range(4):
                act.wait_ge(hy_out, c + 1)
                copy(XH[:, 4 + c, :], hy_z[:, c, :]).then_inc(hy_hi, 1)
            run("even_out")
            act_norm(2)
            run("ffn_0b_in")
            run("ffn_0b_out")
            act_norm(3)
            run("ffn_1a_in")
            act.wait_ge(ret_loaded, 32)
            act.wait_ge(lg_ready, 1)
            for h in range(RET_HEADS):
                if h:
                    act.wait_ge(dec_ready, h)
                for n, (d, m) in enumerate(((h, 0), (RET_HEADS + h, 0), (h, 3), (RET_HEADS + h, 4))):
                    act.activation(ret_e[:, n, :], ret_k[:, m, :], ACT.Exp, scale=lg[:, d:d + 1]).then_inc(dec_exp, 1)
            run("ffn_1a_out")
            act_norm(4)
            run("ret_q")
            run("ret_k")
            run("ret_v")
            run("ret_g")
            act.wait_ge(units_drained, drained(G["gr"]))
            for h in range(RET_HEADS):
                act.activation(gr[:, 4 * h:4 * h + 4, :], gr[:, 4 * h:4 * h + 4, :], ACT.Silu).then_inc(rg_ready, 1)
            act.wait_ge(rope_ready, 16)
            act.wait_ge(dec_ready, RET_HEADS)
            for h in range(RET_HEADS):
                y = 4 * (h % 2)
                if h >= 2:
                    act.wait_ge(zl_ready, 4 * (h - 1))
                for e in range(4):
                    act.wait_ge(ry_ready, 4 * h + 2 * (e // 2) + 2)
                    copy(ret_y[:, y + e, :], PS[:, 6 + e // 2, SEQ * (e % 2):SEQ * (e % 2) + SEQ]).then_inc(ryc_ready, 1)
                if h:
                    act.wait_ge(rv_ready, h)
                for e in range(4):
                    act.wait_ge(rc_ready, 4 * h + e + 1)
                    act.activation(ret_sq[:, e, :], ret_y[:, y + e, :], ACT.Square).then_inc(rq_ready, 1)
                act.wait_ge(ri_ready, h + 1)
                act.activation(rstd[:, 0:SEQ], var[:, 0:SEQ], ACT.Sqrt).then_inc(rr_ready, 1)
                for e in range(4):
                    act.wait_ge(rz_ready, 4 * h + e + 1)
                    copy(ZH[:, 4 * h + e, :], ret_y[:, y + e, :]).then_inc(zh_ready, 1)
            run("ret_out")
            act_norm(5)
            run("ffn_1b_in")
            run("ffn_1b_out")
            act_norm(6)
            run("ffn_2a_in")
            run("ffn_2a_out")
            act_norm(7)
            run("mix_q")
            run("mix_k")
            run("mix_v")
            act_attend(REL)
            act.wait_ge(out_done, REL[1])
            for t in range(2):
                for n, (a, b) in enumerate(((0, 768), (768, D))):
                    act.activation(O2n[:, t, a:b], O2[:, t, a:b], ACT.Square,
                                   accum_out=onorm[:, 2 * n + t:2 * n + t + 1]).then_inc(on_sq, 1)
            act.wait_ge(on_inv, 1)
            act.activation(onorm[:, 8:12], onorm[:, 4:8], ACT.Sqrt).then_inc(on_rstd, 1)
            act_turn_out(8, SEQ, 4, lambda c: col("g_out_a_2", c))
            run("mix_out")
            act_norm(8)
            run("cross_q")
            for c in range(DC):
                act.wait_ge(mem_turned, c + 1)
                copy(memX[:, c, :], PS[:, 6 + c % 2, 0:SEQ]).then_inc(mem_ready, 1)
            act_norm(9)
            run("cross_k")
            run("cross_v")
            act_attend(CROSS)
            act_turn_out(8, SEQ, 12)
            run("cross_out")
            act_norm(10)
            run("ffn_2b_in")
            run("ffn_2b_out")
            act_norm(11)
            for n in range(4):
                act.wait_ge(fin_turned, n + 1)
                copy(out_tok[:, n // 2, 512 * (n % 2):512 * (n % 2) + 512], PS[:, 4 + n, :]).then_inc(fin_copied, 1)
                if n % 2:
                    act.wait_ge(fin_copied, n + 1)
                    act.dma_start(out[0, P * (n // 2):P * (n // 2) + P, :], out_tok[:, n // 2, :]).then_inc(stored, 16)

        @block.vector
        def _(dve):
            links = [0]

            def link(ins):
                links[0] += 1
                ins.then_inc(dve_chain, 1)
                dve.wait_ge(dve_chain, links[0])

            tt, ts, stt = dve.tensor_tensor, dve.tensor_scalar, dve.scalar_tensor_tensor

            def inverse(dst, sums, n, done):
                link(ts(dst, sums, 1.0 / n, EPS, ALU.mult, ALU.add))
                dve.reciprocal(dst, dst).then_inc(done, 1)

            def split(g, i, k):
                for t in range(2):
                    dve.wait_ge(hi_ready, 2 * (g["w0"] + k) + t + 1 + 4 * i)
                    stt(WL[:, k, t, 0:g["kc"], :], W32[:, k, t, 0:g["kc"], :], W_SCALE, WH[:, k, t, 0:g["kc"], :],
                        ALU.mult, ALU.subtract).then_inc(lo_ready, 1)

            def mod_split(m0, i, k):
                for t in range(2):
                    dve.wait_ge(mod_hi, 2 * (m0 + k) + t + 1 + 4 * i)
                    stt(MWL[k][:, t], M32[k][:, t], W_SCALE, MWH[k][:, t], ALU.mult, ALU.subtract).then_inc(mod_lo, 1)

            def mod_drain(m0, i, k):
                dve.wait_ge(mod_used, m0 + k + 1 + 2 * i)
                src = PS[:, 6 + k, 0:8].rearrange("p (t h s) -> p t s h", t=2, h=2)
                dve.tensor_reduce(modT[:, bass.ds(2 * (m0 + k) + 4 * i, 2), :], src, AXX, ALU.add).then_inc(mod_drained, 1)

            def mod_finish(lo, hi, norms, half, whole):
                dve.wait_ge(mod_drained, hi)
                per = N_MOD * DC
                for layer in range(2):
                    a, b = max(2 * lo, per * layer), min(2 * hi, per * layer + per)
                    if a < b:
                        at = COL[("b_mod", layer)] - per * layer
                        for s in range(2):
                            m = modT[:, a:b, s]
                            ins = stt(m, m, 1.0 / W_SCALE, pcol[:, at + a:at + b], ALU.mult, ALU.add)
                link(ins)
                for layer, m, f in [(*x, 0.5) for x in half] + [(*x, 1.0) for x in whole]:
                    at = per * layer + DC * m
                    ins = ts(modT[:, at:at + DC, :], modT[:, at:at + DC, :], f / W_SCALE, None, ALU.mult)
                for layer, j in norms:
                    at, sc = COL[("norm_gain", None)] + (3 * layer + j) * DC, per * layer + DC * (3 * j + 1)
                    for s in range(2):
                        ins = stt(norm_a[:, 3 * layer + j, :, s], modT[:, sc:sc + DC, s], 1.0, pcol[:, at:at + DC], ALU.add, ALU.mult)
                link(ins)

            def begin(g):
                for k in range(2):
                    split(g, 0, k)
                    if g["mods"]:
                        mod_split(g["m0"], 0, k)

            def dve_gemm(g):
                n, T, u0, w0 = g["blocks"] // 2, g["T"], g["u0"], g["w0"]

                def product(i, k):
                    dve.wait_ge(silu_done, FC * g["ffn"] + k + 1 + 2 * i)
                    stt(ffn_g[:, k, 0:T], PS[:, 2 * k + 1, 0:T], 1.0 / W_SCALE, ffn_s[:, k, 0:T], ALU.mult, ALU.mult)\
                        .then_inc(units_drained, 1)

                def rest(i, k):
                    dve.wait_ge(gh_done, FC * g["ffn"] + k + 1 + 2 * i)
                    j = bass.ds(2 * i + k, 1)
                    tt(GL[:, j, 0:T], ffn_g[:, k:k + 1, 0:T], GH[:, j, 0:T], ALU.subtract).then_inc(gl_done, 1)

                def store(i, k):
                    dve.wait_ge(block_used, w0 + k + 1 + 2 * i)
                    if g["tok"]:
                        src = PS[:, 2 * k:2 * k + 2, :].rearrange("p b (t n) -> p (b t) n", t=2)[:, 0:T // P, :]
                        dst = g["dest"][:, 0:T // P, bass.ds(512 * i + 256 * k, 256)]
                    else:
                        src, dst = PS[:, 2 * k:2 * k + 2, 0:T], g["dest"][:, bass.ds(4 * i + 2 * k, 2), 0:T]
                    ts(dst, src, g["scale"] / W_SCALE, None, ALU.mult).then_inc(units_drained, 1)

                def add(u):
                    dve.wait_ge(block_used, w0 + g["parts"] * (u + 1))
                    for t in range(2):
                        c = 2 * u + t
                        for s, tok in segs(T):
                            gate = g["gate"](c, s) if callable(g["gate"]) else g["gate"] / W_SCALE
                            ins = stt(X[:, c, tok], PS[:, 2 * (u % 2) + t, tok], gate, X[:, c, tok], ALU.mult, ALU.add)
                    ins.then_inc(units_drained, 1)

                if g["kind"] == "ffn":
                    for lo, hi, mods in ((1, g["mods"], True), (max(g["mods"], 1), n, False)):
                        if lo < hi:
                            with dve.Fori(lo, hi) as i:
                                for k in range(2):
                                    product(i - 1, k)
                                    split(g, i, k)
                                    rest(i - 1, k)
                                    if mods:
                                        mod_drain(g["m0"], i - 1, k)
                                        mod_split(g["m0"], i, k)
                        if mods and g["mods"]:
                            for k in range(2):
                                mod_drain(g["m0"], g["mods"] - 1, k)
                    for k in range(2):
                        product(n - 1, k)
                        rest(n - 1, k)
                elif g["kind"] == "store":
                    if n > 1:
                        with dve.Fori(1, n) as i:
                            for k in range(2):
                                store(i - 1, k)
                                split(g, i, k)
                    for k in range(2):
                        store(n - 1, k)
                else:
                    u = 0
                    for b in range(2, g["blocks"]):
                        if g["parts"] == 1:
                            add(u)
                            u += 1
                        split(g, b // 2, b % 2)
                        if g["parts"] == 2 and b % 2:
                            add(u)
                            u += 1
                    while u < g["units"]:
                        add(u)
                        u += 1

            def dve_norm(n):
                N = NORMS[n]
                T, sq = N["T"], N["sq"]
                dve.wait_ge(ms_ready, n + 1)
                inverse(var[:, 0:T], PS[:, BANK_N, 0:T], D, inv_ready)
                for c in range(DC + 1):
                    if c < DC:
                        dve.wait_ge(t_ready, DC * n + c + 1)
                        for s, tok in segs(T):
                            if N["b"]:
                                ins = ts(sq[:, c, tok], sq[:, c, tok], N["a"](c, s), N["b"](c, s), ALU.mult, ALU.add)
                            else:
                                ins = ts(sq[:, c, tok], sq[:, c, tok], N["a"](c, s), None, ALU.mult)
                        ins.then_inc(h_ready, 1)
                    if c and N["h"] is not None:
                        dve.wait_ge(xh_ready, DC * n + c)
                        tt(N["l"][:, c - 1, 0:T], sq[:, c - 1, 0:T], N["h"][:, c - 1, 0:T], ALU.subtract).then_inc(xl_ready, 1)

            def dve_attend(span):
                lo, hi = span
                for u in range(lo, hi + 2):
                    if u < hi:
                        dve.wait_ge(scores_ready, u + 1)
                        dve.tensor_reduce(stats[:, 0, u:u + 1], PS[:, 4 + u % 2, 0:UNITS[u]["nk"]], AXX, ALU.max,
                                          negate=True).then_inc(max_ready, 1)
                    if lo <= u - 1 < hi:
                        v = u - 1
                        U = UNITS[v]
                        dve.wait_ge(probs_ready, v + 1)
                        if U["count"] is not None:
                            p = probs[:, v % 2, 0:U["nk"]]
                            dve.tensor_tensor_reduce(p, p, U["count"], 1.0, 0.0, ALU.mult, ALU.add,
                                                     stats[:, 1, v:v + 1]).then_inc(probs_counted, 1)
                            dve.wait_ge(probs_counted, counted[v])
                        dve.reciprocal(stats[:, 2, v:v + 1], stats[:, 1, v:v + 1]).then_inc(denoms, 1)
                    if u - 2 >= lo:
                        v = u - 2
                        dst = UNITS[v]["dst"]
                        dve.wait_ge(denoms, v + 1)
                        dve.wait_ge(out_ready, v + 1)
                        ts(dst, PS[:, 6 + v % 2, 0:dst.shape[-1]], stats[:, 2, v:v + 1], None, ALU.mult).then_inc(out_done, 1)

            def dve_turn_out(n, T, base, gain=None):
                for c in range(n):
                    dve.wait_ge(ot_hi, base + c + 1)
                    stt(XL[:, c, 0:T], PS[:, 4 + c % 2, 0:T], gain(c) if gain else 1.0, XH[:, c, 0:T],
                        ALU.mult, ALU.subtract).then_inc(ot_lo, 1)

            dve.memset(prow[:, :, :], 0.0).then_inc(rows_clear, 1)
            dve.wait_ge(rows_turned, 1)
            link(dve.tensor_copy(pcol[:, :], PS[:, 4, 0:3 * P]))
            q_gain = col("na_q_gain")
            ts(q_gain, q_gain, 0.125, None, ALU.mult).then_inc(pcol_ready, 1)
            dve.wait_ge(lg_loaded, 32)
            stt(lgt[:, 0, :], lg[:, :], -1.0, lg[:, :], ALU.mult, ALU.max).then_inc(lg_abs, 1)
            dve.wait_ge(lg_exp, 1)
            ts(lgt[:, 2, :], lgt[:, 1, :], 1.0, None, ALU.add).then_inc(lg_u, 1)
            dve.wait_ge(lg_u, 1)
            link(ts(lgt[:, 4, :], lgt[:, 2, :], -1.0, 1e-30, ALU.add, ALU.max))
            link(dve.reciprocal(lgt[:, 5, :], lgt[:, 4, :]))
            link(tt(lgt[:, 6, :], lgt[:, 5, :], lgt[:, 1, :], ALU.mult))
            dve.wait_ge(lg_ln, 1)
            link(tt(lgt[:, 6, :], lgt[:, 6, :], lgt[:, 3, :], ALU.mult))
            link(ts(lgt[:, 7, :], lg[:, :], 0.0, None, ALU.min))
            tt(lg[:, :], lgt[:, 7, :], lgt[:, 6, :], ALU.subtract).then_inc(lg_ready, 1)
            a, k_, r = (h_tmp[0:64, n, :] for n in range(3))
            MAGIC = 1.5 * 2.0 ** 23
            C1 = 6.28125
            C2 = float(np.float32(np.round((2 * math.pi - C1) * 2 ** 20) / 2 ** 20))
            C3 = 2 * math.pi - C1 - C2
            PI = 3.1415925

            def filter_step(n):
                if n < 3:
                    dve.wait_ge(filt_mm, n + 1)
                    if n:
                        dve.wait_ge(filt_sin, n)
                    link(ts(a, PS[0:64, 4, 0:SEQ], col(f"hy_fb{n + 1}", 0, 64), col("hy_freq", 0, 64), ALU.add, ALU.mult))
                    link(ts(k_, a, 1.0 / (2 * math.pi), MAGIC, ALU.mult, ALU.add))
                    link(ts(k_, k_, -MAGIC, None, ALU.add))
                    link(stt(r, k_, -C1, a, ALU.mult, ALU.add))
                    link(stt(r, k_, -C2, r, ALU.mult, ALU.add))
                    link(stt(r, k_, -C3, r, ALU.mult, ALU.add))
                    ts(r, r, PI, -PI, ALU.min, ALU.max).then_inc(filt_arg, 1)
                elif n == 3:
                    dve.wait_ge(filt_mm, 3 + 4)
                    for t in range(2):
                        link(tt(h_sum[:, t, :], PS[:, 2 + 2 * t, :], h_window[:, t, :], ALU.mult))
                        link(tt(hy_taps[:, t, :], PS[:, 3 + 2 * t, :], h_window[:, t, :], ALU.mult))
                        tt(h_dif[:, t, :], h_sum[:, t, :], hy_taps[:, t, :], ALU.subtract).then_inc(filt_sd, 1)
                        tt(h_sum[:, t, :], h_sum[:, t, :], hy_taps[:, t, :], ALU.add).then_inc(filt_sd, 1)

            dve.wait_ge(silu_hi, 1)
            tt(silu_s[:, :, 2:4], silu_c[:, :, :], silu_s[:, :, 0:2], ALU.subtract).then_inc(silu_s_ready, 1)
            for i in range(MOD_FIRST // 2):
                for k in range(2):
                    mod_split(0, i, k)
                filter_step(i)
                for k in range(2):
                    mod_drain(0, i, k)
            dve.wait_ge(rel_mm, 1)
            tt(relvec[:, :], PS[0:N_HEADS_2, 5, :], rel_mask[0:N_HEADS_2, :], ALU.add).then_inc(rel_vec, 1)
            begin(GEMMS[0])
            mod_finish(0, MOD_FIRST, [(0, 0)], [], [])

            order = iter(GEMMS[1:] + [None])

            def run(name):
                g = next(x for x in GEMMS if x["name"] == name)
                dve_gemm(g)
                after = next(order)
                if after is not None:
                    begin(after)

            dve_norm(0)
            run("ffn_0a_in")
            mod_finish(MOD_FIRST, 32, [(0, 1), (0, 2)], [(0, 2)], [(0, 5)])
            run("ffn_0a_out")
            dve_norm(1)
            run("even_qk")
            run("even_v")
            run("even_u")
            for t in range(9):
                if t < 8:
                    dve.wait_ge(qk_ms, t + 1)
                    inverse(area(25088 + 512 * (t % 2), BOTH), PS[:, 4 + t % 2, :], 64, qk_inv)
                if t >= 1:
                    dve.wait_ge(qk_rstd, t)
                    gain = col("na_q_gain" if t - 1 < 4 else "na_k_gain")
                    stt(qk1[:, t - 1, :], qk1[:, t - 1, :], gain, area(24064 + 512 * ((t - 1) % 2), BOTH),
                        ALU.mult, ALU.mult).then_inc(qk_ready, 1)
            dve_attend(NA)
            for n in range(12):
                tile = n if n < 4 else (4 + (n - 4) // 2 if n % 2 == 0 else 8 + (n - 4) // 2)
                dst = hy_x0[:, n, :] if n < 4 else hy_xv[:, 2 * (((n - 4) // 2) % 2) + n % 2, :]
                dst, src = (a.rearrange("p (s t) -> p s t", s=2) for a in (dst, u1[:, tile, :]))
                dve.wait_ge(conv_mid, n + 1)
                link(stt(dst[:, :, 1:], src[:, :, :SEQ - 1], col("hy_conv_w", tile), dst[:, :, 1:], ALU.mult, ALU.add))
                stt(dst[:, :, :SEQ - 1], src[:, :, 1:], col("hy_conv_w", 24 + tile), dst[:, :, :SEQ - 1],
                    ALU.mult, ALU.add).then_inc(conv_ready, 1)
            dve_turn_out(4, BOTH, 0)
            for s in range(2):
                dve.wait_ge(spec_copied, 4 * s + 4)
                for f in range(2):
                    y, t = hy_y[:, 4 * s + f, :], hy_xv[:, f, :]
                    tt(y, hy_spec[:, f, :], filt[:, f, :], ALU.mult)
                    link(tt(t, hy_spec[:, 2 + f, :], filt[:, 3 + f, :], ALU.mult))
                    tt(y, y, t, ALU.subtract).then_inc(y_re, 1)
            for c in range(5):
                if c < 4:
                    dve.wait_ge(inv_mm, c + 1)
                    link(stt(hy_xv[:, c % 2, :], hy_z[:, c, :], col("hy_bias", c), PS[:, 2 + c % 2, :], ALU.mult, ALU.add))
                    tt(hy_z[:, c, :], hy_xv[:, c % 2, :], hy_x0[:, c, :], ALU.mult).then_inc(hy_out, 1)
                if c >= 1:
                    dve.wait_ge(hy_hi, c)
                    tt(XL[:, 3 + c, :], hy_z[:, c - 1, :], XH[:, 3 + c, :], ALU.subtract).then_inc(hy_lo, 1)
            run("even_out")
            dve_norm(2)
            run("ffn_0b_in")
            mod_finish(32, 54, [(1, 0)], [(0, 8), (1, 2)], [])
            run("ffn_0b_out")
            dve_norm(3)
            run("ffn_1a_in")
            mod_finish(54, MOD_BLOCKS, [(1, 1), (1, 2)], [(1, 8)], [(1, 5)])
            run("ffn_1a_out")
            dve_norm(4)
            run("ret_q")
            run("ret_k")
            run("ret_v")
            run("ret_g")
            for t in range(16):
                x = qr[:, t, :] if t < 8 else kr[:, t - 8, 0:SEQ]
                dve.wait_ge(rope_mm, t + 1)
                link(tt(rope_t[:, 2 + t % 2, :], PS[:, 4 + t % 2, 0:SEQ], rope[:, 2 * (t % 2) + 1, :], ALU.mult))
                dve.wait_ge(rope_cos, t + 1)
                tt(x, rope_t[:, t % 2, :], rope_t[:, 2 + t % 2, :], ALU.add).then_inc(rope_ready, 1)
            dve.wait_ge(dec_ready, RET_HEADS)
            for h in range(RET_HEADS):
                y = 4 * (h % 2)
                for t in range(4):
                    dve.wait_ge(rs_ready, 4 * h + t + 1)
                    stt(ret_p[:, y + t, :], PS[:, 4 + t % 2, 0:SEQ], 0.0625, decay[:, 4 * h + t, :], ALU.mult, ALU.mult)\
                        .then_inc(rp_ready, 1)
                dve.wait_ge(rm_ready, h + 1)
                for e in range(4):
                    stt(ret_y[:, y + e, :], PS[:, 2, 0:SEQ], -1.0 / 512, ret_y[:, y + e, :], ALU.mult, ALU.add)\
                        .then_inc(rc_ready, 1)
                dve.wait_ge(rv_ready, h + 1)
                inverse(var[:, 0:SEQ], PS[:, 3, 0:SEQ], 512, ri_ready)
                dve.wait_ge(rg_ready, h + 1)
                for e in range(5):
                    if e < 4:
                        dve.wait_ge(rn_ready, 4 * h + e + 1)
                        tt(ret_y[:, y + e, :], ret_y[:, y + e, :], gr[:, 4 * h + e, :], ALU.mult).then_inc(rz_ready, 1)
                    if e >= 1:
                        dve.wait_ge(zh_ready, 4 * h + e)
                        tt(ZL[:, 4 * h + e - 1, :], ret_y[:, y + e - 1, :], ZH[:, 4 * h + e - 1, :], ALU.subtract)\
                            .then_inc(zl_ready, 1)
            run("ret_out")
            dve_norm(5)
            run("ffn_1b_in")
            run("ffn_1b_out")
            dve_norm(6)
            run("ffn_2a_in")
            run("ffn_2a_out")
            dve_norm(7)
            run("mix_q")
            run("mix_k")
            run("mix_v")
            dve.wait_ge(cnt_loaded, 16)
            dve_attend(REL)
            dve.wait_ge(on_sq, 4)
            for n, width in enumerate((768, 256)):
                ins = ts(onorm[:, 4 + 2 * n:6 + 2 * n], onorm[:, 2 * n:2 * n + 2], 1.0 / width, EPS, ALU.mult, ALU.add)
            link(ins)
            dve.reciprocal(onorm[:, 4:8], onorm[:, 4:8]).then_inc(on_inv, 1)
            dve.wait_ge(on_rstd, 1)
            for t in range(2):
                for n, (a, b) in enumerate(((0, 768), (768, D))):
                    ts(O2n[:, t, a:b], O2[:, t, a:b], onorm[:, 8 + 2 * n + t:9 + 2 * n + t], None, ALU.mult).then_inc(on_ready, 1)
            dve_turn_out(8, SEQ, 4, lambda c: col("g_out_a_2", c))
            run("mix_out")
            dve_norm(8)
            run("cross_q")
            dve_norm(9)
            run("cross_k")
            run("cross_v")
            dve_attend(CROSS)
            dve_turn_out(8, SEQ, 12)
            run("cross_out")
            dve_norm(10)
            run("ffn_2b_in")
            run("ffn_2b_out")
            dve_norm(11)

        @block.gpsimd
        def _(pool):
            tt = pool.tensor_tensor

            def pool_norm(n):
                T = NORMS[n]["T"]
                pool.wait_ge(rstd_ready, n + 1)
                for c in range(DC):
                    tt(NORMS[n]["sq"][:, c, 0:T], NORMS[n]["src"][:, c, 0:T], rstd[:, 0:T], ALU.mult).then_inc(t_ready, 1)

            pool.dma_start(na_mask, io["k_na_mask"]).then_inc(nab_loaded, 16)
            width, rows = 2 * WIN_C - 1, 15
            for h in range(NA_HEADS):
                for r in range(4):
                    src = bass.AP(tensor=io["na_rpb"].tensor, offset=(h * rows + 7 - r) * width + WIN_C - GRID_W,
                                  ap=[[1, GRID_W], [width, 4], [1, GRID_W]])
                    at = GRID_W * (1 - r % 2)
                    dst = na_bias[at:at + GRID_W, 2 * h + r // 2, :].rearrange("p (a b) -> p a b", a=4)
                    pool.dma_start(dst, src).then_inc(nab_loaded, 16)
            pool.wait_ge(nab_loaded, 16 * 33)
            for n in range(16):
                tt(na_bias[:, n, :], na_bias[:, n, :], na_mask[:, 0, :], ALU.mult).then_inc(pool_chain, 1)
            for n in range(16):
                pool.wait_ge(pool_chain, n + 1)
                tt(na_bias[:, n, :], na_bias[:, n, :], na_mask[:, 1, :], ALU.add).then_inc(nab_ready, 1)
            pool_norm(0)
            pool.wait_ge(mod_used, 32)
            pool.dma_start(dft, io["k_fwd"].rearrange("p m t f -> p (m t) f")).then_inc(dft_back, 16)
            pool.dma_start(idft, io["k_inv"].rearrange("p m t f -> p (m t) f")).then_inc(dft_back, 16)
            pool_norm(1)
            for c in range(4):
                pool.wait_ge(conv_ready, 4 + 2 * c + 2)
                tt(hy_z[:, c, :], hy_xv[:, 2 * (c % 2), :], hy_xv[:, 2 * (c % 2) + 1, :], ALU.mult).then_inc(z_ready, 1)
            for s in range(2):
                pool.wait_ge(spec_copied, 4 * s + 4)
                for f in range(2):
                    y, t = hy_y[:, 4 * s + 2 + f, :], hy_xv[:, 2 + f, :]
                    tt(y, hy_spec[:, f, :], filt[:, 3 + f, :], ALU.mult).then_inc(pool_chain, 1)
                    tt(t, hy_spec[:, 2 + f, :], filt[:, 2 if f == 0 else 1, :], ALU.mult).then_inc(pool_chain, 1)
                    pool.wait_ge(pool_chain, 16 + 2 * (2 * s + f + 1))
                    tt(y, y, t, ALU.add).then_inc(y_im, 1)
            pool_norm(2)
            pool_norm(3)
            pool.wait_ge(mod_used, MOD_BLOCKS)
            pool.dma_start(ret_k, io["k_ret"].rearrange("p m t q -> p m (t q)")).then_inc(ret_loaded, 16)
            pool.dma_start(rope, io["k_rope"].rearrange("p a b t -> p (a b) t")).then_inc(ret_loaded, 16)
            for h in range(RET_HEADS):
                pool.wait_ge(dec_exp, 4 * h + 4)
                lat, cx = (decay[:, 4 * h + 2 * n:4 * h + 2 * n + 2, :].rearrange("p a b -> p (a b)") for n in range(2))
                tt(ret_e[:, 0, :], ret_e[:, 0, :], ret_k[:, 1, :], ALU.mult).then_inc(dec_used, 1)
                tt(ret_e[:, 1, :], ret_e[:, 1, :], ret_k[:, 2, :], ALU.mult).then_inc(dec_used, 1)
                tt(cx, ret_e[:, 2, :], ret_e[:, 3, :], ALU.add).then_inc(dec_used, 1)
                pool.wait_ge(dec_used, 3 * h + 3)
                tt(lat, ret_e[:, 0, :], ret_e[:, 1, :], ALU.add).then_inc(dec_ready, 1)
            pool_norm(4)
            for t in range(16):
                x = qr[:, t, :] if t < 8 else kr[:, t - 8, 0:SEQ]
                pool.wait_ge(units_drained, drained(G["qr"] if t < 8 else G["kr"]))
                if t >= 2:
                    pool.wait_ge(rope_ready, t - 1)
                tt(rope_t[:, t % 2, :], x, rope[:, 2 * (t % 2), :], ALU.mult).then_inc(rope_cos, 1)
            for h in range(RET_HEADS):
                pool.wait_ge(rr_ready, h + 1)
                for e in range(4):
                    y = ret_y[:, 4 * (h % 2) + e, :]
                    tt(y, y, rstd[:, 0:SEQ], ALU.mult).then_inc(rn_ready, 1)
            pool.wait_ge(zl_ready, 16)
            pool.wait_ge(rel_stored, 16)
            for t in range(2):
                src = bass.AP(tensor=rel_dram.tensor, offset=P - P * t, ap=[[1, P], [BOTH, N_HEADS_2], [1, P * (t + 1)]])
                pool.dma_start(rel_bias[:, :, P * t:P * t + P * (t + 1)], src).then_inc(rel_back, 16)
            pool.dma_start(rel_count, io["k_rel_count"]).then_inc(cnt_loaded, 16)
            pool.dma_start(mem_tok, io["mem_2"][0].rearrange("(t p) d -> p t d", p=P)).then_inc(mem_loaded, 16)
            for n in range(5, 12):
                pool_norm(n)


def kernel(**inputs):
    import concourse.bacc as bacc
    from concourse.bass_utils import run_bass_kernel_spmd

    nc = bacc.Bacc("TRN2", target_bir_lowering=False, num_devices=1)
    arrays, io = {}, {}
    for name, a in {**inputs, **shape_constants()}.items():
        a = np.ascontiguousarray(a)
        arrays[f"in_{name}"] = a
        io[name] = nc.dram_tensor(f"in_{name}", a.shape, mybir.dt.from_np(a.dtype), kind="ExternalInput").ap()
    out = nc.dram_tensor("out", (1, SEQ, D), F32, kind="ExternalOutput").ap()
    program(nc, io, out)
    r = run_bass_kernel_spmd(nc, [arrays], core_ids=[0])
    return r.results[0]["out"]
```

```python
import math
from contextlib import ExitStack

import numpy as np

import concourse.bass as bass
from concourse import mybir

ACT = mybir.ActivationFunctionType
ALU = mybir.AluOpType
AXX = mybir.AxisListType.X
F32 = mybir.dt.float32
F16 = mybir.dt.float16

P = 128
D = 1024
DC = D // P
SEQ = 256
BOTH = 2 * SEQ
FF = 2816
FC = FF // P
N_MOD = 9
NEG = -1.0e30
EPS = 1e-6
GRID_W = 64
WIN_C = 16
NA_HEADS = 8
HY_W = 512
REL_BUCKETS = 32
N_HEADS_2 = 16
N_HEADS_A = 12
RET_HEADS = 4
KC_MAX = FC // 2
W_SCALE = 64.0


def shape_constants():
    f = np.float32
    eye = np.eye(P, dtype=f)
    rot = np.zeros((P, P), f)
    for i in range(64):
        rot[64 + i, i] = -1.0
        rot[i, 64 + i] = 1.0
    strip = np.zeros((P, 2 * P), f)
    strip[:, 96:128] = 1.0
    for half in range(2):
        strip[64 * half:64 * half + 64, 224 + 14 + half] = 1.0
    spread = [np.zeros((P, P), f) for _ in range(4)]
    for j in range(4):
        spread[j][32 * j] = 1.0
    mats = np.stack([eye, np.ones((P, P), f), rot, eye[::-1], np.full((P, P), D * EPS / P, f),
                     strip[:, :P], strip[:, P:], *spread], 1)

    head = np.arange(16)[:, None, None]
    head_spread = (head == 2 * np.arange(8)[:, None] + np.arange(P) // 64).astype(f)

    n = 2 * SEQ
    t = np.arange(SEQ)
    ang = 2.0 * np.pi * ((t[:, None] * t[None, :]) % n) / n
    cos, sin = np.cos(ang), np.sin(ang)
    nyq = (-1.0) ** t
    cos_n, sin_n = cos.copy(), sin.copy()
    cos_n[:, 0] = nyq
    sin_n[:, 0] = nyq
    fwd = np.stack([cos, cos_n, sin, sin_n], 0).reshape(4, 2, P, SEQ).transpose(2, 0, 1, 3)
    icos, isin = 2.0 * cos.T / n, 2.0 * sin.T / n
    icos[0] = 1.0 / n
    isin[0] = nyq / n
    inv = np.stack([icos, isin], 0).reshape(2, 2, P, SEQ).transpose(2, 0, 1, 3)

    pos = np.linspace(0.0, 1.0, SEQ, dtype=f)[:, None]
    w = f(2.0 * math.pi) * np.arange(SEQ, dtype=f)[:, None] / f(SEQ)
    bands = np.linspace(1e-4, 7, 8, dtype=f)
    emb = np.concatenate([pos, np.cos(bands * w), -np.sin(bands * w)], -1).astype(f)
    deltas = np.linspace(math.log(1e-2) / 1.5, math.log(1e-2) / 0.3, HY_W, dtype=f)
    window = np.exp(-pos * np.abs(deltas)).astype(f).reshape(2, P, HY_W).transpose(1, 0, 2)

    col = np.arange(GRID_W)
    start = np.clip(col - WIN_C // 2, 0, GRID_W - WIN_C)
    seen = (col[None] >= start[:, None]) & (col[None] < start[:, None] + WIN_C)
    seen = np.tile(seen, (2, SEQ // GRID_W))[::-1].astype(f)
    na_mask = np.stack([seen, (1.0 - seen) * f(NEG)], 1)

    dist = np.arange(SEQ - 1, -1, -1)
    large = 16 + (np.log(np.maximum(dist, 1).astype(f) / f(16)) / f(math.log(2048 / 16)) * f(16)).astype(np.int32)
    bucket = np.where(dist < 16, dist, np.minimum(large, REL_BUCKETS - 1))
    onehot = np.zeros((REL_BUCKETS, BOTH), f)
    onehot[bucket, np.arange(SEQ)] = 1.0
    count = (dist <= 128).astype(f) + (dist % 4 == 0) + (dist % 16 == 0)
    rel_mask = np.zeros((N_HEADS_2, BOTH), f)
    rel_mask[:, SEQ:] = NEG
    rel_mask[:N_HEADS_A, :SEQ] = np.where(count > 0, np.log(np.maximum(count, 1)), NEG)

    inv_f = f(10000.0) ** (-np.arange(64, dtype=f) / f(64))
    ang_r = (t // GRID_W).astype(f)[:, None] * inv_f
    ang_c = (t % GRID_W).astype(f)[:, None] * inv_f
    rope = np.stack([np.stack([np.tile(fn(a).T, (2, 1)) for fn in (np.cos, np.sin)], 0) for a in (ang_r, ang_c)], 0)
    rope = rope.transpose(2, 0, 1, 3)

    j, i = np.arange(SEQ)[:, None], np.arange(SEQ)[None]
    ret = np.stack([np.abs(i - j), i >= j, j >= i, i + SEQ - j, SEQ - i + j], 0)
    ret = ret.reshape(5, 2, P, SEQ).transpose(2, 0, 1, 3)
    return {n: np.ascontiguousarray(a, dtype=f) for n, a in dict(
        k_mats=mats, k_head_spread=head_spread, k_fwd=fwd, k_inv=inv, k_emb=emb.T, k_window=window, k_na_mask=na_mask,
        k_onehot=onehot, k_rel_mask=rel_mask, k_rope=rope, k_ret=ret).items()}


def program(nc, io, out):
    ctx = ExitStack()
    with ctx:
        def sb(name, shape, dt=F32):
            return ctx.enter_context(nc.sbuf_tensor(name, shape, dt))

        def sem(name):
            return ctx.enter_context(nc.semaphore(name))

        X = sb("X", [P, DC, BOTH])
        XH = sb("XH", [P, DC, BOTH], F16)
        XL = sb("XL", [P, DC, BOTH], F16)
        W32 = sb("W32", [P, 2, 2, KC_MAX, P])
        WH = sb("WH", [P, 2, 2, KC_MAX, P], F16)
        WL = sb("WL", [P, 2, 2, KC_MAX, P], F16)
        mats = sb("mats", [P, 11, P])
        prow = sb("prow", [P, 3, P])
        pcol = sb("pcol", [P, 3 * P])
        silu_c = sb("silu_c", [P, DC, 2])
        silu_s = sb("silu_s", [P, DC, 4], F16)
        modT = sb("modT", [P, 2 * N_MOD * DC, 2])
        norm_a = sb("norm_a", [P, 6, DC, 2])
        lg = sb("lg", [P, 2 * RET_HEADS])
        lgt = sb("lgt", [P, 8, 2 * RET_HEADS])
        inv = sb("inv", [P, SEQ])
        root = sb("root", [P, SEQ])
        stats = sb("stats", [P, 3, 80])
        onorm = sb("onorm", [P, 12])
        relb = sb("relb", [REL_BUCKETS, N_HEADS_2])
        warm = sb("warm", [P, 2])
        relvec = sb("relvec", [N_HEADS_2, BOTH])
        arena = sb("arena", [P, 29184])
        PS = ctx.enter_context(nc.psum_tensor("PS", [P, 8, 512], F32))
        rel_dram = nc.dram_tensor("rel_scratch", (N_HEADS_2, BOTH), F32, kind="Internal").ap()

        def area(off, *shape, dt=F32):
            n = int(np.prod(shape)) // (2 if dt is F16 else 1)
            a = arena[:, off:off + n]
            if dt is not F32:
                a = a.bitcast(dt)
            if len(shape) == 2:
                return a.rearrange("p (a b) -> p a b", a=shape[0])
            if len(shape) == 3:
                return a.rearrange("p (a b c) -> p a b c", a=shape[0], b=shape[1])
            return a

        eye, ones, rot, flip, eps_mat = (mats[:, n, :] for n in range(5))
        strip = mats[:, 5:7, :].rearrange("p a b -> p (a b)")
        gather = [strip[:, 96 - 32 * j:96 - 32 * j + P] for j in range(4)]
        spread = [mats[:, 7 + j, :] for j in range(4)]
        head_sum = [strip[:, 238 - 2 * t:254 - 2 * t] for t in range(8)]
        SQ, SQ_first, SQ_mid = area(23040, DC, BOTH), area(0, DC, BOTH), area(13312, DC, BOTH)
        GH, GL = area(0, FC, BOTH, dt=F16), area(FC * SEQ, FC, BOTH, dt=F16)
        ffn_s, ffn_g = area(2 * FC * SEQ, 2, BOTH), area(2 * FC * SEQ + 1024, 2, BOTH)
        M32 = [area(19968 + 2048 * k, 2, DC, P) for k in range(2)]
        MWH = [area(24064 + 2048 * k, 2, DC, P, dt=F16) for k in range(2)]
        MWL = [area(25088 + 2048 * k, 2, DC, P, dt=F16) for k in range(2)]
        x_tok = [a[:, :, :].rearrange("p c t -> p (c t)").bitcast(F32).rearrange("p (t d) -> p t d", t=2) for a in (XH, XL)]
        onehot, rel_mask = area(8704, BOTH), area(9216, BOTH)
        dft_filter = [area(n, 2, SEQ) for n in (19968, 20992, 21504)]
        h_window, hy_taps = area(27136, 2, HY_W), area(28160, HY_W)
        h_sum, h_dif = area(11264, 2, HY_W), area(12288, 2, HY_W)
        h_tmp, h_act = area(11264, 3, SEQ), area(12288, 2, SEQ)
        fw_out, fw, embT = area(22016, D)[0:64], area(28672, 3 * 64)[0:64], area(28864, SEQ)[0:17]
        qk1, u1, V1 = area(0, 8, BOTH), area(4096, 12, BOTH), area(10240, 4, HY_W)
        filt, na_bias = area(13312, 5, HY_W), area(15872, 16, SEQ)
        dft, idft = area(19968, 4, SEQ), area(20992, 4, SEQ)
        na_mask = area(28160, 2, SEQ)
        probs, probsT = area(23040, 3, BOTH), area(12288, 2, BOTH)
        O1 = area(25088, 4, HY_W)
        head_spread = area(12288, 8, P)[0:16]
        qk_square, head_inv, head_root = area(23040, 8, BOTH), area(22016, BOTH)[0:16], area(22528, BOTH)[0:16]
        hy_zt, hy_z, hy_x0 = (u1[:, n:n + 4, :] for n in (0, 4, 8))
        hy_xv, hy_tmp = area(27136, 4, BOTH), area(5120, 2, HY_W)
        hy_spec = [[area(27136 + 512 * n, HY_W) for n in range(4)],
                   [area(n, HY_W) for n in (22016, 22528, 4096, 4608)]]
        qr, kr, gr, Vr = area(0, 8, SEQ), area(2048, 8, BOTH), area(6144, 16, SEQ), area(10240, 4, 2 * D)
        decay, ret_k, rope = area(18432, 16, SEQ), area(22528, 5, BOTH), area(25088, 4, SEQ)
        ret_p, rope_t, ret_e = area(26112, 8, SEQ), area(28160, 4, SEQ), area(26112, 4, BOTH)
        ret_y, ret_sq = area(22528, 8, SEQ), area(25088, 4, SEQ)
        qk2, V2, rel_bias = area(0, 16, SEQ), area(4096, 2, D), area(13312, 16, 384)
        mem_tok = area(19840, 2, D)
        qkc, Vc, memX = area(0, 16, SEQ), area(4096, 2, D), area(6144, DC, SEQ)
        MH, ML = area(8192, DC, SEQ, dt=F16), area(9216, DC, SEQ, dt=F16)
        SQM = area(10240, DC, SEQ)
        O2, O2n = area(25088, 2, D), area(27136, 2, D)
        out_tok = area(19840, 2, D)
        ZH, ZL = ([area(18432 + SEQ * (4 * (n // 4) + 2 * part) + P * (n % 4), SEQ, dt=F16) for n in range(16)] for part in range(2))

        loaded = [[sem(f"loaded_{k}{t}") for t in range(2)] for k in range(2)]
        mod_loaded = [[sem(f"mod_loaded_{k}{t}") for t in range(2)] for k in range(2)]
        mod_hi, mod_lo = sem("mod_hi"), sem("mod_lo")
        mod_used, mod_drained = sem("mod_used"), sem("mod_drained")
        hi_ready = sem("hi_ready")
        lo_ready = sem("lo_ready")
        block_used = sem("block_used")
        units_drained = sem("units_drained")
        silu_done, gh_done, gl_done = sem("silu_done"), sem("gh_done"), sem("gl_done")
        sq_ready, ms_ready, inv_ready, root_ready, rstd_ready = (sem(n) for n in ("sq_ready", "ms_ready", "inv_ready", "root_ready", "rstd_ready"))
        added_up = sem("added_up")
        early_used, early_added = sem("early_used"), sem("early_added")
        h_ready, xh_ready, xl_ready = sem("h_ready"), sem("xh_ready"), sem("xl_ready")
        dve_chain, pool_chain = sem("dve_chain"), sem("pool_chain")
        mats_loaded, rows_clear, rows_loaded, short_loaded, x_loaded = (
            sem(n) for n in ("mats_loaded", "rows_clear", "rows_loaded", "short_loaded", "x_loaded"))
        rows_turned, pcol_ready, x_turned, x_ready = sem("rows_turned"), sem("pcol_ready"), sem("x_turned"), sem("x_ready")
        silu_c_ready, silu_hi, silu_s_ready = sem("silu_c_ready"), sem("silu_hi"), sem("silu_s_ready")
        dft_back = sem("dft_back")
        lg_loaded, lg_abs, lg_exp, lg_u, lg_ln, lg_ready = (sem(n) for n in ("lg_loaded", "lg_abs", "lg_exp", "lg_u", "lg_ln", "lg_ready"))
        filt_loaded, filt_mm, filt_arg, filt_sin, filt_sd, filt_k, filt_ready = (
            sem(n) for n in ("filt_loaded", "filt_mm", "filt_arg", "filt_sin", "filt_sd", "filt_k", "filt_ready"))
        rel_loaded, rel_mm, rel_vec, rel_stored, rel_back = (sem(n) for n in ("rel_loaded", "rel_mm", "rel_vec", "rel_stored", "rel_back"))
        nab_loaded, nab_ready = sem("nab_loaded"), sem("nab_ready")
        qk_sq, qk_ms, qk_inv, qk_root, qk_rstd, qk_ready = (sem(n) for n in ("qk_sq", "qk_ms", "qk_inv", "qk_root", "qk_rstd", "qk_ready"))
        scores_ready, max_ready, probs_ready = (sem(n) for n in ("scores_ready", "max_ready", "probs_ready"))
        turned_ready, turned_copied, out_ready, out_done, denoms = (
            sem(n) for n in ("turned_ready", "turned_copied", "out_ready", "out_done", "denoms"))
        ot_turned, ot_hi, ot_lo = sem("ot_turned"), sem("ot_hi"), sem("ot_lo")
        conv_mid, conv_ready, z_ready = sem("conv_mid"), sem("conv_ready"), sem("z_ready")
        zt_turned, zt_copied, spec_mm, spec_copied, y_ready, heads_back = (
            sem(n) for n in ("zt_turned", "zt_copied", "spec_mm", "spec_copied", "y_ready", "heads_back"))
        inv_mm, hy_out, hy_hi, hy_lo = sem("inv_mm"), sem("hy_out"), sem("hy_hi"), sem("hy_lo")
        ret_loaded, dec_exp, dec_used, dec_ready = sem("ret_loaded"), sem("dec_exp"), sem("dec_used"), sem("dec_ready")
        rope_mm, rope_cos, rope_ready = sem("rope_mm"), sem("rope_cos"), sem("rope_ready")
        rs_ready, rp_ready, ry_ready, ryc_ready = sem("rs_ready"), sem("rp_ready"), sem("ry_ready"), sem("ryc_ready")
        rm_ready, rc_ready, rq_ready, rv_ready, ri_ready, rr_ready, rn_ready = (
            sem(n) for n in ("rm_ready", "rc_ready", "rq_ready", "rv_ready", "ri_ready", "rr_ready", "rn_ready"))
        rz_ready, zh_ready, zl_ready = sem("rz_ready"), sem("zh_ready"), sem("zl_ready")
        on_sq, on_inv, on_rstd, on_ready = sem("on_sq"), sem("on_inv"), sem("on_rstd"), sem("on_ready")
        mem_loaded, mem_turned, mem_ready = sem("mem_loaded"), sem("mem_turned"), sem("mem_ready")
        fin_turned, fin_copied, stored = sem("fin_turned"), sem("fin_copied"), sem("stored")

        ROWS = [("b_mod", 0, 0, 72), ("norm_gain", None, 72, 48), ("c", None, 120, 8),
                ("b_mod", 1, 128, 72), ("hy_conv_w", None, 200, 36), ("hy_conv_b", None, 236, 12), ("hy_bias", None, 248, 4),
                ("c_ctx", None, 256, 8), ("g_ffn1_2", None, 264, 8), ("g_mix_2", None, 272, 8), ("g_out_a_2", None, 280, 6),
                ("g_out_b_2", None, 286, 2), ("g_cross_2", None, 288, 8), ("g_mem_2", None, 296, 8),
                ("g_ffn2_2", None, 304, 8), ("g_final_2", None, 312, 8)]
        SHORT = [("na_q_gain", 320, 2), ("na_k_gain", 321, 2), ("hy_fb1", 322, 1), ("hy_fb2", 323, 1),
                 ("hy_fb3", 324, 1), ("hy_freq", 325, 1)]
        COL = {(n, i): at for n, i, at, _ in ROWS} | {(n, None): at for n, at, _ in SHORT}

        def col(name, c=0, rows=P):
            at = COL[(name, None)] + c
            return pcol[0:rows, at:at + 1]

        def mod_col(layer, m, c, s):
            return modT[:, (layer * N_MOD + m) * DC + c, s:s + 1]

        def load_rows(engine, rows):
            for name, index, at, n in rows:
                src = flat(io[name] if index is None else io[name][index]).rearrange("(r p) -> r p", p=P)
                engine.dma_start(prow[at % P:at % P + n, at // P, :], src).then_inc(rows_loaded, 16)

        def flat(ap):
            n = len(ap.shape)
            return ap.rearrange({1: "a -> a", 2: "a b -> (a b)", 3: "a b c -> (a b c)"}[n])

        GEMMS = []

        def gemm(name, kind, w, kc, blocks, T, cols, rhs, parts=1, tok=False, dest=None, scale=1.0, gate=None, ffn=None, need=(), need_2=None, norm=None):
            g = dict(name=name, kind=kind, w=w, kc=kc, blocks=blocks, T=T, cols=cols, rhs=rhs, parts=parts, tok=tok,
                     dest=dest, scale=scale, gate=gate, ffn=ffn, units=blocks // parts, need=list(need), need_2=need_2, norm=norm, mods=0, m0=0, packed=name == "ret_g")
            last = GEMMS[-1] if GEMMS else None
            g["w0"] = last["w0"] + last["blocks"] if last else 0
            g["u0"] = last["u0"] + last["units"] if last else 0
            assert blocks % (2 * parts) == 0
            if kind == "resid":
                g["r"] = sum(x["kind"] == "resid" for x in GEMMS)
                g["then"] = (1, 2, 3, 4, 5, 6, 7, 9, 10, 11)[g["r"]]
                g["order"] = [(u, kp) for v in (0, 2) for kp in range(parts) for u in (v, v + 1)]
                g["done"] = [g["order"].index((u, parts - 1)) for u in range(4)]
                assert g["units"] == 4
            GEMMS.append(g)
            return g

        def x_rhs(kp, c, T, kc):
            return XH[:, c, 0:T], XL[:, c, 0:T]

        def z_rhs(kp, c, T, kc):
            return ZH[kp * kc + c], ZL[kp * kc + c]

        def g_rhs(kp, c, T, kc):
            return GH[:, kp * kc + c, 0:T], GL[:, kp * kc + c, 0:T]

        def m_rhs(kp, c, T, kc):
            return MH[:, c, 0:T], ML[:, c, 0:T]

        ffns = []
        MEM_NORM = 8

        def ffn(name, w_in, w_out, T, gate, norm):
            f = len(ffns)
            ffns.append(name)
            gemm(name + "_in", "ffn", w_in, DC, FC, T, None, x_rhs, ffn=f, norm=norm)
            return gemm(name + "_out", "resid", w_out, KC_MAX, 8, T, 256, g_rhs, parts=2, gate=gate, need=[(gl_done, FC * f + KC_MAX)], need_2=(gl_done, FC * f + FC))

        def gates(layer, m):
            return lambda c, s: mod_col(layer, m, c, s)

        w = io
        G = {}
        G["f0a"] = ffn("ffn_0a", w["ffn_a_in"][0], w["ffn_a_out"][0], BOTH, gates(0, 2), 0)
        G["u1"] = gemm("even_u", "store", w["even_in"][0][:, 1536:], DC, 6, BOTH, 256, x_rhs, dest=u1, norm=1)
        G["qk1"] = gemm("even_qk", "store", w["even_in"][0], DC, 4, BOTH, 256, x_rhs, dest=qk1)
        G["v1"] = gemm("even_v", "store", w["even_in"][0][:, 1024:], DC, 2, BOTH, 256, x_rhs, tok=True, dest=V1)
        G["o1"] = gemm("even_out", "resid", w["even_out"][0], DC, 4, BOTH, 256, x_rhs, gate=gates(0, 5),
                       need=[(ot_lo, 4), (hy_lo, 4)])
        G["f0b"] = ffn("ffn_0b", w["ffn_b_in"][0], w["ffn_b_out"][0], BOTH, gates(0, 8), 2)
        G["f1a"] = ffn("ffn_1a", w["ffn_a_in"][1], w["ffn_a_out"][1], BOTH, gates(1, 2), 3)
        G["qr"] = gemm("ret_q", "store", w["ret_in"][0], DC, 4, SEQ, 256, x_rhs, dest=qr, norm=4)
        G["kr"] = gemm("ret_k", "store", w["ret_in"][0][:, 1024:], DC, 4, BOTH, 256, x_rhs, dest=kr)
        G["vr"] = gemm("ret_v", "store", w["ret_in"][0][:, 2048:], DC, 8, BOTH, 256, x_rhs, tok=True, dest=Vr)
        G["gr"] = gemm("ret_g", "store", w["ret_in"][0][:, 4096:], DC, 8, SEQ, 256, x_rhs, dest=gr)
        G["or"] = gemm("ret_out", "resid", w["ret_out"][0], DC, 8, SEQ, 256, z_rhs, parts=2, gate=gates(1, 5),
                       need=[(zl_ready, 8)], need_2=(zl_ready, 16))
        G["f1b"] = ffn("ffn_1b", w["ffn_b_in"][1], w["ffn_b_out"][1], SEQ, gates(1, 8), 5)
        G["f2a"] = ffn("ffn_2a", w["w_ffn1_gu_2"][0], w["w_ffn1_down_2"][0], SEQ, 0.5, 6)
        wi = w["w_in_2"][0]
        G["q2"] = gemm("mix_q", "store", wi, DC, 4, SEQ, [0, 256, 512, 2304], x_rhs, dest=qk2[:, 0:8], scale=0.125, norm=7)
        G["k2"] = gemm("mix_k", "store", wi, DC, 4, SEQ, [768, 1024, 1280, 2560], x_rhs, dest=qk2[:, 8:16])
        G["v2"] = gemm("mix_v", "store", wi, DC, 4, SEQ, [1536, 1792, 2048, 2816], x_rhs, tok=True, dest=V2)
        G["o2"] = gemm("mix_out", "resid", w["w_out_2"][0], DC, 4, SEQ, 256, x_rhs, gate=1.0, need=[(ot_lo, 4 + 8)])
        G["qc"] = gemm("cross_q", "store", w["w_cq_2"][0], DC, 4, SEQ, 256, x_rhs, dest=qkc[:, 0:8], scale=0.0625, norm=9)
        G["kc"] = gemm("cross_k", "store", w["w_ckv_2"][0], DC, 4, SEQ, 256, m_rhs, dest=qkc[:, 8:16], norm=MEM_NORM)
        G["vc"] = gemm("cross_v", "store", w["w_ckv_2"][0][:, 1024:], DC, 4, SEQ, 256, m_rhs, tok=True, dest=Vc)
        G["oc"] = gemm("cross_out", "resid", w["w_co_2"][0], DC, 4, SEQ, 256, x_rhs, gate=1.0, need=[(ot_lo, 4 + 8 + 8)])
        G["f2b"] = ffn("ffn_2b", w["w_ffn2_gu_2"][0], w["w_ffn2_down_2"][0], SEQ, 0.5, 10)
        MOD_BLOCKS = N_MOD * DC
        MOD_FIRST = 10
        m = MOD_FIRST
        for name, pairs in (("ffn_0a_in", FC // 2), ("ffn_0b_in", FC // 2), ("ffn_1a_in", 9)):
            g = next(x for x in GEMMS if x["name"] == name)
            g["mods"], g["m0"] = pairs, m
            m += 2 * pairs
        assert m == MOD_BLOCKS

        def drained(g):
            return g["u0"] + g["units"]

        def segs(T):
            return [(s, slice(s * SEQ, (s + 1) * SEQ)) for s in range(T // SEQ)]

        UNITS = []

        def na_units():
            for part in range(2):
                for h in range(NA_HEADS):
                    rows = slice(64 * (h % 2), 64 * (h % 2) + 64)
                    for qt in range(2):
                        q0, k0 = SEQ * part + P * qt, SEQ * part
                        UNITS.append(dict(
                            q=[qk1[rows, h // 2, q0:q0 + P]], k=[qk1[rows, 4 + h // 2, k0:BOTH]], nk=BOTH - k0,
                            bias=na_bias[:, 2 * h + qt, :] if part == 0 else None,
                            v=[V1[:, k0 // P + t, 64 * h:64 * h + 64] for t in range((BOTH - k0) // P)],
                            dst=O1[:, 2 * part + qt, 64 * h:64 * h + 64]))

        def rel_units():
            for h in range(N_HEADS_2):
                rows = slice(64 * (h % 2), 64 * (h % 2) + 64)
                for qt in range(2):
                    nk, at = P * (qt + 1), P * qt
                    UNITS.append(dict(
                        q=[qk2[rows, h // 2, P * qt:P * qt + P]], k=[qk2[rows, 8 + h // 2, 0:nk]], nk=nk,
                        bias=rel_bias[:, h, at:at + nk],
                        v=[V2[:, t, 64 * h:64 * h + 64] for t in range(qt + 1)], dst=O2[:, qt, 64 * h:64 * h + 64]))

        def cross_units():
            for h in range(4):
                for qt in range(2):
                    UNITS.append(dict(
                        q=[qkc[:, 2 * h + c, P * qt:P * qt + P] for c in range(2)], k=[qkc[:, 8 + 2 * h + c, :] for c in range(2)],
                        nk=SEQ, bias=None, v=[Vc[:, t, SEQ * h:SEQ * h + SEQ] for t in range(2)],
                        dst=O2[:, qt, SEQ * h:SEQ * h + SEQ]))

        na_units()
        NA = (0, len(UNITS))
        rel_units()
        REL = (NA[1], len(UNITS))
        cross_units()
        CROSS = (REL[1], len(UNITS))

        def conv_tile(n):
            if n < 8:
                c = n // 2
                return 4 + c + 4 * (n % 2), hy_xv[:, 2 * (c % 2) + n % 2, :]
            return n - 8, hy_x0[:, n - 8, :]

        def drained_chunk(g):
            return lambda c: (early_added, g["r"] + 1) if c == DC - 2 else (units_drained, g["u0"] + c // 2 + 1)

        def mod_norm(layer, j, T, wait):
            return dict(src=X, T=T, a=lambda c, s: norm_a[:, 3 * layer + j, c, s:s + 1],
                        b=lambda c, s: mod_col(layer, 3 * j, c, s), h=XH, l=XL, wait=wait,
                        sq={(0, 0): SQ_first, (0, 1): SQ, (1, 2): SQ}.get((layer, j), SQ_mid))

        def gain_norm(name, wait, src=X, h=XH, l=XL, sq=SQ):
            return dict(src=src, T=SEQ, a=lambda c, s: col(name, c), b=None, h=h, l=l, wait=wait, sq=sq)

        NORMS = [mod_norm(0, 0, BOTH, lambda c: (x_ready, c + 1)), mod_norm(0, 1, BOTH, drained_chunk(G["f0a"])),
                 mod_norm(0, 2, BOTH, drained_chunk(G["o1"])), mod_norm(1, 0, BOTH, drained_chunk(G["f0b"])),
                 mod_norm(1, 1, BOTH, drained_chunk(G["f1a"])), mod_norm(1, 2, SEQ, drained_chunk(G["or"])),
                 gain_norm("g_ffn1_2", drained_chunk(G["f1b"])), gain_norm("g_mix_2", drained_chunk(G["f2a"])),
                 gain_norm("g_mem_2", lambda c: (mem_ready, c + 1), src=memX, h=MH, l=ML, sq=SQM),
                 gain_norm("g_cross_2", drained_chunk(G["o2"])),
                 gain_norm("g_ffn2_2", drained_chunk(G["oc"])), gain_norm("g_final_2", drained_chunk(G["f2b"]), h=None)]
        SUM_BANKS = [(2, 3)] * (RET_HEADS - 1) + [(5, 4)]
        BANK_N = 4
        for n, N in enumerate(g["then"] for g in GEMMS if g["kind"] == "resid"):
            NORMS[N]["added"] = n + 1
        H0 = [0]
        for N in NORMS:
            H0.append(H0[-1] + DC * (N["T"] // SEQ))
        G["kr"]["need"].append((xl_ready, H0[G["qr"]["norm"] + 1]))

        block = ctx.enter_context(nc.Block())

        @block.sync
        def _(sp):
            sp.dma_start(x_tok[0], io["x"][0].rearrange("(t p) d -> p t d", p=P)).then_inc(x_loaded, 16)
            sp.dma_start(x_tok[1], io["ctx"][0].rearrange("(t p) d -> p t d", p=P)).then_inc(x_loaded, 16)
            sp.wait_ge(rows_clear, 1)
            load_rows(sp, ROWS[:8])

            mod_w = io["w_mod"].rearrange("l (c p) n -> p l c n", p=P)

            def mod_load(m0, i, k):
                layer, first = divmod(m0, MOD_BLOCKS // 2)
                for t in range(2):
                    if not (isinstance(i, int) and m0 + 2 * i < 2):
                        sp.wait_ge(mod_lo, 2 * (m0 + k - 2) + t + 1 + 4 * i)
                    src = mod_w[:, layer, :, bass.ds(256 * (first + k) + P * t + 512 * i, P)]
                    sp.dma_start(M32[k][:, t], src).then_inc(mod_loaded[k][t], 16)

            def load(g, wv, k, t, col0, kp):
                src = wv[:, kp * g["kc"]:(kp + 1) * g["kc"], bass.ds(col0, P)]
                sp.dma_start(W32[:, k, t, 0:g["kc"], :], src).then_inc(loaded[k][t], 16)

            for g in GEMMS:
                wv = g["w"].rearrange("(c p) n -> p c n", p=P)

                def pair(i, slot_free, g=g, wv=wv):
                    for k in range(2):
                        for t in range(2):
                            slot_free(k, t)
                            if g["kind"] == "ffn":
                                load(g, wv, k, t, (2 * i + k) * P + t * FF, 0)
                            elif g["cols"] == 256:
                                load(g, wv, k, t, 512 * i + 256 * k + P * t, 0)
                            else:
                                load(g, wv, k, t, g["cols"][2 * i + k] + P * t, 0)

                def split_before(i, w0=g["w0"]):
                    return lambda k, t: sp.wait_ge(lo_ready, 2 * (w0 - 2 + k) + t + 1 + 4 * i)

                n, mods = g["blocks"] // 2, g["mods"]
                begin = 0
                if g["w0"] == 0:
                    for i in range(2):
                        for k in range(2):
                            mod_load(0, i, k)
                    with sp.Fori(2, MOD_FIRST // 2) as i:
                        for k in range(2):
                            mod_load(0, i, k)
                    pair(0, lambda k, t: None)
                    for k in range(2):
                        mod_load(g["m0"], 0, k)
                    begin = 1
                if mods:
                    if g["name"] == "ffn_0b_in":
                        pair(0, split_before(0))
                        sp.wait_ge(hy_lo, 4)
                        for k in range(2):
                            mod_load(g["m0"], 0, k)
                        begin = 1
                    edge = min(max((MOD_BLOCKS // 2 - g["m0"]) // 2, 0), mods) or mods
                    for lo, hi in ((begin, edge), (edge, mods)):
                        if lo < hi:
                            with sp.Fori(lo, hi) as i:
                                pair(i, split_before(i))
                                for k in range(2):
                                    if lo == edge:
                                        mod_load(g["m0"] + 2 * edge, i - edge, k)
                                    else:
                                        mod_load(g["m0"], i, k)
                    begin = mods
                if g["parts"] == 2:
                    with sp.Fori(0, n // 2) as i:
                        for kp in range(2):
                            for k in range(2):
                                for t in range(2):
                                    split_before(2 * i + kp)(k, t)
                                    load(g, wv, k, t, 512 * i + 256 * k + P * t, kp)
                elif isinstance(g["cols"], list):
                    for i in range(n):
                        pair(i, split_before(i))
                elif begin < n:
                    with sp.Fori(begin, n) as i:
                        pair(i, split_before(i))

            sp.wait_ge(stored, 32)

        @block.tensor
        def _(pe):
            mm, turn = pe.matmul, pe.transpose

            def pe_mod(m, k):
                for t in range(2):
                    pe.wait_ge(mod_lo, 2 * m + t + 1)
                    if t == 0 and not (isinstance(m, int) and m < 2):
                        pe.wait_ge(mod_drained, m - 1)
                    dst = PS[:, 6 + k, 4 * t:4 * t + 4]
                    for c in range(DC):
                        mm(dst, MWH[k][:, t, c], silu_s[:, c, :], start=(c == 0), stop=False, skip_group_check=True)
                        ins = mm(dst[:, 0:2], MWL[k][:, t, c], silu_s[:, c, 0:2], start=False, stop=(c == DC - 1),
                                 skip_group_check=True)
                ins.then_inc(mod_used, 1)

            def pe_sums(n, chunks):
                N = NORMS[n]
                T = N["T"]
                q = T // 4
                mm(PS[:, BANK_N, 0:q], ones, eps_mat[:, 0:q], start=True, stop=False, skip_group_check=True)
                for c in chunks:
                    if c == 0 and len(chunks) == 2:
                        pe.wait_ge(added_up, (DC - 2) * N["added"])
                    else:
                        pe.wait_ge(sq_ready, DC * n + c + 1)
                    for j in range(4):
                        ins = mm(PS[:, BANK_N, 0:q], gather[j], N["sq"][:, c, q * j:q * j + q], start=False,
                                 stop=(c == DC - 1 and j == 3), skip_group_check=True)
                ins.then_inc(ms_ready, 1)

            def pe_spread(n):
                q = NORMS[n]["T"] // 4
                pe.wait_ge(root_ready, n + 1)
                for j in range(4):
                    ins = mm(PS[:, BANK_N + 1, q * j:q * j + q], spread[j], root[:, 0:q], start=True, stop=True, skip_group_check=True)
                ins.then_inc(rstd_ready, 1)

            def pe_norm(n):
                pe_sums(n, range(DC))
                pe_spread(n)

            def pe_gemm(g, between={}):
                kc, T = g["kc"], g["T"]

                def three(dst, t, k, kp, c):
                    xh, xl = g["rhs"](kp, c, T, kc)
                    wh, wl = WH[:, k, t, c, :], WL[:, k, t, c, :]
                    mm(dst, wh, xh, start=(kp == 0 and c == 0), stop=False, skip_group_check=True)
                    mm(dst, wh, xl, start=False, stop=False, skip_group_check=True)
                    return mm(dst, wl, xh, start=False, stop=(kp == g["parts"] - 1 and c == kc - 1), skip_group_check=True)

                def one(k, kp, pair, w, u, first=False, early=False):
                    if kp == 0 and not (isinstance(u, int) and u < 2):
                        pe.wait_ge(units_drained, u - 1)
                    if kp == 1:
                        pe.wait_ge(*g["need_2"])
                    if g["tok"]:
                        pe.wait_ge(lo_ready, 2 * w + 2)
                        for tt in range(T // P):
                            dst = PS[:, 2 * pair + tt // 2, 256 * (tt % 2):256 * (tt % 2) + 256].rearrange("p (a b) -> p a b", a=2)
                            for c in range(kc):
                                xh, xl = g["rhs"](kp, c, T, kc)
                                xh, xl = xh[:, P * tt:P * tt + P], xl[:, P * tt:P * tt + P]
                                wh, wl = WH[:, k, :, c, :], WL[:, k, :, c, :]
                                mm(dst, xh, wh, start=(c == 0), stop=False)
                                mm(dst, xh, wl, start=False, stop=False)
                                ins = mm(dst, xl, wh, start=False, stop=(c == kc - 1))
                    elif first and g["norm"] is not None:
                        pe.wait_ge(lo_ready, 2 * w + 2)
                        for c in range(kc):
                            pe.wait_ge(xl_ready, H0[g["norm"]] + c * (NORMS[g["norm"]]["T"] // SEQ) + T // SEQ)
                            for t in range(2):
                                ins = three(PS[:, 2 * pair + t, 0:T], t, k, kp, c)
                    else:
                        for t in range(2):
                            pe.wait_ge(lo_ready, 2 * w + t + 1)
                            for c in range(kc):
                                dst = PS[:, pair, SEQ * t:SEQ * t + SEQ] if g["packed"] else PS[:, 2 * pair + t, 0:T]
                                ins = three(dst, t, k, kp, c)
                            if early and t == 0:
                                ins.then_inc(early_used, 1)
                    ins.then_inc(block_used, 1)

                def turn_of(i, mods, first=False):
                    for b in range(2 * g["parts"]):
                        pair, kp = b // g["parts"], b % g["parts"]
                        one(b % 2, kp, pair, g["w0"] + b + 2 * g["parts"] * i, g["u0"] + pair + 2 * i, first and b == 0)
                        if mods:
                            pe_mod(g["m0"] + b + 2 * i, b)

                for s, v in g["need"]:
                    pe.wait_ge(s, v)
                if g["kind"] == "resid":
                    for b, (u, kp) in enumerate(g["order"]):
                        one(b % 2, kp, u % 2, g["w0"] + b, g["u0"] + u, early=(b == g["blocks"] - 1))
                        if b in between:
                            between[b]()
                    pe_sums(g["then"], (0, DC - 1))
                    pe_spread(g["then"])
                    return
                if between:
                    for b in range(g["blocks"]):
                        one(b % 2, 0, b % 2, g["w0"] + b, g["u0"] + b)
                        if b in between:
                            between[b]()
                    return
                n, mods, begin = g["units"] // 2, g["mods"], 0
                if g["norm"] is not None:
                    turn_of(0, mods > 0, True)
                    begin = 1
                if mods > begin:
                    with pe.Fori(begin, mods) as i:
                        turn_of(i, True)
                    begin = mods
                if begin < n:
                    with pe.Fori(begin, n) as i:
                        turn_of(i, False)

            def pe_attend(span, values_stored):
                lo, hi = span
                for u in range(lo, hi + 3):
                    if u < hi:
                        U = UNITS[u]
                        s = PS[:, 4 + u % 3, 0:U["nk"]]
                        if u - lo >= 3:
                            pe.wait_ge(probs_ready, u - 2)
                        for c, (q, k) in enumerate(zip(U["q"], U["k"])):
                            ins = mm(s, q, k, start=(c == 0), stop=(c == len(U["q"]) - 1 and U["bias"] is None), skip_group_check=True)
                        if U["bias"] is not None:
                            nb = U["bias"].shape[-1]
                            ins = mm(s[:, 0:nb], flip, U["bias"],
                                     start=False, stop=True, skip_group_check=True)
                        ins.then_inc(scores_ready, 1)
                    v = u - 2
                    if lo <= v < hi:
                        pe.wait_ge(probs_ready, v + 1)
                        if v == lo:
                            pe.wait_ge(units_drained, values_stored)
                        if v - lo >= 2:
                            pe.wait_ge(turned_copied, v - 1)
                        for t in range(UNITS[v]["nk"] // P):
                            ins = turn(PS[:, 2 + v % 2, P * t:P * t + P], probs[:, v % 3, P * t:P * t + P], eye)
                        ins.then_inc(turned_ready, 1)
                    v = u - 3
                    if v >= lo:
                        U = UNITS[v]
                        pe.wait_ge(turned_copied, v + 1)
                        if v - lo >= 2:
                            pe.wait_ge(out_done, v - 1)
                        dv = U["dst"].shape[-1]
                        for t, values in enumerate(U["v"]):
                            ins = mm(PS[:, 7 * (v % 2), 0:dv], probsT[:, v % 2, P * t:P * t + P], values,
                                     start=(t == 0), stop=(t == len(U["v"]) - 1))
                        ins.then_inc(out_ready, 1)

            def pe_turn_out(O, tiles, chunks, base):
                for c in chunks:
                    if c >= 4:
                        pe.wait_ge(ot_lo, base + c - 3)
                    for t in range(tiles):
                        ins = turn(PS[:, 4 + c % 4, P * t:P * t + P], O[:, t, P * c:P * c + P], eye)
                    ins.then_inc(ot_turned, 1)

            pe.wait_ge(mats_loaded, 16)
            pe.wait_ge(x_loaded, 32)
            for c in range(DC):
                if c >= 4:
                    pe.wait_ge(x_ready, c - 3)
                for t in range(4):
                    ins = turn(PS[:, c % 4, P * t:P * t + P], x_tok[t // 2][:, t % 2, P * c:P * c + P], eye)
                ins.then_inc(x_turned, 1)
            pe.wait_ge(rows_loaded, 16 * len(ROWS))
            pe.wait_ge(short_loaded, 16 * sum(n for _, _, n in SHORT))
            for n in range(3):
                ins = turn(PS[:, 6, P * n:P * n + P], prow[:, n, :], eye)
            ins.then_inc(rows_turned, 1)
            pe_norm(0)
            pe.wait_ge(silu_s_ready, 1)
            for m in range(MOD_FIRST):
                pe_mod(m, m % 2)
            pe.wait_ge(inv_ready, 1)
            pe.wait_ge(rel_loaded, 48)
            mm(PS[0:N_HEADS_2, 4, :], relb[:, :], onehot[0:REL_BUCKETS, :], start=True, stop=True).then_inc(rel_mm, 1)

            def filter_step(n):
                if n < 3:
                    if n == 0:
                        pe.wait_ge(filt_loaded, 16 * 9)
                        pe.wait_ge(rel_vec, 1)
                        ins = mm(PS[0:64, 4, 0:SEQ], fw[0:17, 0:64], embT[:, :], start=True, stop=True)
                    else:
                        pe.wait_ge(filt_sin, n)
                        ins = mm(PS[0:64, 4, 0:SEQ], fw[:, 64 * n:64 * n + 64], h_act[0:64, (n - 1) % 2, :], start=True, stop=True)
                    ins.then_inc(filt_mm, 1)
                elif n == 3:
                    pe.wait_ge(filt_sin, 3)
                    for q in range(4):
                        ins = mm(PS[:, 4 + q, :], h_act[0:64, 0, P * (q // 2):P * (q // 2) + P],
                                 fw_out[:, HY_W * (q % 2):HY_W * (q % 2) + HY_W], start=True, stop=True)
                        ins.then_inc(filt_mm, 1)
                else:
                    pe.wait_ge(filt_sd, 4)
                    for q, (m, f, h) in enumerate([(0, 0, h_sum), (0, 1, h_sum), (1, 0, h_sum), (2, 0, h_dif), (2, 1, h_dif)]):
                        if q == 4:
                            pe.wait_ge(filt_ready, 1)
                        for t in range(2):
                            ins = mm(PS[:, 4 + q % 4, :], dft_filter[m][:, t, P * f:P * f + P], h[:, t, :], start=(t == 0), stop=(t == 1))
                        ins.then_inc(filt_k, 1)

            gi = {g["name"]: g for g in GEMMS}
            pe_gemm(gi["ffn_0a_in"])
            pe_gemm(gi["ffn_0a_out"], {b: lambda b=b: filter_step(b) for b in range(5)} | {7: lambda: pe.wait_ge(filt_ready, 5)})
            pe_gemm(gi["even_u"])
            pe_gemm(gi["even_qk"])

            def turn_z():
                for t in range(4):
                    for c in range(4):
                        pe.wait_ge(z_ready, c + 1)
                        ins = turn(PS[:, 4 + t, P * c:P * c + P], hy_z[:, c, P * t:P * t + P], eye)
                    ins.then_inc(zt_turned, 1)

            def spectrum(s):
                for n in range(4):
                    if s == 1:
                        pe.wait_ge(spec_copied, n + 1)
                    for t in range(2):
                        ins = mm(PS[:, (5, 6, 7, 0)[n], :], dft[:, 2 * (n // 2) + t, P * (n % 2):P * (n % 2) + P],
                                 hy_zt[:, 2 * s + t, :], start=(t == 0), stop=(t == 1))
                    ins.then_inc(spec_mm, 1)

            pe_gemm(gi["even_v"], {0: turn_z})
            pe.wait_ge(zt_copied, 4)
            for t in range(8):
                pe.wait_ge(qk_sq, t + 1)
                ins = mm(PS[0:16, 4, :], head_sum[t], qk_square[:, t, :], start=(t == 0), stop=(t == 7))
            ins.then_inc(qk_ms, 1)
            pe.wait_ge(dft_back, 32)
            pe.wait_ge(units_drained, drained(gi["even_v"]))
            spectrum(0)
            pe.wait_ge(qk_root, 1)
            pe.wait_ge(heads_back, 16)
            for t in range(8):
                if t >= 3:
                    pe.wait_ge(qk_ready, t - 2)
                mm(PS[:, 1 + t % 3, :], head_spread[:, t, :], head_root[:, :], start=True, stop=True).then_inc(qk_rstd, 1)
            spectrum(1)
            pe.wait_ge(qk_ready, 8)
            pe.wait_ge(nab_ready, 16)
            pe.wait_ge(spec_copied, 8)
            pe_attend(NA, drained(gi["even_v"]))
            pe.wait_ge(y_ready, 4)
            pe.wait_ge(out_done, NA[1])
            for c in range(4):
                if c >= 2:
                    pe.wait_ge(hy_out, c - 1)
                for s in range(2):
                    for n in range(4):
                        ins = mm(PS[:, 2 + c % 2, SEQ * s:SEQ * s + SEQ], hy_spec[s][n][:, P * c:P * c + P], idft[:, n, :],
                                 start=(n == 0), stop=(n == 3), skip_group_check=True)
                ins.then_inc(inv_mm, 1)
                pe_turn_out(O1, 4, (c,), 0)
            pe_gemm(gi["even_out"])
            pe_gemm(gi["ffn_0b_in"])
            pe_gemm(gi["ffn_0b_out"])
            pe_gemm(gi["ffn_1a_in"])
            pe_gemm(gi["ffn_1a_out"])
            pe_gemm(gi["ret_q"])
            pe_gemm(gi["ret_k"])

            def rotary(t):
                if t in (0, 8):
                    pe.wait_ge(units_drained, drained(gi["ret_q"] if t < 8 else gi["ret_k"]))
                if t >= 2:
                    pe.wait_ge(rope_ready, t - 1)
                src = qr[:, t, :] if t < 8 else kr[:, t - 8, 0:SEQ]
                mm(PS[:, 4 + t % 2, 0:SEQ], rot, src, start=True, stop=True).then_inc(rope_mm, 1)

            def retain(h):
                for t in range(4):
                    n = 4 * h + t
                    if n >= 2:
                        pe.wait_ge(rp_ready, n - 1)
                    for c in range(2):
                        ins = mm(PS[:, 4 + t % 2, 0:SEQ], kr[:, 2 * h + c, P * t:P * t + P], qr[:, 2 * h + c, :],
                                 start=(c == 0), stop=(c == 1))
                    ins.then_inc(rs_ready, 1)
                pe.wait_ge(rp_ready, 4 * h + 4)
                if h:
                    pe.wait_ge(ryc_ready, 4 * h)
                for e in range(4):
                    for t in range(4):
                        ins = mm(PS[:, 6 + e // 2, SEQ * (e % 2):SEQ * (e % 2) + SEQ], Vr[:, t, 512 * h + P * e:512 * h + P * e + P],
                                 ret_p[:, 4 * (h % 2) + t, :], start=(t == 0), stop=(t == 3), skip_group_check=True)
                    ins.then_inc(ry_ready, 1)

            def ret_sum(h):
                for e in range(4):
                    pe.wait_ge(ryc_ready, 4 * h + e + 1)
                    ins = mm(PS[:, SUM_BANKS[h][0], 0:SEQ], ones, ret_y[:, 4 * (h % 2) + e, :], start=(e == 0), stop=(e == 3))
                ins.then_inc(rm_ready, 1)

            def ret_squares(h):
                for e in range(4):
                    pe.wait_ge(rq_ready, 4 * h + e + 1)
                    ins = mm(PS[:, SUM_BANKS[h][1], 0:SEQ], ones, ret_sq[:, e, :], start=(e == 0), stop=(e == 3))
                ins.then_inc(rv_ready, 1)

            def head_step(h):
                if h:
                    ret_sum(h - 1)
                if h < RET_HEADS:
                    retain(h)
                if h:
                    ret_squares(h - 1)

            def rotary_pair(b):
                rotary(2 * b)
                rotary(2 * b + 1)

            rotary_pair(0)
            pe_gemm(gi["ret_v"], {b: lambda b=b: rotary_pair(b + 1) for b in range(7)})
            pe.wait_ge(rope_ready, 16)
            pe.wait_ge(units_drained, drained(gi["ret_v"]))
            head_step(0)
            pe_gemm(gi["ret_g"], {2 * h + 1: lambda h=h: head_step(h + 1) for h in range(RET_HEADS)})
            pe_gemm(gi["ret_out"])
            pe_gemm(gi["ffn_1b_in"])
            pe_gemm(gi["ffn_1b_out"])
            pe_gemm(gi["ffn_2a_in"])
            pe_gemm(gi["ffn_2a_out"])
            pe_gemm(gi["mix_q"])
            pe.wait_ge(mem_loaded, 16)
            for c in range(DC):
                if c >= 2:
                    pe.wait_ge(mem_ready, c - 1)
                for t in range(2):
                    ins = turn(PS[:, 6 + c % 2, P * t:P * t + P], mem_tok[:, t, P * c:P * c + P], eye)
                ins.then_inc(mem_turned, 1)
            pe_gemm(gi["mix_k"])
            pe_sums(MEM_NORM, range(DC))
            pe_gemm(gi["mix_v"], {0: lambda: pe_spread(MEM_NORM)})
            pe.wait_ge(units_drained, drained(gi["mix_k"]))
            pe.wait_ge(h_ready, H0[MEM_NORM + 1])
            pe.wait_ge(rel_back, 32)
            pe_attend(REL, drained(gi["mix_v"]))
            pe.wait_ge(on_ready, 2)
            pe_turn_out(O2n, 2, range(6), 4)
            pe.wait_ge(on_ready, 4)
            pe_turn_out(O2n, 2, range(6, 8), 4)
            pe_gemm(gi["mix_out"])
            pe_gemm(gi["cross_q"])
            pe_gemm(gi["cross_k"])
            pe_gemm(gi["cross_v"])
            pe.wait_ge(units_drained, drained(gi["cross_k"]))
            pe_attend(CROSS, drained(gi["cross_v"]))
            pe.wait_ge(out_done, CROSS[1])
            pe_turn_out(O2, 2, range(8), 12)
            pe_gemm(gi["cross_out"])
            pe_gemm(gi["ffn_2b_in"])
            pe_gemm(gi["ffn_2b_out"])
            for c in range(DC):
                pe.wait_ge(h_ready, H0[11] + c + 1)
                for t in range(2):
                    ins = turn(PS[:, 2 * (c // 4) + t, P * (c % 4):P * (c % 4) + P], SQ[:, c, P * t:P * t + P], eye)
                    if c % 4 == 3:
                        ins.then_inc(fin_turned, 1)

        @block.scalar
        def _(act):
            def copy(dst, src, scale=1.0):
                return act.activation(dst, src, ACT.Copy, scale=scale)

            def split(g, i, k, first=False):
                if not (first and g["w0"] == 0):
                    act.wait_ge(block_used, g["w0"] + k - 1 + 2 * i)
                for t in range(2):
                    act.wait_ge(loaded[k][t], 16 * (g["w0"] // 2 + 1) + 16 * i)
                    copy(WH[:, k, t, 0:g["kc"], :], W32[:, k, t, 0:g["kc"], :], W_SCALE).then_inc(hi_ready, 1)

            def mod_split(m0, i, k, first=False):
                if not first:
                    act.wait_ge(mod_used, m0 + k - 1 + 2 * i)
                for t in range(2):
                    act.wait_ge(mod_loaded[k][t], 16 * (m0 // 2 + 1) + 16 * i)
                    copy(MWH[k][:, t], M32[k][:, t], W_SCALE).then_inc(mod_hi, 1)

            def begin(g, ks=(0, 1)):
                for k in ks:
                    split(g, 0, k, True)

            def begin_mods(g):
                if g["mods"]:
                    for k in range(2):
                        mod_split(g["m0"], 0, k)

            def act_gemm(g, after, between={}):
                n, T, u0 = g["blocks"] // 2, g["T"], g["u0"]

                def silu(i, k):
                    act.wait_ge(block_used, g["w0"] + k + 1 + 2 * i)
                    act.activation(ffn_s[:, k, 0:T], PS[:, 2 * k, 0:T], ACT.Silu, scale=1.0 / W_SCALE).then_inc(silu_done, 1)

                def hidden(i, k):
                    act.wait_ge(units_drained, u0 + k + 1 + 2 * i)
                    copy(GH[:, bass.ds(2 * i + k, 1), 0:T], ffn_g[:, k:k + 1, 0:T]).then_inc(gh_done, 1)

                is_ffn = g["kind"] == "ffn"
                if between:
                    for b in range(g["blocks"]):
                        if g["packed"]:
                            between[b]()
                        if b + 2 < g["blocks"]:
                            split(g, b // 2 + 1, b % 2)
                        else:
                            begin(after, (b % 2,))
                        if b in between and not g["packed"]:
                            between[b]()
                    return
                for lo, hi, mods in ((1, g["mods"], True), (max(g["mods"], 1), n, False)):
                    if lo < hi:
                        with act.Fori(lo, hi) as i:
                            for k in range(2):
                                if is_ffn:
                                    silu(i - 1, k)
                                split(g, i, k)
                                if is_ffn:
                                    hidden(i - 1, k)
                                if mods:
                                    mod_split(g["m0"], i, k)
                for k in range(2):
                    if is_ffn:
                        silu(n - 1, k)
                    if not is_ffn or k == 0:
                        begin(after, (k,))
                    if is_ffn:
                        hidden(n - 1, k)
                if is_ffn:
                    begin(after, (1,))

            def squares(n, chunks):
                N = NORMS[n]
                for c in chunks:
                    act.wait_ge(*N["wait"](c))
                    act.activation(N["sq"][:, c, 0:N["T"]], N["src"][:, c, 0:N["T"]], ACT.Square).then_inc(sq_ready, 1)

            def act_resid(g, after, between={}):
                n, nb, done = g["then"], g["blocks"], 0
                for b in range(2, nb):
                    split(g, b // 2, b % 2)
                    while g["done"][done] <= b - 2:
                        squares(n, (2 * done, 2 * done + 1))
                        done += 1
                    if b in between:
                        between[b]()
                act.activation(warm[:, 1:2], mats[:, 1, 0:1], ACT.Sqrt)
                while g["done"][done] <= nb - 3:
                    squares(n, (2 * done, 2 * done + 1))
                    done += 1
                if after is not None:
                    begin(after, (0,))
                squares(n, range(2 * done, DC))
                act_norm(n, after)

            def act_norm(n, after=None):
                if after is not None:
                    begin(after, (1,))
                act_root(n)
                act.activation(warm[:, 0:1], mats[:, 1, 0:1], ACT.Silu)
                act_apply(n, after)

            def act_root(n):
                T = NORMS[n]["T"]
                act.wait_ge(inv_ready, n + 1)
                act.activation(root[:, 0:T // 4], inv[:, 0:T // 4], ACT.Sqrt, scale=float(D)).then_inc(root_ready, 1)

            def act_apply(n, after=None):
                N = NORMS[n]
                T = N["T"]
                if N["h"] is not None:
                    for c in range(DC):
                        for s, tok in segs(T):
                            act.wait_ge(h_ready, H0[n] + (T // SEQ) * c + s + 1)
                            if N["b"]:
                                ins = act.activation(N["h"][:, c, tok], N["sq"][:, c, tok], ACT.Identity, bias=N["b"](c, s))
                            else:
                                ins = copy(N["h"][:, c, tok], N["sq"][:, c, tok])
                            ins.then_inc(xh_ready, 1)
                if after is not None:
                    begin_mods(after)

            def act_attend(span, between={}):
                lo, hi = span
                for u in range(lo, hi + 2):
                    if u - lo in between:
                        between[u - lo]()
                    v = u - 2
                    if v >= lo:
                        nk = UNITS[v]["nk"]
                        act.wait_ge(turned_ready, v + 1)
                        if v - lo >= 2:
                            act.wait_ge(out_ready, v - 1)
                        copy(probsT[:, v % 2, 0:nk], PS[:, 2 + v % 2, 0:nk]).then_inc(turned_copied, 1)
                    if u < hi:
                        nk = UNITS[u]["nk"]
                        act.wait_ge(max_ready, u + 1)
                        if u - lo >= 3:
                            act.wait_ge(turned_ready, u - 2)
                        act.activation(probs[:, u % 3, 0:nk], PS[:, 4 + u % 3, 0:nk], ACT.Exp, bias=stats[:, 0, u:u + 1],
                                       accum_out=stats[:, 1, u:u + 1]).then_inc(probs_ready, 1)

            def act_turn_out(chunks, T, base, gain=None):
                for c in chunks:
                    act.wait_ge(ot_turned, base + c + 1)
                    copy(XH[:, c, 0:T], PS[:, 4 + c % 4, 0:T], gain(c) if gain else 1.0).then_inc(ot_hi, 1)

            act.dma_start(mats[:, :, :], io["k_mats"]).then_inc(mats_loaded, 16)
            act.wait_ge(rows_clear, 1)
            load_rows(act, ROWS[8:])
            squares(0, range(DC))
            act.wait_ge(pcol_ready, 1)
            for s, name in enumerate(("c", "c_ctx")):
                at = COL[(name, None)]
                act.activation(silu_c[:, :, s], pcol[:, at:at + DC], ACT.Silu).then_inc(silu_c_ready, 1)
            act.wait_ge(silu_c_ready, 2)
            copy(silu_s[:, :, 0:2], silu_c[:, :, :]).then_inc(silu_hi, 1)
            for k in range(2):
                mod_split(0, 0, k, True)
            act_root(0)
            act.wait_ge(lg_abs, 1)
            act.activation(lgt[:, 1, :], lgt[:, 0, :], ACT.Exp, scale=-1.0).then_inc(lg_exp, 1)
            act.wait_ge(lg_u, 1)
            act.activation(lgt[:, 3, :], lgt[:, 2, :], ACT.Ln).then_inc(lg_ln, 1)
            for i in range(1, MOD_FIRST // 2):
                for k in range(2):
                    mod_split(0, i, k)
            begin(GEMMS[0])

            def filter_step(n):
                if n < 3:
                    act.wait_ge(filt_arg, n + 1)
                    act.activation(h_act[0:64, n % 2, :], h_tmp[0:64, 2, :], ACT.Sin).then_inc(filt_sin, 1)
                elif n == 4:
                    for q in range(5):
                        act.wait_ge(filt_k, q + 1)
                        copy(filt[:, q, :], PS[:, 4 + q % 4, :]).then_inc(filt_ready, 1)

            act.wait_ge(rel_vec, 1)
            act.dma_start(rel_dram, relvec[:, :]).then_inc(rel_stored, 16)
            act.activation(warm[:, 0:1], mats[:, 1, 0:1], ACT.Silu)
            act_apply(0, GEMMS[0])

            order = iter(GEMMS[1:] + [None])

            def run(name, **more):
                g, after = next(x for x in GEMMS if x["name"] == name), next(order)
                (act_resid if g["kind"] == "resid" else act_gemm)(g, after, **more)

            run("ffn_0a_in")
            run("ffn_0a_out", between={b: lambda n=b - 2: filter_step(n) for b in range(2, 7)})
            run("even_u")

            def convolve(n):
                tile, dst = conv_tile(n)
                if n == 0:
                    act.wait_ge(units_drained, drained(G["u1"]))
                    act.wait_ge(nab_ready, 16)
                if n >= 4 and n % 2 == 0 and n < 8:
                    act.wait_ge(z_ready, n // 2 - 1)
                if n == 8:
                    act.wait_ge(conv_ready, 8)
                act.activation(dst, u1[:, tile, :], ACT.Identity, scale=col("hy_conv_w", 12 + tile),
                               bias=col("hy_conv_b", tile)).then_inc(conv_mid, 1)

            run("even_qk", between={b: lambda b=b: [convolve(n) for n in range(3 * b, 3 * b + 3)] for b in range(4)})

            def copy_z():
                act.wait_ge(conv_ready, 12)
                for t in range(4):
                    act.wait_ge(zt_turned, t + 1)
                    copy(hy_zt[:, t, :], PS[:, 4 + t, :]).then_inc(zt_copied, 1)

            def qk_squares():
                act.wait_ge(units_drained, drained(G["qk1"]))
                for t in range(8):
                    act.activation(qk_square[:, t, :], qk1[:, t, :], ACT.Square).then_inc(qk_sq, 1)
                act.activation(warm[:, 1:2], mats[:, 1, 0:1], ACT.Sqrt)

            run("even_v", between={0: copy_z, 1: qk_squares})
            for s in range(2):
                for n in range(4):
                    act.wait_ge(spec_mm, 4 * s + n + 1)
                    copy(hy_spec[s][n], PS[:, (5, 6, 7, 0)[n], :]).then_inc(spec_copied, 1)
                    if s == 0 and n == 1:
                        act.wait_ge(qk_inv, 1)
                        act.activation(head_root[:, :], head_inv[:, :], ACT.Sqrt).then_inc(qk_root, 1)
                        act.activation(warm[:, 0:1], mats[:, 1, 0:1], ACT.Exp)
            act_attend(NA)
            for c in range(5):
                if c < 4:
                    act_turn_out((c,), BOTH, 0)
                if c >= 1:
                    act.wait_ge(hy_out, c)
                    copy(XH[:, 3 + c, :], hy_z[:, c - 1, :]).then_inc(hy_hi, 1)
            run("even_out")
            run("ffn_0b_in")
            run("ffn_0b_out")
            run("ffn_1a_in")
            def decays(h):
                if h == 0:
                    act.wait_ge(ret_loaded, 32)
                    act.wait_ge(lg_ready, 1)
                else:
                    act.wait_ge(dec_ready, h)
                for n, (d, m) in enumerate(((h, 0), (RET_HEADS + h, 0), (h, 3), (RET_HEADS + h, 4))):
                    act.activation(ret_e[:, n, :], ret_k[:, m, :], ACT.Exp, scale=lg[:, d:d + 1]).then_inc(dec_exp, 1)

            run("ffn_1a_out", between={b: lambda h=b - 2: decays(h) for b in range(2, 2 + RET_HEADS)})
            run("ret_q")
            run("ret_k")
            run("ret_v")

            def gate(b):
                act.wait_ge(block_used, G["gr"]["w0"] + b + 1)
                act.activation(gr[:, 2 * b:2 * b + 2, :], PS[:, b % 2, :].rearrange("p (t n) -> p t n", t=2), ACT.Silu,
                               scale=1.0 / W_SCALE).then_inc(units_drained, 1)

            def outputs(h):
                if h == 0:
                    act.wait_ge(dec_ready, RET_HEADS)
                if h >= 2:
                    act.wait_ge(zl_ready, 4 * (h - 1))
                for e in range(4):
                    act.wait_ge(ry_ready, 4 * h + 2 * (e // 2) + 2)
                    copy(ret_y[:, 4 * (h % 2) + e, :], PS[:, 6 + e // 2, SEQ * (e % 2):SEQ * (e % 2) + SEQ]).then_inc(ryc_ready, 1)

            def ret_square(h):
                if h == 0:
                    act.wait_ge(rope_ready, 16)
                else:
                    act.wait_ge(rv_ready, h)
                for e in range(4):
                    act.wait_ge(rc_ready, 4 * h + e + 1)
                    act.activation(ret_sq[:, e, :], ret_y[:, 4 * (h % 2) + e, :], ACT.Square).then_inc(rq_ready, 1)

            def ret_root(h):
                act.wait_ge(ri_ready, h + 1)
                act.activation(root[:, :], inv[:, :], ACT.Sqrt).then_inc(rr_ready, 1)

            def gated(h):
                for e in range(4):
                    act.wait_ge(rz_ready, 4 * h + e + 1)
                    copy(ZH[4 * h + e], ret_y[:, 4 * (h % 2) + e, :]).then_inc(zh_ready, 1)

            def head_step(b):
                gate(b)
                if b % 2:
                    h = b // 2 + 1
                    ret_square(h - 1)
                    if h < RET_HEADS:
                        outputs(h)
                    ret_root(h - 1)
                elif b:
                    gated(b // 2 - 1)

            outputs(0)
            run("ret_g", between={b: lambda b=b: head_step(b) for b in range(8)})
            gated(RET_HEADS - 1)
            run("ret_out")
            run("ffn_1b_in")
            run("ffn_1b_out")
            run("ffn_2a_in")
            run("ffn_2a_out")
            run("mix_q")
            act.activation(warm[:, 1:2], mats[:, 1, 0:1], ACT.Sqrt)
            for c in range(DC):
                act.wait_ge(mem_turned, c + 1)
                copy(memX[:, c, :], PS[:, 6 + c % 2, 0:SEQ]).then_inc(mem_ready, 1)
            squares(MEM_NORM, range(DC))
            run("mix_k")
            act_root(MEM_NORM)
            run("mix_v", between={1: lambda: act_apply(MEM_NORM)})

            def head_squares(n, a, b, units):
                act.wait_ge(out_done, units)
                for t in range(2):
                    act.activation(O2n[:, t, a:b], O2[:, t, a:b], ACT.Square,
                                   accum_out=onorm[:, 2 * n + t:2 * n + t + 1]).then_inc(on_sq, 1)

            groups = 2 * N_HEADS_A
            act_attend(REL, {groups + 5: lambda: head_squares(0, 0, 64 * N_HEADS_A, REL[0] + groups)})
            act.activation(warm[:, 1:2], mats[:, 1, 0:1], ACT.Sqrt)
            head_squares(1, 64 * N_HEADS_A, D, REL[1])
            act.wait_ge(on_inv, 1)
            act.activation(onorm[:, 8:12], onorm[:, 4:8], ACT.Sqrt).then_inc(on_rstd, 1)
            act_turn_out(range(8), SEQ, 4, lambda c: col("g_out_a_2", c))
            run("mix_out")
            run("cross_q")
            run("cross_k")
            run("cross_v")
            act_attend(CROSS)
            act_turn_out(range(8), SEQ, 12)
            run("cross_out")
            run("ffn_2b_in")
            run("ffn_2b_out")
            for n in range(4):
                act.wait_ge(fin_turned, n + 1)
                copy(out_tok[:, n % 2, 512 * (n // 2):512 * (n // 2) + 512], PS[:, n, :]).then_inc(fin_copied, 1)
                if n >= 2:
                    act.wait_ge(fin_copied, n + 1)
                    act.dma_start(out[0, P * (n - 2):P * (n - 2) + P, :], out_tok[:, n - 2, :]).then_inc(stored, 16)

        @block.vector
        def _(dve):
            links = [0]

            def link(ins):
                links[0] += 1
                ins.then_inc(dve_chain, 1)
                dve.wait_ge(dve_chain, links[0])

            tt, ts, stt = dve.tensor_tensor, dve.tensor_scalar, dve.scalar_tensor_tensor

            def inverse(dst, sums, n, done):
                link(ts(dst, sums, 1.0 / n, EPS, ALU.mult, ALU.add))
                dve.reciprocal(dst, dst).then_inc(done, 1)

            def split(g, i, k, tiles=(0, 1)):
                for t in tiles:
                    dve.wait_ge(hi_ready, 2 * (g["w0"] + k) + t + 1 + 4 * i)
                    stt(WL[:, k, t, 0:g["kc"], :], W32[:, k, t, 0:g["kc"], :], W_SCALE, WH[:, k, t, 0:g["kc"], :],
                        ALU.mult, ALU.subtract).then_inc(lo_ready, 1)

            def mod_split(m0, i, k):
                for t in range(2):
                    dve.wait_ge(mod_hi, 2 * (m0 + k) + t + 1 + 4 * i)
                    stt(MWL[k][:, t], M32[k][:, t], W_SCALE, MWH[k][:, t], ALU.mult, ALU.subtract).then_inc(mod_lo, 1)

            def mod_drain(m0, i, k):
                dve.wait_ge(mod_used, m0 + k + 1 + 2 * i)
                src = PS[:, 6 + k, 0:8].rearrange("p (t h s) -> p t s h", t=2, h=2)
                dve.tensor_reduce(modT[:, bass.ds(2 * (m0 + k) + 4 * i, 2), :], src, AXX, ALU.add).then_inc(mod_drained, 1)

            def mod_finish(lo, hi, norms, half, whole):
                dve.wait_ge(mod_drained, hi)
                per = N_MOD * DC
                for layer in range(2):
                    a, b = max(2 * lo, per * layer), min(2 * hi, per * layer + per)
                    if a < b:
                        at = COL[("b_mod", layer)] - per * layer
                        for s in range(2):
                            m = modT[:, a:b, s]
                            ins = stt(m, m, 1.0 / W_SCALE, pcol[:, at + a:at + b], ALU.mult, ALU.add)
                link(ins)
                for layer, m, f in [(*x, 0.5) for x in half] + [(*x, 1.0) for x in whole]:
                    at = per * layer + DC * m
                    ins = ts(modT[:, at:at + DC, :], modT[:, at:at + DC, :], f / W_SCALE, None, ALU.mult)
                for layer, j in norms:
                    at, sc = COL[("norm_gain", None)] + (3 * layer + j) * DC, per * layer + DC * (3 * j + 1)
                    for s in range(2):
                        ins = stt(norm_a[:, 3 * layer + j, :, s], modT[:, sc:sc + DC, s], 1.0, pcol[:, at:at + DC], ALU.add, ALU.mult)
                link(ins)

            def begin_mods(g):
                if g["mods"]:
                    for k in range(2):
                        mod_split(g["m0"], 0, k)

            def dve_gemm(g, after, between={}):
                n, T, u0, w0 = g["blocks"] // 2, g["T"], g["u0"], g["w0"]

                def product(i, k):
                    dve.wait_ge(silu_done, FC * g["ffn"] + k + 1 + 2 * i)
                    stt(ffn_g[:, k, 0:T], PS[:, 2 * k + 1, 0:T], 1.0 / W_SCALE, ffn_s[:, k, 0:T], ALU.mult, ALU.mult)\
                        .then_inc(units_drained, 1)

                def rest(i, k):
                    dve.wait_ge(gh_done, FC * g["ffn"] + k + 1 + 2 * i)
                    j = bass.ds(2 * i + k, 1)
                    tt(GL[:, j, 0:T], ffn_g[:, k:k + 1, 0:T], GH[:, j, 0:T], ALU.subtract).then_inc(gl_done, 1)

                def store(i, k):
                    dve.wait_ge(block_used, w0 + k + 1 + 2 * i)
                    if g["tok"]:
                        src = PS[:, 2 * k:2 * k + 2, :].rearrange("p b (t n) -> p (b t) n", t=2)[:, 0:T // P, :]
                        dst = g["dest"][:, 0:T // P, bass.ds(512 * i + 256 * k, 256)]
                    else:
                        src, dst = PS[:, 2 * k:2 * k + 2, 0:T], g["dest"][:, bass.ds(4 * i + 2 * k, 2), 0:T]
                    ts(dst, src, g["scale"] / W_SCALE, None, ALU.mult).then_inc(units_drained, 1)

                if between:
                    for b in range(g["blocks"]):
                        if g["packed"]:
                            between[b]()
                        else:
                            store(b // 2, b % 2)
                        if b + 2 < g["blocks"]:
                            split(g, b // 2 + 1, b % 2)
                        else:
                            split(after, 0, b % 2)
                        if b in between and not g["packed"]:
                            between[b]()
                    return
                if g["kind"] == "ffn":
                    for lo, hi, mods in ((1, g["mods"], True), (max(g["mods"], 1), n, False)):
                        if lo < hi:
                            with dve.Fori(lo, hi) as i:
                                for k in range(2):
                                    product(i - 1, k)
                                    split(g, i, k)
                                    rest(i - 1, k)
                                    if mods:
                                        mod_drain(g["m0"], i - 1, k)
                                        mod_split(g["m0"], i, k)
                    for k in range(2):
                        product(n - 1, k)
                        if k == 0:
                            split(after, 0, 0)
                        rest(n - 1, k)
                    split(after, 0, 1)
                    if g["mods"]:
                        for k in range(2):
                            mod_drain(g["m0"], g["mods"] - 1, k)
                else:
                    if n > 1:
                        with dve.Fori(1, n) as i:
                            for k in range(2):
                                store(i - 1, k)
                                split(g, i, k)
                    for k in range(2):
                        store(n - 1, k)
                        split(after, 0, k)

            def dve_resid(g, after, between={}):
                T, nb = g["T"], g["blocks"]

                def add(u, tiles=(0, 1)):
                    for t in tiles:
                        c = 2 * u + t
                        for s, tok in segs(T):
                            gate = g["gate"](c, s) if callable(g["gate"]) else g["gate"] / W_SCALE
                            ins = stt(X[:, c, tok], PS[:, 2 * (u % 2) + t, tok], gate, X[:, c, tok], ALU.mult, ALU.add)
                    return ins

                u = 0
                for b in range(2, nb + 1):
                    while u < 3 and g["done"][u] <= b - 2:
                        dve.wait_ge(block_used, g["w0"] + g["done"][u] + 1)
                        add(u).then_inc(units_drained, 1)
                        u += 1
                    if b < nb:
                        split(g, b // 2, b % 2)
                    if b in between:
                        between[b]()
                if after is not None:
                    split(after, 0, 0)
                dve.wait_ge(early_used, g["r"] + 1)
                add(3, (0,)).then_inc(early_added, 1)
                dve.wait_ge(block_used, g["w0"] + nb)
                add(3, (1,)).then_inc(units_drained, 1)
                dve_norm(g["then"], after)

            def dve_inverse(n):
                q = NORMS[n]["T"] // 4
                dve.wait_ge(ms_ready, n + 1)
                dve.reciprocal(inv[:, 0:q], PS[:, BANK_N, 0:q]).then_inc(inv_ready, 1)

            def dve_norm(n, after=None):
                dve_inverse(n)
                if after is not None:
                    split(after, 0, 1, (0,))
                dve_apply(n, after)

            def dve_apply(n, after=None):
                N = NORMS[n]
                T, sq = N["T"], N["sq"]
                S = T // SEQ
                parts = [(c, s, tok) for c in range(DC) for s, tok in segs(T)]
                dve.wait_ge(rstd_ready, n + 1)
                for i in range(len(parts) + S):
                    if i < len(parts):
                        c, s, tok = parts[i]
                        stt(sq[:, c, tok], N["src"][:, c, tok], N["a"](c, s), PS[:, BANK_N + 1, tok], ALU.mult, ALU.mult)\
                            .then_inc(h_ready, 1)
                    if i >= S and N["h"] is not None:
                        c, s, tok = parts[i - S]
                        dve.wait_ge(xh_ready, H0[n] + i - S + 1)
                        if N["b"]:
                            ins = stt(N["l"][:, c, tok], sq[:, c, tok], N["b"](c, s), N["h"][:, c, tok], ALU.add, ALU.subtract)
                        else:
                            ins = tt(N["l"][:, c, tok], sq[:, c, tok], N["h"][:, c, tok], ALU.subtract)
                        ins.then_inc(xl_ready, 1)
                    if i == len(parts) // 2 and after is not None:
                        split(after, 0, 1, (1,))
                if after is not None:
                    begin_mods(after)

            def dve_attend(span):
                lo, hi = span
                for u in range(lo, hi + 3):
                    if u < hi:
                        dve.wait_ge(scores_ready, u + 1)
                        dve.tensor_reduce(stats[:, 0, u:u + 1], PS[:, 4 + u % 3, 0:UNITS[u]["nk"]], AXX, ALU.max,
                                          negate=True).then_inc(max_ready, 1)
                    v = u - 2
                    if lo <= v < hi:
                        dve.wait_ge(probs_ready, v + 1)
                        dve.reciprocal(stats[:, 2, v:v + 1], stats[:, 1, v:v + 1]).then_inc(denoms, 1)
                    v = u - 3
                    if v >= lo:
                        dst = UNITS[v]["dst"]
                        dve.wait_ge(denoms, v + 1)
                        dve.wait_ge(out_ready, v + 1)
                        ts(dst, PS[:, 7 * (v % 2), 0:dst.shape[-1]], stats[:, 2, v:v + 1], None, ALU.mult).then_inc(out_done, 1)

            def dve_turn_out(chunks, T, base, gain=None):
                for c in chunks:
                    dve.wait_ge(ot_hi, base + c + 1)
                    stt(XL[:, c, 0:T], PS[:, 4 + c % 4, 0:T], gain(c) if gain else 1.0, XH[:, c, 0:T],
                        ALU.mult, ALU.subtract).then_inc(ot_lo, 1)

            dve.memset(prow[:, :, :], 0.0).then_inc(rows_clear, 1)
            for c in range(DC):
                dve.wait_ge(x_turned, c + 1)
                dve.tensor_copy(X[:, c, :], PS[:, c % 4, :]).then_inc(x_ready, 1)
            dve.wait_ge(rows_turned, 1)
            link(dve.tensor_copy(pcol[:, :], PS[:, 6, 0:3 * P]))
            q_gain = col("na_q_gain")
            ts(q_gain, q_gain, 0.125, None, ALU.mult).then_inc(pcol_ready, 1)
            a, k_, r = (h_tmp[0:64, n, :] for n in range(3))
            MAGIC = 1.5 * 2.0 ** 23
            C1 = 6.28125
            C2 = float(np.float32(np.round((2 * math.pi - C1) * 2 ** 20) / 2 ** 20))
            C3 = 2 * math.pi - C1 - C2
            PI = 3.1415925

            def filter_step(n):
                if n < 3:
                    dve.wait_ge(filt_mm, n + 1)
                    if n:
                        dve.wait_ge(filt_sin, n)
                    else:
                        dve.wait_ge(gl_done, FC)
                    link(ts(a, PS[0:64, 4, 0:SEQ], col(f"hy_fb{n + 1}", 0, 64), col("hy_freq", 0, 64), ALU.add, ALU.mult))
                    link(ts(k_, a, 1.0 / (2 * math.pi), MAGIC, ALU.mult, ALU.add))
                    link(ts(k_, k_, -MAGIC, None, ALU.add))
                    link(stt(r, k_, -C1, a, ALU.mult, ALU.add))
                    link(stt(r, k_, -C2, r, ALU.mult, ALU.add))
                    link(stt(r, k_, -C3, r, ALU.mult, ALU.add))
                    ts(r, r, PI, -PI, ALU.min, ALU.max).then_inc(filt_arg, 1)
                elif n == 3:
                    dve.wait_ge(filt_mm, 3 + 4)
                    dve.wait_ge(nab_ready, 16)
                    for t in range(2):
                        link(tt(h_sum[:, t, :], PS[:, 4 + 2 * t, :], h_window[:, t, :], ALU.mult))
                        link(tt(hy_taps[:, :], PS[:, 5 + 2 * t, :], h_window[:, t, :], ALU.mult))
                        tt(h_dif[:, t, :], h_sum[:, t, :], hy_taps[:, :], ALU.subtract).then_inc(filt_sd, 1)
                        tt(h_sum[:, t, :], h_sum[:, t, :], hy_taps[:, :], ALU.add).then_inc(filt_sd, 1)

            dve.wait_ge(silu_hi, 1)
            tt(silu_s[:, :, 2:4], silu_c[:, :, :], silu_s[:, :, 0:2], ALU.subtract).then_inc(silu_s_ready, 1)
            dve_inverse(0)
            for k in range(2):
                mod_split(0, 0, k)
            dve.wait_ge(lg_loaded, 32)
            stt(lgt[:, 0, :], lg[:, :], -1.0, lg[:, :], ALU.mult, ALU.max).then_inc(lg_abs, 1)
            dve.wait_ge(lg_exp, 1)
            ts(lgt[:, 2, :], lgt[:, 1, :], 1.0, None, ALU.add).then_inc(lg_u, 1)
            dve.wait_ge(lg_u, 1)
            link(ts(lgt[:, 4, :], lgt[:, 2, :], -1.0, 1e-30, ALU.add, ALU.max))
            link(dve.reciprocal(lgt[:, 5, :], lgt[:, 4, :]))
            link(tt(lgt[:, 6, :], lgt[:, 5, :], lgt[:, 1, :], ALU.mult))
            dve.wait_ge(lg_ln, 1)
            link(tt(lgt[:, 6, :], lgt[:, 6, :], lgt[:, 3, :], ALU.mult))
            link(ts(lgt[:, 7, :], lg[:, :], 0.0, None, ALU.min))
            tt(lg[:, :], lgt[:, 7, :], lgt[:, 6, :], ALU.subtract).then_inc(lg_ready, 1)
            for i in range(MOD_FIRST // 2):
                if i + 1 < MOD_FIRST // 2:
                    for k in range(2):
                        mod_split(0, i + 1, k)
                for k in range(2):
                    mod_drain(0, i, k)
            mod_finish(0, MOD_FIRST, [(0, 0)], [], [])
            dve.wait_ge(rel_mm, 1)
            tt(relvec[:, :], PS[0:N_HEADS_2, 4, :], rel_mask[0:N_HEADS_2, :], ALU.add).then_inc(rel_vec, 1)
            split(GEMMS[0], 0, 0)
            split(GEMMS[0], 0, 1, (0,))
            dve_apply(0, GEMMS[0])

            order = iter(GEMMS[1:] + [None])

            def run(name, **more):
                g, after = next(x for x in GEMMS if x["name"] == name), next(order)
                (dve_resid if g["kind"] == "resid" else dve_gemm)(g, after, **more)

            run("ffn_0a_in")
            mod_finish(MOD_FIRST, 32, [(0, 1), (0, 2)], [(0, 2)], [(0, 5)])
            run("ffn_0a_out", between={b: lambda n=b - 2: filter_step(n) for b in range(2, 7)})
            run("even_u")

            def convolve(n):
                tile, dst = conv_tile(n)
                dst, src = (a.rearrange("p (s t) -> p s t", s=2) for a in (dst, u1[:, tile, :]))
                dve.wait_ge(conv_mid, n + 1)
                link(stt(dst[:, :, 1:], src[:, :, :SEQ - 1], col("hy_conv_w", tile), dst[:, :, 1:], ALU.mult, ALU.add))
                stt(dst[:, :, :SEQ - 1], src[:, :, 1:], col("hy_conv_w", 24 + tile), dst[:, :, :SEQ - 1],
                    ALU.mult, ALU.add).then_inc(conv_ready, 1)

            run("even_qk", between={b: lambda b=b: [convolve(n) for n in range(3 * b, 3 * b + 3)] for b in range(4)})
            run("even_v")
            dve.wait_ge(qk_ms, 1)
            inverse(head_inv[:, :], PS[0:16, 4, :], 64, qk_inv)
            for t in range(8):
                dve.wait_ge(qk_rstd, t + 1)
                gain = col("na_q_gain" if t < 4 else "na_k_gain")
                stt(qk1[:, t, :], qk1[:, t, :], gain, PS[:, 1 + t % 3, :], ALU.mult, ALU.mult).then_inc(qk_ready, 1)
            dve_attend(NA)
            for c in range(5):
                if c < 4:
                    dve.wait_ge(inv_mm, c + 1)
                    link(stt(hy_tmp[:, c % 2, :], hy_z[:, c, :], col("hy_bias", c), PS[:, 2 + c % 2, :], ALU.mult, ALU.add))
                    tt(hy_z[:, c, :], hy_tmp[:, c % 2, :], hy_x0[:, c, :], ALU.mult).then_inc(hy_out, 1)
                    dve_turn_out((c,), BOTH, 0)
                if c >= 1:
                    dve.wait_ge(hy_hi, c)
                    tt(XL[:, 3 + c, :], hy_z[:, c - 1, :], XH[:, 3 + c, :], ALU.subtract).then_inc(hy_lo, 1)
            run("even_out")
            run("ffn_0b_in")
            mod_finish(32, 54, [(1, 0)], [(0, 8), (1, 2)], [])
            run("ffn_0b_out")
            run("ffn_1a_in")
            mod_finish(54, MOD_BLOCKS, [(1, 1), (1, 2)], [(1, 8)], [(1, 5)])
            run("ffn_1a_out")
            run("ret_q")
            run("ret_k")

            def rotary(t):
                x = qr[:, t, :] if t < 8 else kr[:, t - 8, 0:SEQ]
                dve.wait_ge(rope_mm, t + 1)
                link(tt(rope_t[:, 2 + t % 2, :], PS[:, 4 + t % 2, 0:SEQ], rope[:, 2 * (t % 2) + 1, :], ALU.mult))
                dve.wait_ge(rope_cos, t + 1)
                tt(x, rope_t[:, t % 2, :], rope_t[:, 2 + t % 2, :], ALU.add).then_inc(rope_ready, 1)

            def decayed(h):
                for t in range(4):
                    dve.wait_ge(rs_ready, 4 * h + t + 1)
                    stt(ret_p[:, 4 * (h % 2) + t, :], PS[:, 4 + t % 2, 0:SEQ], 0.0625, decay[:, 4 * h + t, :], ALU.mult, ALU.mult)\
                        .then_inc(rp_ready, 1)

            def centre(h):
                dve.wait_ge(rm_ready, h + 1)
                for e in range(4):
                    y = ret_y[:, 4 * (h % 2) + e, :]
                    stt(y, PS[:, SUM_BANKS[h][0], 0:SEQ], -1.0 / 512, y, ALU.mult, ALU.add).then_inc(rc_ready, 1)

            def gated(h):
                dve.wait_ge(units_drained, G["gr"]["u0"] + 2 * h + 2)
                for e in range(5):
                    if e < 4:
                        y = ret_y[:, 4 * (h % 2) + e, :]
                        dve.wait_ge(rn_ready, 4 * h + e + 1)
                        tt(y, y, gr[:, 4 * h + e, :], ALU.mult).then_inc(rz_ready, 1)
                    if e >= 1:
                        n = 4 * h + e - 1
                        dve.wait_ge(zh_ready, n + 1)
                        tt(ZL[n], ret_y[:, 4 * (h % 2) + e - 1, :], ZH[n], ALU.subtract).then_inc(zl_ready, 1)

            def head_step(b):
                if b % 2:
                    h = b // 2 + 1
                    centre(h - 1)
                    if h < RET_HEADS:
                        decayed(h)
                    dve.wait_ge(rv_ready, h)
                    inverse(inv[:, :], PS[:, SUM_BANKS[h - 1][1], 0:SEQ], 512, ri_ready)
                elif b:
                    gated(b // 2 - 1)

            def rotary_pair(b):
                rotary(2 * b)
                rotary(2 * b + 1)

            rotary_pair(0)
            run("ret_v", between={b: lambda b=b: rotary_pair(b + 1) for b in range(7)})
            dve.wait_ge(dec_ready, RET_HEADS)
            decayed(0)
            run("ret_g", between={b: lambda b=b: head_step(b) for b in range(8)})
            gated(RET_HEADS - 1)
            run("ret_out")
            run("ffn_1b_in")
            run("ffn_1b_out")
            run("ffn_2a_in")
            run("ffn_2a_out")
            run("mix_q")
            run("mix_k")
            dve_inverse(MEM_NORM)
            run("mix_v", between={1: lambda: dve_apply(MEM_NORM)})
            dve_attend(REL)
            dve.wait_ge(on_sq, 4)
            for n, width in enumerate((768, 256)):
                ins = ts(onorm[:, 4 + 2 * n:6 + 2 * n], onorm[:, 2 * n:2 * n + 2], 1.0 / width, EPS, ALU.mult, ALU.add)
            link(ins)
            dve.reciprocal(onorm[:, 4:8], onorm[:, 4:8]).then_inc(on_inv, 1)
            dve.wait_ge(on_rstd, 1)
            for n, (a, b) in enumerate(((0, 64 * N_HEADS_A), (64 * N_HEADS_A, D))):
                for t in range(2):
                    ts(O2n[:, t, a:b], O2[:, t, a:b], onorm[:, 8 + 2 * n + t:9 + 2 * n + t], None, ALU.mult).then_inc(on_ready, 1)
            dve_turn_out(range(8), SEQ, 4, lambda c: col("g_out_a_2", c))
            run("mix_out")
            run("cross_q")
            run("cross_k")
            run("cross_v")
            dve_attend(CROSS)
            dve_turn_out(range(8), SEQ, 12)
            run("cross_out")
            run("ffn_2b_in")
            run("ffn_2b_out")

        @block.gpsimd
        def _(pool):
            tt = pool.tensor_tensor

            def pool_sums(n):
                N = NORMS[n]
                for c in range(1, DC - 1):
                    pool.wait_ge(sq_ready, DC * n + c + 1)
                    if c > 1:
                        pool.wait_ge(added_up, (DC - 2) * (N["added"] - 1) + c - 1)
                    tt(N["sq"][:, 0, 0:N["T"]], N["sq"][:, 0, 0:N["T"]], N["sq"][:, c, 0:N["T"]], ALU.add).then_inc(added_up, 1)

            pool.wait_ge(rows_clear, 1)
            for name, at, n in SHORT:
                for m in range(n):
                    pool.dma_start(prow[at % P:at % P + 1, at // P, 64 * m:64 * m + 64], io[name]).then_inc(short_loaded, 16)
            for n, name in enumerate(("ret_logit_f", "ret_logit_b")):
                src = bass.AP(tensor=io[name].tensor, offset=0, ap=[[0, P], [1, RET_HEADS]])
                pool.dma_start(lg[:, RET_HEADS * n:RET_HEADS * n + RET_HEADS], src).then_inc(lg_loaded, 16)
            pool.dma_start(relb[:, :], io["rel_bias_2"]).then_inc(rel_loaded, 16)
            pool.dma_start(onehot[0:REL_BUCKETS, :], io["k_onehot"]).then_inc(rel_loaded, 16)
            pool.dma_start(rel_mask[0:N_HEADS_2, :], io["k_rel_mask"]).then_inc(rel_loaded, 16)
            pool.wait_ge(mod_used, MOD_FIRST)
            pool.dma_start(na_mask, io["k_na_mask"]).then_inc(nab_loaded, 16)
            width, rows = 2 * WIN_C - 1, 15
            for h in range(NA_HEADS):
                for r in range(4):
                    src = bass.AP(tensor=io["na_rpb"].tensor, offset=(h * rows + 7 - r) * width + WIN_C - GRID_W,
                                  ap=[[1, GRID_W], [width, 4], [1, GRID_W]])
                    at = GRID_W * (1 - r % 2)
                    dst = na_bias[at:at + GRID_W, 2 * h + r // 2, :].rearrange("p (a b) -> p a b", a=4)
                    pool.dma_start(dst, src).then_inc(nab_loaded, 16)
            pool.wait_ge(nab_loaded, 16 * 33)
            for n in range(16):
                tt(na_bias[:, n, :], na_bias[:, n, :], na_mask[:, 0, :], ALU.mult).then_inc(pool_chain, 1)
            for n in range(16):
                pool.wait_ge(pool_chain, n + 1)
                tt(na_bias[:, n, :], na_bias[:, n, :], na_mask[:, 1, :], ALU.add).then_inc(nab_ready, 1)
            pool.wait_ge(mod_used, 32)
            pool.dma_start(fw[0:17, 0:64], io["hy_fw1"][0]).then_inc(filt_loaded, 16)
            pool.dma_start(fw[:, 64:128], io["hy_fw2"][0]).then_inc(filt_loaded, 16)
            pool.dma_start(fw[:, 128:192], io["hy_fw3"][0]).then_inc(filt_loaded, 16)
            pool.dma_start(fw_out[:, :], io["hy_fw4"][0]).then_inc(filt_loaded, 16)
            pool.dma_start(embT[:, :], io["k_emb"]).then_inc(filt_loaded, 16)
            pool.dma_start(h_window, io["k_window"]).then_inc(filt_loaded, 16)
            for m in range(3):
                pool.dma_start(dft_filter[m], io["k_fwd"][:, m]).then_inc(filt_loaded, 16)
            pool.dma_start(dft[:, 2:4, :], io["k_fwd"][:, 3]).then_inc(dft_back, 16)
            pool.wait_ge(filt_k, 5)
            pool.dma_start(idft, io["k_inv"].rearrange("p m t f -> p (m t) f")).then_inc(dft_back, 16)
            pool.wait_ge(gl_done, FC)
            pool.dma_start(head_spread, io["k_head_spread"]).then_inc(heads_back, 16)
            pool_sums(1)
            for c in range(4):
                pool.wait_ge(conv_ready, 2 * c + 2)
                tt(hy_z[:, c, :], hy_xv[:, 2 * (c % 2), :], hy_xv[:, 2 * (c % 2) + 1, :], ALU.mult).then_inc(z_ready, 1)
            for s in range(2):
                pool.wait_ge(spec_copied, 4 * s + 4)
                if s == 0:
                    pool.wait_ge(spec_mm, 8)
                for f in range(2):
                    re, im, (t0, t1) = hy_spec[s][f], hy_spec[s][2 + f], (hy_tmp[:, n, :] for n in range(2))
                    if s or f:
                        pool.wait_ge(y_ready, 2 * s + f)
                    tt(t0, im, filt[:, 3 + f, :], ALU.mult)
                    tt(t1, re, filt[:, 3 + f, :], ALU.mult)
                    tt(re, re, filt[:, f, :], ALU.mult)
                    tt(im, im, filt[:, 2 if f == 0 else 1, :], ALU.mult).then_inc(pool_chain, 1)
                    pool.wait_ge(pool_chain, 16 + 2 * s + f + 1)
                    tt(re, re, t0, ALU.subtract)
                    tt(im, im, t1, ALU.add).then_inc(y_ready, 1)
            pool_sums(2)
            pool_sums(3)
            pool.wait_ge(mod_used, MOD_BLOCKS)
            pool.dma_start(ret_k, io["k_ret"].rearrange("p m t q -> p m (t q)")).then_inc(ret_loaded, 16)
            pool.dma_start(rope, io["k_rope"].rearrange("p a b t -> p (a b) t")).then_inc(ret_loaded, 16)
            for h in range(RET_HEADS):
                pool.wait_ge(dec_exp, 4 * h + 4)
                lat, cx = (decay[:, 4 * h + 2 * n:4 * h + 2 * n + 2, :].rearrange("p a b -> p (a b)") for n in range(2))
                tt(ret_e[:, 0, :], ret_e[:, 0, :], ret_k[:, 1, :], ALU.mult).then_inc(dec_used, 1)
                tt(ret_e[:, 1, :], ret_e[:, 1, :], ret_k[:, 2, :], ALU.mult).then_inc(dec_used, 1)
                tt(cx, ret_e[:, 2, :], ret_e[:, 3, :], ALU.add).then_inc(dec_used, 1)
                pool.wait_ge(dec_used, 3 * h + 3)
                tt(lat, ret_e[:, 0, :], ret_e[:, 1, :], ALU.add).then_inc(dec_ready, 1)
            pool_sums(4)
            for t in range(16):
                x = qr[:, t, :] if t < 8 else kr[:, t - 8, 0:SEQ]
                pool.wait_ge(units_drained, drained(G["qr"] if t < 8 else G["kr"]))
                if t >= 2:
                    pool.wait_ge(rope_ready, t - 1)
                tt(rope_t[:, t % 2, :], x, rope[:, 2 * (t % 2), :], ALU.mult).then_inc(rope_cos, 1)
            for h in range(RET_HEADS):
                pool.wait_ge(rr_ready, h + 1)
                for e in range(4):
                    y = ret_y[:, 4 * (h % 2) + e, :]
                    tt(y, y, root[:, 0:SEQ], ALU.mult).then_inc(rn_ready, 1)
            pool_sums(5)
            pool.wait_ge(block_used, G["or"]["w0"] + G["or"]["blocks"])
            pool.wait_ge(rel_stored, 16)
            for t in range(2):
                src = bass.AP(tensor=rel_dram.tensor, offset=P - P * t, ap=[[1, P], [BOTH, N_HEADS_2], [1, P * (t + 1)]])
                pool.dma_start(rel_bias[:, :, P * t:P * t + P * (t + 1)], src).then_inc(rel_back, 16)
            pool.dma_start(mem_tok, io["mem_2"][0].rearrange("(t p) d -> p t d", p=P)).then_inc(mem_loaded, 16)
            for n in (6, 7, 9, 10, 11):
                pool_sums(n)


def kernel(**inputs):
    import concourse.bacc as bacc
    from concourse.bass_utils import run_bass_kernel_spmd

    nc = bacc.Bacc("TRN2", target_bir_lowering=False, num_devices=1)
    arrays, io = {}, {}
    for name, a in {**inputs, **shape_constants()}.items():
        a = np.ascontiguousarray(a)
        arrays[f"in_{name}"] = a
        io[name] = nc.dram_tensor(f"in_{name}", a.shape, mybir.dt.from_np(a.dtype), kind="ExternalInput").ap()
    out = nc.dram_tensor("out", (1, SEQ, D), F32, kind="ExternalOutput").ap()
    program(nc, io, out)
    r = run_bass_kernel_spmd(nc, [arrays], core_ids=[0])
    return r.results[0]["out"]
```
